# Optimizing a Trainium2 kernel written in Bass

```python
import jax, jax.numpy as jnp
from jax import lax
import numpy as np

D_MODEL = 1024
BATCH = 1
SEQ = 256
DEPTH = 1
DEC_BATCH = 8
DEC_SEQ = 4
PAST_LEN = 2048
PAGE_SIZE = 128

LRU_WIDTH = D_MODEL
LRU_HEADS = 16
LRU_HEAD_DIM = LRU_WIDTH // LRU_HEADS
CONV_WIDTH = 4
LRU_C = 8.0
POOL_WIDTH = D_MODEL
POOL_WINDOWS = (2, 4, 8, 16)
POOL_GROUPS = len(POOL_WINDOWS)
POOL_GROUP_DIM = POOL_WIDTH // POOL_GROUPS
POOL_BUF = max(POOL_WINDOWS) - 1
N_EXPERTS = 32
TOP_K = 4
D_EXPERT = D_MODEL
SWIGLU_LIMIT = 7.0
SWIGLU_ALPHA = 1.702
PLE_DIM = 256
EPS = 1e-6
IN_COLS = LRU_WIDTH + POOL_WIDTH + 2 * D_MODEL

kernel_name = "hybrid_rglru_pool_moe_decode_step"

def rmsnorm(x, g):
    xf = x.astype(jnp.float32)
    y = xf * lax.rsqrt(jnp.mean(xf * xf, axis=-1, keepdims=True) + EPS)
    return (y * g.astype(jnp.float32)).astype(x.dtype)

def causal_conv(xa, buf, w, b):
    L = xa.shape[1]
    ext = jnp.concatenate([buf.astype(xa.dtype), xa], axis=1)
    out = b
    for k in range(CONV_WIDTH):
        out = out + ext[:, k:k + L] * w[k]
    return out, ext[:, -(CONV_WIDTH - 1):]

def rg_lru(xc, h0, pos, w_ra, b_ra, w_rx, b_rx, lam):
    B, L, W = xc.shape
    xh = xc.reshape(B, L, LRU_HEADS, LRU_HEAD_DIM)
    r = jax.nn.sigmoid((jnp.einsum('blhi,hij->blhj', xh, w_ra).reshape(B, L, W) + b_ra).astype(jnp.float32))
    ig = jax.nn.sigmoid((jnp.einsum('blhi,hij->blhj', xh, w_rx).reshape(B, L, W) + b_rx).astype(jnp.float32))
    log_a = -LRU_C * r * jax.nn.softplus(-lam.astype(jnp.float32))
    a = jnp.exp(log_a)
    mult = jnp.where((pos == 0)[None, :, None], 1.0, jnp.sqrt(-jnp.expm1(2.0 * log_a)))
    bterm = mult * ig * xc.astype(jnp.float32)
    bterm = bterm.at[:, 0].add(a[:, 0] * h0.astype(jnp.float32))

    def combine(lhs, rhs):
        a1, b1 = lhs
        a2, b2 = rhs
        return a1 * a2, a2 * b1 + b2

    _, h = lax.associative_scan(combine, (a, bterm), axis=1)
    return h.astype(xc.dtype), h[:, -1]

def pool_mix(xb, buf, pos, pool_w, pool_scale):
    B, L, W = xb.shape
    ext = jnp.concatenate([buf.astype(xb.dtype), xb], axis=1)
    extf = ext.astype(jnp.float32)
    cs = jnp.concatenate([jnp.zeros((B, 1, W), jnp.float32), jnp.cumsum(extf, axis=1)], axis=1)
    xbf = xb.astype(jnp.float32)
    outs = []
    for g, win in enumerate(POOL_WINDOWS):
        sl = slice(g * POOL_GROUP_DIM, (g + 1) * POOL_GROUP_DIM)
        tot = cs[:, POOL_BUF + 1:POOL_BUF + 1 + L, sl] - cs[:, POOL_BUF + 1 - win:POOL_BUF + 1 - win + L, sl]
        count = jnp.minimum(win, pos + 1).astype(jnp.float32)
        mixed = (tot / count[None, :, None] - xbf[..., sl]).astype(xb.dtype)
        outs.append(jnp.einsum('bld,de->ble', mixed, pool_w[g]))
    y = jnp.concatenate(outs, axis=-1) * pool_scale
    return y, ext[:, -POOL_BUF:]

def moe(u, w_router, b_router, w_gate_up, b_gate_up, w_down, b_down):
    B, L, D = u.shape
    t = u.reshape(B * L, D)
    logits = (t @ w_router + b_router).astype(jnp.float32)
    vals, idx = lax.top_k(logits, TOP_K)
    wts = jax.nn.softmax(vals, axis=-1)
    comb = jnp.einsum('tk,tke->te', wts, jax.nn.one_hot(idx, N_EXPERTS, dtype=jnp.float32)).astype(u.dtype)
    out = jnp.zeros_like(t)
    for e in range(N_EXPERTS):
        gu = t @ w_gate_up[e] + b_gate_up[e]
        gate = jnp.minimum(gu[:, :D_EXPERT], SWIGLU_LIMIT)
        up = jnp.clip(gu[:, D_EXPERT:], -SWIGLU_LIMIT, SWIGLU_LIMIT)
        h = (up + 1.0) * (gate * jax.nn.sigmoid(SWIGLU_ALPHA * gate))
        out = out + comb[:, e:e + 1] * (h @ w_down[e] + b_down[e])
    return out.reshape(B, L, D)

def layer(x, p, h0, conv_buf, pool_buf, pos0, i, g_mix, w_in, conv_w, conv_b, w_rg_a, b_rg_a, w_rg_x, b_rg_x,
          lru_lambda, pool_w, pool_scale, w_proj_a, w_proj_b, w_out, g_moe, w_router, b_router,
          w_gate_up, b_gate_up, w_down, b_down, g_ple, w_ple_gate, w_ple, g_ple_post):
    L = x.shape[1]
    pos = pos0 + jnp.arange(L, dtype=jnp.int32)
    u = rmsnorm(x, g_mix[i])
    z = u @ w_in[i]
    xa = z[..., :LRU_WIDTH]
    xb = z[..., LRU_WIDTH:LRU_WIDTH + POOL_WIDTH]
    ga = z[..., LRU_WIDTH + POOL_WIDTH:LRU_WIDTH + POOL_WIDTH + D_MODEL]
    gb = z[..., LRU_WIDTH + POOL_WIDTH + D_MODEL:]
    xc, conv_new = causal_conv(xa, conv_buf, conv_w[i], conv_b[i])
    ya, h_last = rg_lru(xc, h0, pos, w_rg_a[i], b_rg_a[i], w_rg_x[i], b_rg_x[i], lru_lambda[i])
    yb, pool_new = pool_mix(xb, pool_buf, pos, pool_w[i], pool_scale[i])
    merged = jax.nn.sigmoid(ga) * (ya @ w_proj_a[i]) + jax.nn.sigmoid(gb) * (yb @ w_proj_b[i])
    x = x + merged @ w_out[i]
    x = x + moe(rmsnorm(x, g_moe[i]), w_router[i], b_router[i], w_gate_up[i], b_gate_up[i], w_down[i], b_down[i])
    ple = rmsnorm(p @ w_ple[i], g_ple_post[i]) * jax.nn.sigmoid(rmsnorm(x, g_ple[i]) @ w_ple_gate[i])
    x = x + ple
    return x, h_last, conv_new, pool_new

def setup_inputs(seed: int = 0) -> dict:
    key = jax.random.key(seed)
    ks = iter(jax.random.split(key, 40))
    f32 = jnp.float32

    def nrm(shape, scale):
        return jax.random.normal(next(ks), shape, f32) * scale

    def gain(shape):
        return 1.0 + nrm(shape, 0.05)

    u = jax.random.uniform(next(ks), (DEPTH, LRU_WIDTH), f32, 0.9, 0.999)
    s = u ** (1.0 / LRU_C)
    lam = jnp.log(s) - jnp.log1p(-s)
    return {
        "x_prompt": nrm((BATCH, SEQ, D_MODEL), 1.0),
        "x_sample": nrm((DEC_BATCH, DEC_SEQ, D_MODEL), 1.0),
        "p_prompt": nrm((DEPTH, BATCH, SEQ, PLE_DIM), 1.0),
        "p_sample": nrm((DEPTH, DEC_BATCH, DEC_SEQ, PLE_DIM), 1.0),
        "state_lru_h": nrm((DEPTH, DEC_BATCH, LRU_WIDTH), 0.5),
        "state_conv": nrm((DEPTH, DEC_BATCH, CONV_WIDTH - 1, LRU_WIDTH), 1.0),
        "state_pool": nrm((DEPTH, DEC_BATCH, POOL_BUF, POOL_WIDTH), 1.0),
        "g_mix": gain((DEPTH, D_MODEL)),
        "w_in": nrm((DEPTH, D_MODEL, IN_COLS), D_MODEL ** -0.5),
        "conv_w": nrm((DEPTH, CONV_WIDTH, LRU_WIDTH), CONV_WIDTH ** -0.5),
        "conv_b": nrm((DEPTH, LRU_WIDTH), 0.01),
        "w_rg_a": nrm((DEPTH, LRU_HEADS, LRU_HEAD_DIM, LRU_HEAD_DIM), LRU_HEAD_DIM ** -0.5),
        "b_rg_a": nrm((DEPTH, LRU_WIDTH), 0.01),
        "w_rg_x": nrm((DEPTH, LRU_HEADS, LRU_HEAD_DIM, LRU_HEAD_DIM), LRU_HEAD_DIM ** -0.5),
        "b_rg_x": nrm((DEPTH, LRU_WIDTH), 0.01),
        "lru_lambda": lam,
        "pool_w": nrm((DEPTH, POOL_GROUPS, POOL_GROUP_DIM, POOL_GROUP_DIM), POOL_GROUP_DIM ** -0.5),
        "pool_scale": gain((DEPTH, POOL_WIDTH)),
        "w_proj_a": nrm((DEPTH, LRU_WIDTH, D_MODEL), LRU_WIDTH ** -0.5),
        "w_proj_b": nrm((DEPTH, POOL_WIDTH, D_MODEL), POOL_WIDTH ** -0.5),
        "w_out": nrm((DEPTH, D_MODEL, D_MODEL), D_MODEL ** -0.5),
        "g_moe": gain((DEPTH, D_MODEL)),
        "w_router": nrm((DEPTH, D_MODEL, N_EXPERTS), D_MODEL ** -0.5),
        "b_router": nrm((DEPTH, N_EXPERTS), 0.01),
        "w_gate_up": nrm((DEPTH, N_EXPERTS, D_MODEL, 2 * D_EXPERT), D_MODEL ** -0.5),
        "b_gate_up": nrm((DEPTH, N_EXPERTS, 2 * D_EXPERT), 0.01),
        "w_down": nrm((DEPTH, N_EXPERTS, D_EXPERT, D_MODEL), D_EXPERT ** -0.5),
        "b_down": nrm((DEPTH, N_EXPERTS, D_MODEL), 0.01),
        "g_ple": gain((DEPTH, D_MODEL)),
        "w_ple_gate": nrm((DEPTH, D_MODEL, D_MODEL), D_MODEL ** -0.5),
        "w_ple": nrm((DEPTH, PLE_DIM, D_MODEL), PLE_DIM ** -0.5),
        "g_ple_post": gain((DEPTH, D_MODEL)),
        "g_final": gain((D_MODEL,)),
    }

def reference(x_prompt, x_sample, p_prompt, p_sample, state_lru_h, state_conv, state_pool,
              g_mix, w_in, conv_w, conv_b, w_rg_a, b_rg_a, w_rg_x, b_rg_x, lru_lambda,
              pool_w, pool_scale, w_proj_a, w_proj_b, w_out, g_moe, w_router, b_router,
              w_gate_up, b_gate_up, w_down, b_down, g_ple, w_ple_gate, w_ple, g_ple_post, g_final):
    bp = x_prompt.shape[0]
    xp, xs = x_prompt, x_sample
    hp_l, cp_l, pp_l, hs_l, cs_l, ps_l = [], [], [], [], [], []
    for i in range(DEPTH):
        h0p = jnp.zeros((bp, LRU_WIDTH), jnp.float32)
        cb0p = jnp.zeros((bp, CONV_WIDTH - 1, LRU_WIDTH), xp.dtype)
        pb0p = jnp.zeros((bp, POOL_BUF, POOL_WIDTH), xp.dtype)
        xp, hp, cp, pp = layer(xp, p_prompt[i], h0p, cb0p, pb0p, 0, i, g_mix, w_in, conv_w, conv_b,
                               w_rg_a, b_rg_a, w_rg_x, b_rg_x, lru_lambda, pool_w, pool_scale,
                               w_proj_a, w_proj_b, w_out, g_moe, w_router, b_router, w_gate_up,
                               b_gate_up, w_down, b_down, g_ple, w_ple_gate, w_ple, g_ple_post)
        xs, hs, cs, ps = layer(xs, p_sample[i], state_lru_h[i], state_conv[i], state_pool[i], PAST_LEN, i,
                               g_mix, w_in, conv_w, conv_b, w_rg_a, b_rg_a, w_rg_x, b_rg_x, lru_lambda,
                               pool_w, pool_scale, w_proj_a, w_proj_b, w_out, g_moe, w_router, b_router,
                               w_gate_up, b_gate_up, w_down, b_down, g_ple, w_ple_gate, w_ple, g_ple_post)
        hp_l.append(hp.astype(x_prompt.dtype))
        cp_l.append(cp.astype(x_prompt.dtype))
        pp_l.append(pp.astype(x_prompt.dtype))
        hs_l.append(hs.astype(state_lru_h.dtype))
        cs_l.append(cs.astype(state_conv.dtype))
        ps_l.append(ps.astype(state_pool.dtype))
    y_prompt = rmsnorm(xp, g_final)
    y_sample = rmsnorm(xs, g_final)
    h_prompt = jnp.stack(hp_l)
    conv_prompt = jnp.stack(cp_l)
    pool_prompt = jnp.stack(pp_l)
    h_sample = jnp.stack(hs_l)
    conv_sample = jnp.stack(cs_l)
    pool_sample = jnp.stack(ps_l)
    return (y_prompt, y_sample, h_prompt, conv_prompt, pool_prompt, h_sample, conv_sample, pool_sample)


_drawn_inputs = setup_inputs


def setup_inputs(seed=0):
    import zlib

    import numpy as np

    out = dict(_drawn_inputs(seed))
    spreads = {}
    factors = {'b_rg_a': 8.0,
     'b_rg_x': 6.342,
     'b_gate_up': 8.0,
     'b_down': 8.0,
     'g_ple': 6.972,
     'g_ple_post': 2.887}
    for name, (base, spread) in spreads.items():
        noise = np.random.default_rng([zlib.crc32(name.encode()), seed]).standard_normal(out[name].shape)
        drawn = base * np.exp(spread * noise) if base else spread * noise
        out[name] = __import__('jax').numpy.asarray(drawn.astype(out[name].dtype))
    for name, factor in factors.items():
        out[name] = (out[name] * factor).astype(out[name].dtype)
    return out
```

```python
from contextlib import ExitStack

import concourse.bass as bass
from concourse import mybir

ALU = mybir.AluOpType
ACT = mybir.ActivationFunctionType
AX = mybir.AxisListType
F32 = mybir.dt.float32
I32 = mybir.dt.int32
U32 = mybir.dt.uint32

P = 128
D = 1024
KC = D // P
SEQ = 256
DB, DS = 8, 4
NTOK = SEQ + DB * DS
TT = 3
ROWS = [128, 128, 32]
TAIL = 48
CONV = 4
PB = 15
PG = 4
WIN = [2, 4, 8, 16]
PLE = 256
EPS = 1e-6
NE = 32
TOPK = 4
CAP = 64
PASSES = -(-NTOK // CAP)
NCH = NE * PASSES
LIMIT, ALPHA = 7.0, 1.702

XA_W = (CONV - 1) + SEQ + DB * (CONV - 1 + DS)
XC_W = XA_W - (CONV - 1)
XB_W = PB + SEQ + DB * (PB + DS)

SLOTS = 6
FRONT = [("in", 0, 0), ("in", 2, 1), ("in", 1, 2), ("in", 3, 3), ("in", 4, 4), ("in", 5, 5),
         ("in", 6, 0), ("in", 7, 1), ("b", 0, 2), ("b", 1, 3), ("a", 0, 4), ("a", 1, 5),
         ("out", 0, 0), ("out", 1, 1)]
MOE_SLOT = [2, 3, 4, 5, 0, 1]

B_G, B_U, B_O, B_X, B_XT, B_HT = range(6)

RAW_LOADS, GATE_LOADS, SMALL_LOADS = 12, 4, 3

V_GMIX, V_CW, V_CB, V_BRA, V_BRX, V_LAM, V_PS, V_GMOE, V_GPLE = 0, 8, 40, 48, 56, 64, 72, 80, 88
NVEC = 96


def front_uses():
    uses, turn = [0] * SLOTS, {}
    for w, j, s in FRONT:
        turn[(w, j)] = (s, uses[s])
        uses[s] += 1
    return uses, turn


def z_order():
    out = []
    for p in range(4):
        out += [2 * p, 2 * p + 1, 8 + 2 * p, 9 + 2 * p]
    return out + list(range(16, 32))


def plan_psum():
    turns, uses = {}, [0] * 8
    ring, at = [0, 1, 2, 7], [0]

    def take(name, bank=None):
        if bank is None:
            bank = ring[at[0] % 4]
            at[0] += 1
        turns[name] = (bank, uses[bank])
        uses[bank] += 1

    take("vec")
    for c in range(KC):
        take(("uT", c))
    for c in range(KC):
        take(("hist", c))
    order = z_order()
    for n, c in enumerate(order):
        take(("z", c))
        if n % 4 == 3 and n < 16:
            for i in range(4):
                take(("gate", n // 4, i), 3 + i)
        if n % 4 == 1 and 4 < n < 20:
            for e in range(2):
                take(("pool", n // 4 - 1, e))
    for w in "ba":
        for c in range(KC):
            take((w, c))
    for half in range(2):
        for t in range(TT):
            take(("out", half, t))
    for i in range(3):
        for h in range(2):
            take(("state", i, h))
    for t in range(TT):
        for h in range(2):
            take(("umT", t, h))
    take("logits")
    take("rank")
    return turns, uses


def plan_tail():
    names = [("pT", t) for t in range(TT)] + [("ple", t, h) for t in range(TT) for h in range(2)]
    for t in range(TT):
        names += [("unT", t, h) for h in range(2)] + [("pg", t, h) for h in range(2)]
    return {name: (n % 8, n // 8) for n, name in enumerate(names)}


def last_product(w, j):
    if w == "in":
        return ("z", [c for c in z_order() if c // 4 == j][-1])
    return ("out", j, TT - 1) if w == "out" else (w, 4 * j + 3)


def hybrid_layer(nc, x_prompt, x_sample, p_prompt, p_sample, state_lru_h, state_conv, state_pool,
                 g_mix, w_in, conv_w, conv_b, w_rg_a, b_rg_a, w_rg_x, b_rg_x, lru_lambda,
                 pool_w, pool_scale, w_proj_a, w_proj_b, w_out, g_moe, w_router, b_router,
                 w_gate_up, b_gate_up, w_down, b_down, g_ple, w_ple_gate, w_ple, g_ple_post, g_final,
                 y_prompt, y_sample, h_prompt, conv_prompt, pool_prompt, h_sample, conv_sample, pool_sample):
    slot_uses, piece_turn = front_uses()
    turns, bank_uses = plan_psum()
    ctx = ExitStack()
    with ctx:
        def sb(name, shape, dt=F32):
            return ctx.enter_context(nc.sbuf_tensor(name, shape, dt))

        def sem(name):
            return ctx.enter_context(nc.semaphore(name))

        y_rows = nc.dram_tensor("moe_rows", (NCH * CAP, D), F32, kind="Internal").ap()
        ps = ctx.enter_context(nc.psum_tensor("ps", [P, 8, 512], F32))
        ring = sb("ring", [P, SLOTS, KC, 512])
        x_tok = sb("x_tok", [P, TT, D])
        u_tok = sb("u_tok", [P, TT, D])
        work = sb("work", [P, 5, KC * NTOK])
        uT, ya, yb, ga, gb = (work[:, i, :].rearrange("p (c t) -> p c t", c=KC) for i in range(5))
        ident = sb("ident", [P, P])
        before = sb("before", [P, P])
        ones = sb("ones", [P, P])
        iota_cap = sb("iota_cap", [P, CAP])
        iota_row = sb("iota_row", [P, NE])
        gate_a = sb("gate_a", [P, KC, P])
        gate_x = sb("gate_x", [P, KC, P])
        poolw = sb("poolw", [P, PG, 2, 256])
        wrouter = sb("wrouter", [P, KC, NE])
        brouter = sb("brouter", [P, NE])
        vec = sb("vec", [P, NVEC])
        lam = sb("lam", [P, 12, KC])
        expert_col = sb("expert_col", [P, NE + 1])
        hist_pool = sb("hist_pool", [P, KC, DB * PB])
        hist_h = sb("hist_h", [P, KC, DB])
        hist_conv = sb("hist_conv", [P, KC, DB * (CONV - 1)])
        tail_a = sb("tail_a", [P, KC, TAIL])
        tail_b = sb("tail_b", [P, KC, TAIL])
        xa = sb("xa", [P, 2, 2 * XA_W])
        mixed = sb("mixed", [P, 2, NTOK])
        inv_count = sb("inv_count", [P, PB])
        stat = sb("stat", [P, 5, 4, TT])
        logits = sb("logits", [P, TT, NE])
        top = sb("top", [P, TT, 8])
        topi = sb("topi", [P, TT, 8], U32)
        topf = sb("topf", [P, TT, 8])
        wts = sb("wts", [P, TT, 8])
        member = sb("member", [P, TT, NE])
        rank_w = sb("rank_w", [P, TT, NE])
        slot = sb("slot", [P, TT, NCH + 1])
        row_f = sb("row_f", [P, TT, TOPK])
        row_i = sb("row_i", [P, TT, TOPK], U32)
        passes_f = sb("passes_f", [P, 4])
        passes_i = sb("passes_i", [P, 1], I32)

        flat_u = u_tok[:].rearrange("p t d -> p (t d)")
        flat_x = x_tok[:].rearrange("p t d -> p (t d)")
        xc, r_, i_, a_ = (flat_u[:, k * 2 * XC_W:(k + 1) * 2 * XC_W].rearrange("p (c w) -> p c w", c=2)
                          for k in range(4))
        xb, s1, s2 = (flat_x[:, k * 2 * XB_W:(k + 1) * 2 * XB_W].rearrange("p (c w) -> p c w", c=2)
                      for k in range(3))
        raw_hist = work[:, 3, 0:D]
        raw_conv = work[:, 3, D:2 * D]
        raw_vec = work[:, 4, 0:P]
        moe = poolw[:].rearrange("p a b c -> p (a b c)")
        xg = moe[:, 0:KC * CAP].rearrange("p (c s) -> p c s", c=KC)
        gate = moe[:, 512:1024]
        up = moe[:, 1024:1536]
        sg = moe[:, 1536:2048]
        hT = gate_a[:].rearrange("p c w -> p (c w)")[:, 0:KC * CAP].rearrange("p (c s) -> p c s", s=CAP)
        x_rows = gate_a[:].rearrange("p c w -> p (c w)")[:, 512:1024]
        o_rows = gate_x[:].rearrange("p c w -> p (c w)")[:, 0:512]
        picks = mixed[:].rearrange("p c t -> p (c t)")
        sel = picks[:, 0:TT * CAP].rearrange("p (t s) -> p t s", s=CAP)
        pick_gu = picks[:, TT * CAP:(TT + 1) * CAP]
        pick_d = picks[:, (TT + 1) * CAP:(TT + 2) * CAP]
        bias = work[:].rearrange("p a b -> p (a b)")[:, KC * NTOK:KC * NTOK + 3 * D]
        onehot = gate_x[:].rearrange("p c w -> p (c w)")[:, 512:512 + TT * TOPK * NE] \
            .rearrange("p (t k e) -> p t k e", t=TT, k=TOPK)
        pick = gate_x[:].rearrange("p c w -> p (c w)")[:, 896:1024].rearrange("p (k e) -> p k e", k=TOPK)
        state_z = work[:, 4, 0:2 * D].rearrange("p (i d) -> p i d", i=2)
        state_h = work[:, 3, 0:D]

        wple = ring[:, MOE_SLOT[2], 0:4, :].rearrange("p a b -> p (a b)").rearrange("p (k c) -> p k c", k=2)
        back = [ring[:, s, :, :].rearrange("p a b -> p (a b)").rearrange("p (k d) -> p k d", k=TOPK)
                for s in MOE_SLOT[3:6]]
        ple = u_tok
        un = work[:].rearrange("p a b -> p (a b)")[:, KC * NTOK:KC * NTOK + TT * D] \
            .rearrange("p (t d) -> p t d", t=TT)
        g_post = work[:, 3, 0:D]
        g_last = work[:, 3, D:2 * D]
        p_tok = work[:, 4, 0:TT * PLE].rearrange("p (t c) -> p t c", t=TT)
        pT = work[:, 4, TT * PLE:TT * PLE + 2 * NTOK].rearrange("p (k t) -> p k t", k=2)
        unT = uT
        y_tok = un
        sig = xa[:].rearrange("p a b -> p (a b)")[:, 0:1024].rearrange("p (b c) -> p b c", b=2)

        landed = [sem(f"ring_landed{s}") for s in range(SLOTS)]
        filled = [sem(f"psum_filled{b}") for b in range(8)]
        emptied = [sem(f"psum_emptied{b}") for b in range(8)]
        x_landed = [sem(f"x_landed{t}") for t in range(TT)]
        raw_landed = sem("raw_landed")
        gates_landed = sem("gates_landed")
        small_landed = sem("small_landed")
        consts_set = sem("consts_set")
        gates_zeroed = sem("gates_zeroed")
        lam_abs = sem("lam_abs")
        lam_exp = sem("lam_exp")
        u_ready = sem("u_ready")
        uT_ready = sem("uT_ready")
        xc_ready = sem("xc_ready")
        decay_ready = sem("decay_ready")
        square_ready = sem("square_ready")
        mult_ready = sem("mult_ready")
        h_scanned = sem("h_scanned")
        ya_ready = sem("ya_ready")
        mixed_ready = sem("mixed_ready")
        merged_ready = sem("merged_ready")
        x_back = sem("x_back")
        um_ready = sem("um_ready")
        umT_ready = sem("umT_ready")
        state_stored = sem("state_stored")
        top_ready = sem("top_ready")
        member_ready = sem("member_ready")
        passes_ready = sem("passes_ready")
        sel_ready = sem("sel_ready")
        pick_gu_ready = sem("pick_gu_ready")
        pick_d_ready = sem("pick_d_ready")
        sig_ready = sem("sig_ready")
        swish_ready = sem("swish_ready")
        hidden_ready = sem("hidden_ready")
        bias_zeroed = sem("bias_zeroed")
        bias_landed = sem("bias_landed")
        rows_filled = sem("rows_filled")
        rows_stored = sem("rows_stored")
        all_rows = sem("all_rows")
        rows_back = [sem(f"rows_back{t}") for t in range(TT)]
        t_landed = sem("tail_weights_landed")
        p_landed = sem("p_landed")
        t_filled = [sem(f"tail_filled{b}") for b in range(8)]
        t_emptied = [sem(f"tail_emptied{b}") for b in range(8)]
        pT_ready = sem("pT_ready")
        un_ready = sem("un_ready")
        unT_ready = sem("unT_ready")
        ple_sig = sem("ple_sig")
        y_ready = sem("y_ready")
        y_stored = sem("y_stored")
        dve_step = sem("dve_step")
        act_step = sem("act_step")
        pool_step = sem("pool_step")
        squares = [sem(f"squares{g}") for g in range(5)]
        means = [sem(f"means{g}") for g in range(5)]
        roots = [sem(f"roots{g}") for g in range(5)]
        lam_set = sem("lam_set")
        stat_set = sem("stat_set")
        pads_set = sem("pads_set")
        x2_ready = sem("x2_ready")
        x3_ready = sem("x3_ready")
        wts_raw = sem("wts_raw")
        tail_stats_set = sem("tail_stats_set")

        def tok(t):
            return slice(t * P, t * P + ROWS[t])

        def prompt_samples(buf, pad):
            return buf[:, pad:pad + SEQ], \
                buf[:, pad + SEQ:pad + SEQ + DB * (pad + DS)].rearrange("p (b w) -> p b w", b=DB)

        def wait_filled(eng, name):
            bank, turn = turns[name]
            eng.wait_ge(filled[bank], turn + 1)
            return bank

        def wait_read(eng, name):
            bank, turn = turns[name]
            eng.wait_ge(emptied[bank], turn + 1)

        tail_turns = plan_tail()

        def wait_tail_filled(eng, name):
            bank, turn = tail_turns[name]
            eng.wait_ge(t_filled[bank], turn + 1)
            return bank

        def wait_tail_read(eng, name):
            bank, turn = tail_turns[name]
            eng.wait_ge(t_emptied[bank], turn + 1)

        class Chain:
            def __init__(self, eng, s):
                self.eng, self.s, self.n = eng, s, 0

            def __call__(self, ins):
                ins.then_inc(self.s, 1)
                self.n += 1
                return self.n

            def need(self, n):
                self.eng.wait_ge(self.s, n)

            def link(self, ins):
                self.need(self(ins))

        FRONT_IN = {"in": w_in[0], "a": w_proj_a[0], "b": w_proj_b[0], "out": w_out[0]}

        block = ctx.enter_context(nc.Block())


        @block.sync
        def _(sp):
            def piece(dst_slot, src):
                return sp.dma_start(ring[:, dst_slot, :, :], src.rearrange("(k p) c -> p k c", p=P))

            def front_piece_used(w, j):
                bank, turn = turns[last_product(w, j)]
                sp.wait_ge(filled[bank], turn + 1)

            holder = {}
            for w, j, s in FRONT:
                if s in holder:
                    front_piece_used(*holder[s])
                piece(s, FRONT_IN[w][:, 512 * j:512 * j + 512]).then_inc(landed[s], 16)
                holder[s] = (w, j)

            gu_rows = w_gate_up[0].rearrange("e k c -> (e k) c")
            dn_rows = w_down[0].rearrange("e k c -> (e k) c")

            def chunk_piece_used(q, n):
                bank = [B_G, B_U, B_O][q // 2]
                sp.wait_ge(filled[bank], n + bank_uses[bank])

            def expert_piece(q, e):
                if q < 4:
                    src = gu_rows[bass.ds(e * D, D), 512 * q:512 * q + 512]
                else:
                    src = dn_rows[bass.ds(e * D, D), (q - 4) * 512:(q - 4) * 512 + 512]
                piece(MOE_SLOT[q], src).then_inc(landed[MOE_SLOT[q]], 16)

            for q in range(6):
                front_piece_used(*holder[MOE_SLOT[q]])
                expert_piece(q, 0)
            with sp.Fori(1, NE) as e:
                for q in range(6):
                    chunk_piece_used(q, e)
                    expert_piece(q, e)
            sp.wait_ge(passes_ready, 1)
            passes = sp.value_load(passes_i[0:1, 0:1], min_val=1, max_val=PASSES)
            with sp.If(passes > 1):
                with sp.Fori(1, passes) as c:
                    with sp.Fori(0, NE) as e:
                        for q in range(6):
                            chunk_piece_used(q, c * NE + e)
                            expert_piece(q, e)
            for half in range(2):
                chunk_piece_used(half, passes * NE)
                piece(MOE_SLOT[half], w_ple_gate[0][:, 512 * half:512 * half + 512]).then_inc(t_landed, 16)
            chunk_piece_used(2, passes * NE)
            sp.dma_start(wple, w_ple[0].rearrange("(k p) c -> p k c", p=P)).then_inc(t_landed, 16)
            for t in range(TT):
                sp.wait_ge(y_ready, t + 1)
                dst = y_prompt[0, P * t:P * t + P, :] if t < 2 else y_sample.rearrange("b t d -> (b t) d")
                sp.dma_start(dst, y_tok[0:ROWS[t], t, :]).then_inc(y_stored, 16)
            sp.wait_ge(y_stored, 16 * TT)

        @block.gpsimd
        def _(pool):
            nc.gpsimd.memset(ident[:], 0.0).then_inc(pool_step, 1)
            nc.gpsimd.memset(before[:], 1.0).then_inc(pool_step, 1)
            pool.wait_ge(pool_step, 2)
            nc.gpsimd.affine_select(out=ident[:], in_=ident[:], compare_op=ALU.not_equal, fill=1.0, base=0,
                                    pattern=[[-1, P]], channel_multiplier=1).then_inc(consts_set, 1)
            nc.gpsimd.affine_select(out=before[:], in_=before[:], compare_op=ALU.is_gt, fill=0.0, base=0,
                                    pattern=[[1, P]], channel_multiplier=-1).then_inc(consts_set, 1)
            nc.gpsimd.memset(ones[:], 1.0).then_inc(consts_set, 1)
            nc.gpsimd.iota(iota_cap[:], pattern=[[1, CAP]], base=0, channel_multiplier=0,
                           allow_small_or_imprecise_dtypes=True).then_inc(consts_set, 1)
            nc.gpsimd.iota(iota_row[:], pattern=[[CAP, NE]], base=0, channel_multiplier=0,
                           allow_small_or_imprecise_dtypes=True).then_inc(consts_set, 1)
            pool.dma_start(pool_sample[0, :, 0:PB - DS, :], state_pool[0, :, DS:PB, :]).then_inc(state_stored, 16)
            pool.wait_ge(mixed_ready, PG)
            for t in range(2):
                pool.dma_start(x_tok[:, t, :], x_prompt[0, P * t:P * t + P, :]).then_inc(x_back, 16)
            pool.dma_start(x_tok[0:32, 2, :], x_sample.rearrange("b t d -> (b t) d")).then_inc(x_back, 16)
            pool.wait_ge(filled[turns[("state", 2, 1)][0]], turns[("state", 2, 1)][1] + 1)
            nc.gpsimd.memset(bias, 0.0).then_inc(bias_zeroed, 1)
            pool.wait_ge(bias_zeroed, 1)
            pool.dma_start(bias[0:NE, 0:2 * D], b_gate_up[0]).then_inc(bias_landed, 16)
            pool.dma_start(bias[0:NE, 2 * D:3 * D], b_down[0]).then_inc(bias_landed, 16)
            for i in range(3):
                for h in range(2):
                    wait_read(pool, ("state", i, h))
            stores = [
                (conv_prompt[0, 0], state_z[13:16, 0, :]),
                (pool_prompt[0, 0], state_z[1:16, 1, :]),
                (h_prompt[0], state_h[15:16, :]),
            ]
            for b in range(DB):
                at = 16 + DS * b
                stores += [(conv_sample[0, b], state_z[at + 1:at + DS, 0, :]),
                           (pool_sample[0, b, PB - DS:PB, :], state_z[at:at + DS, 1, :]),
                           (h_sample[0, b:b + 1, :], state_h[at + DS - 1:at + DS, :])]
            for dst, src in stores:
                pool.dma_start(dst, src).then_inc(state_stored, 16)
            pool.wait_ge(state_stored, 16 * (len(stores) + 1))
            pool.dma_start(g_post, g_ple_post[0:1, :].partition_broadcast(P)).then_inc(p_landed, 16)
            pool.dma_start(g_last, g_final.rearrange("(a d) -> a d", a=1).partition_broadcast(P)) \
                .then_inc(p_landed, 16)
            for t in range(2):
                pool.dma_start(p_tok[:, t, :], p_prompt[0, 0, P * t:P * t + P, :]).then_inc(p_landed, 16)
            pool.dma_start(p_tok[0:32, 2, :], p_sample[0].rearrange("b t d -> (b t) d")).then_inc(p_landed, 16)
            def fetch(rows):
                for t in range(TT):
                    for k in range(TOPK):
                        nc.gpsimd.indirect_dma_start(
                            out=back[t][0:ROWS[t], k, :], out_offset=None, in_=rows,
                            in_offset=bass.IndirectOffsetOnAxis(ap=row_i[0:ROWS[t], t, k:k + 1], axis=0),
                        ).then_inc(rows_back[t], 16)

            pool.wait_ge(passes_ready, 1)
            passes = pool.value_load(passes_i[0:1, 0:1], min_val=1, max_val=PASSES)
            pool.wait_ge(all_rows, 1)
            with pool.If(passes > 1):
                fetch(y_rows)
            with pool.If(passes < 2):
                fetch(y_rows[0:NE * CAP, :])

        @block.tensor
        def _(pe):
            def begin(name):
                bank, turn = turns[name]
                if turn:
                    pe.wait_ge(emptied[bank], turn)
                return bank

            def turn_block(bank, col, src, rows, width=P):
                return pe.transpose(ps[0:width, bank, col:col + rows], src, ident[0:rows, 0:rows])

            def product(name, pairs, out):
                b = begin(name)
                for k, (lhs, rhs) in enumerate(pairs):
                    mm = pe.matmul(out(b), lhs, rhs, start=(k == 0), stop=(k == len(pairs) - 1))
                mm.then_inc(filled[b], 1)

            def wait_piece(w, j):
                s, turn = piece_turn[(w, j)]
                pe.wait_ge(landed[s], 16 * (turn + 1))
                return s

            def channel_block(name, s, c, rhs):
                col = (c % 4) * P
                product(name, [(ring[:, s, k, col:col + P], rhs[:, k, :]) for k in range(KC)],
                        lambda b: ps[:, b, 0:NTOK])

            pe.wait_ge(consts_set, 5)
            pe.wait_ge(raw_landed, 16 * RAW_LOADS)
            b = begin("vec")
            turn_block(b, 0, raw_vec[0:NVEC, :], NVEC).then_inc(filled[b], 1)
            pe.wait_ge(u_ready, TT)
            for c in range(KC):
                b = begin(("uT", c))
                for t in range(TT):
                    mm = turn_block(b, t * P, u_tok[0:ROWS[t], t, c * P:c * P + P], ROWS[t])
                mm.then_inc(filled[b], 1)
            for c in range(KC):
                b = begin(("hist", c))
                turn_block(b, 0, raw_hist[:, c * P:c * P + P], P)
                turn_block(b, P, raw_conv[0:24, c * P:c * P + P], 24).then_inc(filled[b], 1)

            wait_read(pe, ("uT", KC - 2))
            wait_read(pe, ("uT", KC - 1))
            seen = set()
            for n, c in enumerate(z_order()):
                s, _ = piece_turn[("in", c // 4)]
                if c // 4 not in seen:
                    wait_piece("in", c // 4)
                    seen.add(c // 4)
                channel_block(("z", c), s, c, uT)
                if n % 4 == 3 and n < 16:
                    p = n // 4
                    if p == 0:
                        pe.wait_ge(gates_landed, 16 * GATE_LOADS)
                    pe.wait_ge(xc_ready, p + 1)
                    for i in range(4):
                        w = gate_a if i < 2 else gate_x
                        product(("gate", p, i), [(w[:, 2 * p + i % 2, :], xc[:, i % 2, :])],
                                lambda b: ps[:, b, 0:XC_W])
                if n % 4 == 1 and 4 < n < 20:
                    g = n // 4 - 1
                    if g == 0:
                        pe.wait_ge(small_landed, 16 * SMALL_LOADS)
                    pe.wait_ge(mixed_ready, g + 1)
                    for e in range(2):
                        product(("pool", g, e),
                                [(poolw[:, g, k, e * P:e * P + P], mixed[:, k, :]) for k in range(2)],
                                lambda b: ps[:, b, 0:NTOK])
            wait_read(pe, ("pool", PG - 1, 0))
            wait_read(pe, ("pool", PG - 1, 1))
            for c in range(KC):
                s = wait_piece("b", c // 4)
                channel_block(("b", c), s, c, yb)
            pe.wait_ge(ya_ready, PG)
            for c in range(KC):
                s = wait_piece("a", c // 4)
                channel_block(("a", c), s, c, ya)
            pe.wait_ge(merged_ready, KC)
            for half in range(2):
                s = wait_piece("out", half)
                for t in range(TT):
                    product(("out", half, t), [(ga[:, k, tok(t)], ring[:, s, k, :]) for k in range(KC)],
                            lambda b: ps[0:ROWS[t], b, :])
            for i, src in enumerate([tail_a, tail_b, ya[:, :, NTOK - TAIL:NTOK]]):
                for h in range(2):
                    b = begin(("state", i, h))
                    for c in range(4):
                        mm = turn_block(b, c * P, src[:, 4 * h + c, :], P, TAIL)
                    mm.then_inc(filled[b], 1)
            for t in range(TT):
                pe.wait_ge(um_ready, t + 1)
                for h in range(2):
                    b = begin(("umT", t, h))
                    for c in range(4):
                        mm = turn_block(b, c * P, u_tok[0:ROWS[t], t, (4 * h + c) * P:(4 * h + c) * P + P], ROWS[t])
                    mm.then_inc(filled[b], 1)
            for t in range(TT):
                for h in range(2):
                    wait_read(pe, ("umT", t, h))
            b = begin("logits")
            for t in range(TT):
                for k in range(KC):
                    mm = pe.matmul(ps[0:ROWS[t], b, t * NE:t * NE + NE], uT[:, k, tok(t)], wrouter[:, k, :],
                                   start=(k == 0), stop=(k == KC - 1))
            mm.then_inc(filled[b], 1)
            pe.wait_ge(member_ready, TT)
            b = begin("rank")
            for t in range(TT):
                for q in range(t + 1):
                    mm = pe.matmul(ps[:, b, t * NE:t * NE + NE], (before if q == t else ones)[:], member[:, q, :],
                                   start=(q == 0), stop=(q == t))
            for t in range(TT):
                mm = pe.matmul(ps[:, b, TT * NE:TT * NE + NE], ones[:], member[:, t, :],
                               start=(t == 0), stop=(t == TT - 1))
            mm.then_inc(filled[b], 1)

            def begin_chunk(bank, n):
                pe.wait_ge(emptied[bank], n + bank_uses[bank])

            def wait_chunk_piece(q, n):
                s = MOE_SLOT[q]
                pe.wait_ge(landed[s], n * 16 + 16 * (slot_uses[s] + 1))
                return s

            def half(g):
                return slice(g * CAP, g * CAP + CAP)

            def gather(n):
                pe.wait_ge(sel_ready, n + 1)
                begin_chunk(B_X, n)
                for t in range(TT):
                    for g in range(2):
                        mm = pe.matmul(ps[half(g), B_X, :], sel[:, t, :], u_tok[:, t, 512 * g:512 * g + 512],
                                       start=(t == 0), stop=(t == TT - 1))
                mm.then_inc(filled[B_X], 1)

            def turn_rows(bank, src):
                for j in range(4):
                    mm = pe.transpose(ps[:, bank, j * P:j * P + P], src[:, j * P:j * P + P], ident[:])
                mm.then_inc(filled[bank], 1)

            def turn_inputs(n):
                pe.wait_ge(emptied[B_X], n + (bank_uses[B_X] + 1))
                begin_chunk(B_XT, n)
                turn_rows(B_XT, x_rows)

            def bias_rows(bank, pick, at):
                for g in range(2):
                    pe.matmul(ps[half(g), bank, :], pick, bias[:, at + 512 * g:at + 512 * g + 512],
                              start=True, stop=False)

            def weigh(bank, q, n, rows):
                slots = [wait_chunk_piece(q + g, n) for g in range(2)]
                for k in range(KC):
                    for g in range(2):
                        mm = pe.matmul(ps[half(g), bank, :], rows[:, k, :], ring[:, slots[g], k, :],
                                       start=False, stop=(k == KC - 1))
                mm.then_inc(filled[bank], 1)

            gather(0)
            turn_inputs(0)
            pe.wait_ge(bias_landed, 16 * 2)
            pe.wait_ge(passes_ready, 1)
            passes = pe.value_load(passes_i[0:1, 0:1], min_val=1, max_val=PASSES)
            with pe.Fori(0, passes) as c:
                with pe.Fori(0, NE) as e:
                    n = c * NE + e
                    pe.wait_ge(pick_gu_ready, n + 1)
                    begin_chunk(B_G, n)
                    bias_rows(B_G, pick_gu, 0)
                    pe.wait_ge(emptied[B_XT], n + (bank_uses[B_XT] + 1))
                    weigh(B_G, 0, n, xg)
                    begin_chunk(B_U, n)
                    bias_rows(B_U, pick_gu, D)
                    weigh(B_U, 2, n, xg)
                    gather(n + 1)
                    pe.wait_ge(hidden_ready, n + 1)
                    begin_chunk(B_HT, n)
                    turn_rows(B_HT, up)
                    turn_inputs(n + 1)
                    pe.wait_ge(pick_d_ready, n + 1)
                    begin_chunk(B_O, n)
                    bias_rows(B_O, pick_d, 2 * D)
                    pe.wait_ge(emptied[B_HT], n + (bank_uses[B_HT] + 1))
                    weigh(B_O, 4, n, hT)

            def begin_tail(name):
                bank, turn = tail_turns[name]
                if turn:
                    pe.wait_ge(t_emptied[bank], turn)
                return bank

            pe.wait_ge(tail_stats_set, 1)
            pe.wait_ge(all_rows, 1)
            pe.wait_ge(p_landed, 16 * 5)
            for t in range(TT):
                b = begin_tail(("pT", t))
                for k in range(2):
                    mm = turn_block(b, k * P, p_tok[0:ROWS[t], t, k * P:k * P + P], ROWS[t])
                mm.then_inc(t_filled[b], 1)
            pe.wait_ge(t_landed, 16 * 3)
            for t in range(TT):
                wait_tail_read(pe, ("pT", t))
                for half in range(2):
                    b = begin_tail(("ple", t, half))
                    for k in range(2):
                        mm = pe.matmul(ps[0:ROWS[t], b, :], pT[:, k, tok(t)], wple[:, k, 512 * half:512 * half + 512],
                                       start=(k == 0), stop=(k == 1))
                    mm.then_inc(t_filled[b], 1)
            for t in range(TT):
                pe.wait_ge(un_ready, t + 1)
                for h in range(2):
                    b = begin_tail(("unT", t, h))
                    for c in range(4):
                        mm = turn_block(b, c * P, un[0:ROWS[t], t, (4 * h + c) * P:(4 * h + c) * P + P], ROWS[t])
                    mm.then_inc(t_filled[b], 1)
                for h in range(2):
                    wait_tail_read(pe, ("unT", t, h))
                for half in range(2):
                    b = begin_tail(("pg", t, half))
                    for k in range(KC):
                        mm = pe.matmul(ps[0:ROWS[t], b, :], unT[:, k, tok(t)], ring[:, MOE_SLOT[half], k, :],
                                       start=(k == 0), stop=(k == KC - 1))
                    mm.then_inc(t_filled[b], 1)

        @block.scalar
        def _(act):
            step = Chain(act, act_step)

            def emptied_by(ins, bank):
                ins.then_inc(emptied[bank], 1)

            for t in range(2):
                act.dma_start(x_tok[:, t, :], x_prompt[0, P * t:P * t + P, :]).then_inc(x_landed[t], 16)
            act.dma_start(x_tok[0:32, 2, :], x_sample.rearrange("b t d -> (b t) d")).then_inc(x_landed[2], 16)
            vectors = [(V_GMIX, g_mix), (V_CW, conv_w), (V_CB, conv_b), (V_BRA, b_rg_a), (V_BRX, b_rg_x),
                       (V_LAM, lru_lambda), (V_PS, pool_scale), (V_GMOE, g_moe), (V_GPLE, g_ple)]
            loads = []
            for at, v in vectors:
                rows = v.rearrange("a (c p) -> (a c) p", p=P) if v is not conv_w \
                    else v.rearrange("a k (c p) -> (a k c) p", p=P)
                loads.append((raw_vec[at:at + rows.shape[0], :], rows))
            loads.append((raw_hist[0:DB * PB, :], state_pool[0].rearrange("b t d -> (b t) d")))
            loads.append((raw_hist[DB * PB:P, :], state_lru_h[0]))
            loads.append((raw_conv[0:DB * (CONV - 1), :], state_conv[0].rearrange("b t d -> (b t) d")))
            assert len(loads) == RAW_LOADS
            for dst, src in loads:
                act.dma_start(dst, src).then_inc(raw_landed, 16)
            act.wait_ge(gates_zeroed, 2)
            for dst, w in ((gate_a, w_rg_a), (gate_x, w_rg_x)):
                heads = w[0].rearrange("(c q) i j -> q i c j", q=2)
                for q in range(2):
                    act.dma_start(dst[64 * q:64 * q + 64, :, 64 * q:64 * q + 64], heads[q]).then_inc(gates_landed, 16)
            act.dma_start(poolw[:], pool_w[0].rearrange("g (k p) c -> p g k c", p=P)).then_inc(small_landed, 16)
            act.dma_start(wrouter[:], w_router[0].rearrange("(k p) e -> p k e", p=P)).then_inc(small_landed, 16)
            act.dma_start(brouter[:], b_router[0:1, :].partition_broadcast(P)).then_inc(small_landed, 16)

            def square_sums(g, t, src):
                nc.scalar.activation(work[0:ROWS[t], 0, 0:D], src, ACT.Square,
                                     accum_out=stat[0:ROWS[t], g, 0, t:t + 1]).then_inc(squares[g], 1)

            act.wait_ge(stat_set, 1)
            for t in range(TT):
                act.wait_ge(x_landed[t], 16)
                if t:
                    act.wait_ge(squares[0], t)
                square_sums(0, t, x_tok[0:ROWS[t], t, :])
            act.wait_ge(means[0], 1)
            nc.scalar.activation(stat[:, 0, 2, :], stat[:, 0, 1, :], ACT.Sqrt).then_inc(roots[0], 1)
            act.wait_ge(lam_abs, 1)
            nc.scalar.activation(lam[:, 2, :], lam[:, 1, :], ACT.Exp, scale=-1.0).then_inc(lam_exp, 1)

            def z_block(name, buf, pad, hist, tail_buf):
                b = wait_filled(act, name)
                main, samples = prompt_samples(buf, pad)
                nc.scalar.copy(main, ps[:, b, 0:SEQ])
                nc.scalar.copy(samples[:, :, pad:], ps[:, b, SEQ:NTOK].rearrange("p (b t) -> p b t", b=DB))
                nc.scalar.copy(samples[:, :, 0:pad], hist.rearrange("p (b t) -> p b t", b=DB))
                nc.scalar.copy(tail_buf, ps[:, b, NTOK - TAIL:NTOK]).then_inc(emptied[b], 1)

            def z_lru(p, i):
                c = 2 * p + i
                z_block(("z", c), xa[:, p % 2, i * XA_W:(i + 1) * XA_W], CONV - 1, hist_conv[:, c, :],
                        tail_a[:, c, :])

            def z_pool(p, i):
                c = 2 * p + i
                act.wait_ge(mixed_ready, p) if p else act.wait_ge(pads_set, 1)
                z_block(("z", 8 + c), xb[:, i, :], PB, hist_pool[:, c, :], tail_b[:, c, :])

            def lru_gates(p):
                if p:
                    act.wait_ge(h_scanned, p)
                for i in range(4):
                    b = wait_filled(act, ("gate", p, i))
                    c = 2 * p + i % 2
                    dst, bias = (r_, V_BRA) if i < 2 else (i_, V_BRX)
                    nc.scalar.activation(dst[:, i % 2, :], ps[:, b, 0:XC_W], ACT.Sigmoid,
                                         bias=vec[:, bias + c:bias + c + 1]).then_inc(emptied[b], 1)
                if p == 0:
                    act.wait_ge(lam_set, 1)
                for i in range(2):
                    wait_read(act, ("gate", p, i))
                    nc.scalar.activation(a_[:, i, :], r_[:, i, :], ACT.Exp,
                                         scale=lam[:, 6, 2 * p + i:2 * p + i + 1])
                for i in range(2):
                    last = nc.scalar.activation(r_[:, i, :], r_[:, i, :], ACT.Tanh,
                                                scale=lam[:, 7, 2 * p + i:2 * p + i + 1])
                last.then_inc(decay_ready, 1)

            def lru_mult(p):
                act.wait_ge(square_ready, p + 1)
                nc.scalar.activation(r_.rearrange("p c w -> p (c w)"), xa[:, p % 2, 0:2 * XC_W], ACT.Sqrt) \
                    .then_inc(mult_ready, 1)

            def lru_out(p):
                act.wait_ge(h_scanned, p + 1)
                for i in range(2):
                    nc.scalar.copy(ya[:, 2 * p + i, 0:SEQ], xc[:, i, 0:SEQ])
                    last = nc.scalar.copy(ya[:, 2 * p + i, SEQ:NTOK].rearrange("p (b t) -> p b t", b=DB),
                                          xc[:, i, SEQ:XC_W].rearrange("p (b w) -> p b w", b=DB)[:, :, CONV - 1:])
                last.then_inc(ya_ready, 1)

            def pool_out(g):
                for e in range(2):
                    b = wait_filled(act, ("pool", g, e))
                    c = 2 * g + e
                    nc.scalar.activation(yb[:, c, :], ps[:, b, 0:NTOK], ACT.Identity,
                                         scale=vec[:, V_PS + c:V_PS + c + 1]).then_inc(emptied[b], 1)

            def z_gate(c):
                b = wait_filled(act, ("z", c))
                dst = ga[:, c - 16, :] if c < 24 else gb[:, c - 24, :]
                nc.scalar.activation(dst, ps[:, b, 0:NTOK], ACT.Sigmoid).then_inc(emptied[b], 1)

            wait_read(act, ("hist", KC - 2))
            wait_read(act, ("hist", KC - 1))
            wait_read(act, ("hist", KC - 3))
            wait_read(act, ("hist", KC - 4))
            for p in range(4):
                z_lru(p, 0)
                if p:
                    lru_mult(p - 1)
                z_lru(p, 1)
                if p:
                    pool_out(p - 1)
                    lru_out(p - 1)
                z_pool(p, 0)
                z_pool(p, 1)
                lru_gates(p)
            z_gate(16)
            lru_mult(3)
            z_gate(17)
            pool_out(3)
            lru_out(3)
            for c in range(18, 32):
                z_gate(c)

            for i in range(3):
                for h in range(2):
                    b = wait_filled(act, ("state", i, h))
                    dst = state_h[0:TAIL, 512 * h:512 * h + 512] if i == 2 else \
                        state_z[0:TAIL, i, 512 * h:512 * h + 512]
                    nc.scalar.copy(dst, ps[0:TAIL, b, :]).then_inc(emptied[b], 1)

            for t in range(TT):
                for half in range(2):
                    wait_read(act, ("out", half, t))
                if t:
                    act.wait_ge(squares[1], t)
                square_sums(1, t, x_tok[0:ROWS[t], t, :])
            act.wait_ge(means[1], 1)
            nc.scalar.activation(stat[:, 1, 2, :], stat[:, 1, 1, :], ACT.Sqrt).then_inc(roots[1], 1)
            for t in range(TT):
                act.wait_ge(top_ready, t + 1)
                nc.scalar.activation(wts[0:ROWS[t], t, 0:TOPK], top[0:ROWS[t], t, 0:TOPK], ACT.Exp,
                                     bias=wts[0:ROWS[t], t, 6:7],
                                     accum_out=wts[0:ROWS[t], t, 4:5]).then_inc(wts_raw, 1)

            act.wait_ge(passes_ready, 1)
            passes = act.value_load(passes_i[0:1, 0:1], min_val=1, max_val=PASSES)
            with act.If(passes > 1):
                for c in range(1, PASSES):
                    for j in range(NE * CAP // P):
                        at = c * NE * CAP + j * P
                        act.dma_start(y_rows[at:at + P, :], x_tok[:, 0, :]).then_inc(rows_filled, 16)
                act.wait_ge(rows_filled, 16 * (PASSES - 1) * (NE * CAP // P))
            def copy_inputs(n):
                act.wait_ge(filled[B_X], n + (bank_uses[B_X] + 1))
                nc.scalar.copy(x_rows, ps[:, B_X, :]).then_inc(emptied[B_X], 1)

            copy_inputs(0)
            with act.Fori(0, passes) as c:
                with act.Fori(0, NE) as e:
                    n = c * NE + e
                    act.wait_ge(emptied[B_G], n + (bank_uses[B_G] + 1))
                    nc.scalar.activation(sg, gate, ACT.Sigmoid, scale=ALPHA).then_inc(sig_ready, 1)
                    copy_inputs(n + 1)
                    act.wait_ge(filled[B_O], n + (bank_uses[B_O] + 1))
                    nc.scalar.copy(o_rows, ps[:, B_O, :]).then_inc(emptied[B_O], 1)
                    act.wait_ge(emptied[B_O], n + (bank_uses[B_O] + 1))
                    for g in range(2):
                        act.dma_start(y_rows[bass.ds(n * CAP, CAP), 512 * g:512 * g + 512],
                                      o_rows[g * CAP:g * CAP + CAP, :]).then_inc(rows_stored, 16)
                    act.wait_ge(rows_stored, n * 32 + 32)
            act.sem_inc(all_rows, 1)

            for t in range(TT):
                b = wait_tail_filled(act, ("pT", t))
                nc.scalar.copy(pT[:, :, tok(t)], ps[:, b, 0:2 * P].rearrange("p (k t) -> p k t", k=2)[:, :, 0:ROWS[t]]) \
                    .then_inc(t_emptied[b], 1)
            act.wait_ge(tail_stats_set, 1)
            for t in range(TT):
                for half in range(2):
                    b = wait_tail_filled(act, ("ple", t, half))
                    nc.scalar.copy(ple[0:ROWS[t], t, 512 * half:512 * half + 512], ps[0:ROWS[t], b, :]) \
                        .then_inc(t_emptied[b], 1)
                for half in range(2):
                    wait_tail_read(act, ("ple", t, half))
                if t:
                    act.wait_ge(squares[2], t)
                square_sums(2, t, ple[0:ROWS[t], t, :])
            act.wait_ge(means[2], 1)
            nc.scalar.activation(stat[:, 2, 2, :], stat[:, 2, 1, :], ACT.Sqrt).then_inc(roots[2], 1)
            for t in range(TT):
                act.wait_ge(x2_ready, t + 1)
                nc.scalar.activation(back[t][0:ROWS[t], 0, :], x_tok[0:ROWS[t], t, :], ACT.Square,
                                     accum_out=stat[0:ROWS[t], 3, 0, t:t + 1]).then_inc(squares[3], 1)
                act.wait_ge(means[3], t + 1)
                nc.scalar.activation(stat[0:ROWS[t], 3, 2, t:t + 1], stat[0:ROWS[t], 3, 1, t:t + 1], ACT.Sqrt) \
                    .then_inc(roots[3], 1)
            for t in range(TT):
                if t:
                    act.wait_ge(x3_ready, t)
                for half in range(2):
                    b = wait_tail_filled(act, ("pg", t, half))
                    nc.scalar.activation(sig[0:ROWS[t], half, :], ps[0:ROWS[t], b, :], ACT.Sigmoid) \
                        .then_inc(t_emptied[b], 1)
                act.wait_ge(x3_ready, t + 1)
                nc.scalar.activation(back[t][0:ROWS[t], 1, :], x_tok[0:ROWS[t], t, :], ACT.Square,
                                     accum_out=stat[0:ROWS[t], 4, 0, t:t + 1]).then_inc(squares[4], 1)
                act.wait_ge(means[4], t + 1)
                nc.scalar.activation(stat[0:ROWS[t], 4, 2, t:t + 1], stat[0:ROWS[t], 4, 1, t:t + 1], ACT.Sqrt) \
                    .then_inc(roots[4], 1)

        @block.vector
        def _(dve):
            step = Chain(dve, dve_step)
            V = nc.vector

            V.memset(stat[:], 1.0).then_inc(stat_set, 1)
            V.memset(gate_a[:], 0.0).then_inc(gates_zeroed, 1)
            V.memset(gate_x[:], 0.0).then_inc(gates_zeroed, 1)
            V.memset(member[:], 0.0)
            for k in range(PB):
                V.memset(inv_count[:, k:k + 1], 1.0 / (k + 1))
            step.link(V.memset(xa[:].rearrange("p b (c w) -> p (b c) w", c=2)[:, :, 0:CONV - 1], 0.0))

            def mean(g, rows, cols):
                V.tensor_scalar(stat[0:rows, g, 1, cols], stat[0:rows, g, 0, cols], 1.0 / D, EPS,
                                ALU.mult, ALU.add).then_inc(means[g], 1)

            dve.wait_ge(squares[0], TT)
            mean(0, P, slice(0, TT))
            dve.wait_ge(roots[0], 1)
            step.link(V.reciprocal(stat[:, 0, 3, :], stat[:, 0, 2, :]))
            for t in range(TT):
                V.tensor_scalar(u_tok[0:ROWS[t], t, :], x_tok[0:ROWS[t], t, :], stat[0:ROWS[t], 0, 3, t:t + 1], None,
                                ALU.mult).then_inc(u_ready, 1)
            dve.wait_ge(u_ready, TT)
            V.memset(xb[:, :, 0:PB], 0.0).then_inc(pads_set, 1)

            b = wait_filled(dve, "vec")
            V.tensor_copy(vec[:], ps[:, b, 0:NVEC]).then_inc(emptied[b], 1)
            wait_read(dve, "vec")
            for c in range(KC):
                b = wait_filled(dve, ("uT", c))
                V.tensor_scalar(uT[:, c, :], ps[:, b, 0:NTOK], vec[:, V_GMIX + c:V_GMIX + c + 1], None,
                                ALU.mult).then_inc(emptied[b], 1)
            V.tensor_copy(expert_col[:, 0:NE], ident[:, 0:NE])
            V.tensor_copy(expert_col[:, NE:NE + 1], ident[:, 0:1])
            for c in range(KC):
                b = wait_filled(dve, ("hist", c))
                V.tensor_copy(hist_pool[:, c, :], ps[:, b, 0:DB * PB])
                V.tensor_copy(hist_h[:, c, :], ps[:, b, DB * PB:P])
                V.tensor_copy(hist_conv[:, c, :], ps[:, b, P:P + DB * (CONV - 1)]).then_inc(emptied[b], 1)

            lm = vec[:, V_LAM:V_LAM + KC]
            L = [lam[:, k, :] for k in range(12)]
            step.link(V.tensor_scalar(L[0], lm, -1.0, None, ALU.mult))
            V.tensor_tensor(L[1], lm, L[0], ALU.max).then_inc(lam_abs, 1)
            step.link(V.tensor_scalar(L[3], L[0], 0.0, None, ALU.max))
            dve.wait_ge(lam_exp, 1)
            step.link(V.tensor_scalar(L[4], L[2], 2.0, None, ALU.add))
            step.link(V.reciprocal(L[5], L[4]))
            step.link(V.tensor_tensor(L[8], L[2], L[5], ALU.mult))
            step.link(V.tensor_tensor(L[9], L[8], L[8], ALU.mult))
            step.link(V.tensor_scalar(L[10], L[9], 1.0 / 17, None, ALU.mult))
            for m in range(15, 1, -2):
                step.link(V.scalar_tensor_tensor(out=L[10], in0=L[10], scalar=1.0 / m, in1=L[9], op0=ALU.add,
                                                 op1=ALU.mult))
            step.link(V.scalar_tensor_tensor(out=L[11], in0=L[10], scalar=1.0, in1=L[8], op0=ALU.add, op1=ALU.mult))
            step.link(V.scalar_tensor_tensor(out=L[11], in0=L[11], scalar=2.0, in1=L[3], op0=ALU.mult, op1=ALU.add))
            V.tensor_scalar(L[6], L[11], -8.0, None, ALU.mult)
            V.tensor_scalar(L[7], L[11], 8.0, None, ALU.mult).then_inc(lam_set, 1)

            def conv(p):
                for i in range(2):
                    wait_read(dve, ("z", 2 * p + i))
                if p:
                    dve.wait_ge(ya_ready, p)
                before_ = [0, 0]
                for k in range(CONV):
                    for i in range(2):
                        c = 2 * p + i
                        src = xa[:, p % 2, i * XA_W + k:i * XA_W + k + XC_W]
                        w = vec[:, V_CW + k * KC + c:V_CW + k * KC + c + 1]
                        if k == 0:
                            ins = V.tensor_scalar(xc[:, i, :], src, w, vec[:, V_CB + c:V_CB + c + 1],
                                                  ALU.mult, ALU.add)
                        else:
                            step.need(before_[i])
                            ins = V.scalar_tensor_tensor(out=xc[:, i, :], in0=src, scalar=w, in1=xc[:, i, :],
                                                         op0=ALU.mult, op1=ALU.add)
                        if k == CONV - 1 and i == 1:
                            ins.then_inc(xc_ready, 1)
                        else:
                            before_[i] = step(ins)

            def pooling(g):
                for i in range(2):
                    wait_read(dve, ("z", 8 + 2 * g + i))
                src, dst, spare = xb, s1, s2
                for lev in range(g + 1):
                    sh = 1 << lev
                    lo = 2 * sh - 1
                    step.link(V.tensor_tensor(dst[:, :, lo:], src[:, :, lo:], src[:, :, lo - sh:XB_W - sh], ALU.add))
                    src, dst, spare = dst, (spare if lev == 0 else src), None
                w = WIN[g]
                head = src[:, :, PB:PB + w - 1]
                step.link(V.scalar_tensor_tensor(out=head, in0=head, scalar=float(w),
                                                 in1=inv_count[:, 0:w - 1].unsqueeze(1).to_broadcast([P, 2, w - 1]),
                                                 op0=ALU.mult, op1=ALU.mult))
                if g:
                    wait_filled(dve, ("pool", g - 1, 1))
                V.scalar_tensor_tensor(out=mixed[:, :, 0:SEQ], in0=src[:, :, PB:PB + SEQ], scalar=1.0 / w,
                                       in1=xb[:, :, PB:PB + SEQ], op0=ALU.mult, op1=ALU.subtract)
                for i in range(2):
                    own = [prompt_samples(t[:, i, :], PB)[1][:, :, PB:] for t in (src, xb)]
                    last = V.scalar_tensor_tensor(out=mixed[:, i, SEQ:].rearrange("p (b t) -> p b t", b=DB),
                                                  in0=own[0], scalar=1.0 / w, in1=own[1],
                                                  op0=ALU.mult, op1=ALU.subtract)
                last.then_inc(mixed_ready, 1)

            def lru(p):
                dve.wait_ge(decay_ready, p + 1)
                sq = xa[:, p % 2, 0:2 * XC_W]
                flat = [t.rearrange("p c w -> p (c w)") for t in (a_, r_, i_, xc)]
                step.link(V.tensor_tensor(sq, flat[0], flat[0], ALU.mult))
                V.scalar_tensor_tensor(out=sq, in0=sq, scalar=1.0, in1=flat[1], op0=ALU.add, op1=ALU.mult) \
                    .then_inc(square_ready, 1)
                for i in range(2):
                    wait_read(dve, ("gate", p, 2 + i))
                step(V.tensor_tensor(flat[2], flat[2], flat[3], ALU.mult))
                step(V.memset(a_[:, :, SEQ:].rearrange("p c (b w) -> p c b w", b=DB)[:, :, :, CONV - 2:CONV - 1], 0.0))
                dve.wait_ge(mult_ready, p + 1)
                step(V.memset(xa[:, p % 2, :].rearrange("p (c w) -> p c w", c=2)[:, :, 0:CONV - 1], 0.0))
                step.link(V.memset(r_[:, :, 0:1], 1.0))
                step.link(V.tensor_tensor(flat[2], flat[2], flat[1], ALU.mult))
                step.link(V.tensor_copy(i_[:, :, SEQ:].rearrange("p c (b w) -> p c b w", b=DB)[:, :, :, CONV - 2],
                                        hist_h[:, 2 * p:2 * p + 2, :]))
                for i in range(2):
                    last = V.tensor_tensor_scan(out=xc[:, i, :], data0=a_[:, i, :], data1=i_[:, i, :], initial=0.0,
                                                op0=ALU.mult, op1=ALU.add)
                last.then_inc(h_scanned, 1)

            for p in range(4):
                conv(p)
                pooling(p)
                lru(p)

            dve.wait_ge(ya_ready, PG)
            V.memset(u_tok[:, TT - 1, :], 0.0)

            for c in range(KC):
                b = wait_filled(dve, ("b", c))
                wait_read(dve, ("z", 24 + c))
                V.tensor_tensor(gb[:, c, :], gb[:, c, :], ps[:, b, 0:NTOK], ALU.mult).then_inc(emptied[b], 1)
            for c in range(KC):
                b = wait_filled(dve, ("a", c))
                wait_read(dve, ("z", 16 + c))
                V.tensor_tensor(ga[:, c, :], ga[:, c, :], ps[:, b, 0:NTOK], ALU.mult).then_inc(emptied[b], 1)
                wait_read(dve, ("a", c))
                V.tensor_tensor(ga[:, c, :], ga[:, c, :], gb[:, c, :], ALU.add).then_inc(merged_ready, 1)
            dve.wait_ge(x_back, 16 * TT)
            for half in range(2):
                for t in range(TT):
                    b = wait_filled(dve, ("out", half, t))
                    x_half = x_tok[0:ROWS[t], t, 512 * half:512 * half + 512]
                    V.tensor_tensor(x_half, x_half, ps[0:ROWS[t], b, :], ALU.add).then_inc(emptied[b], 1)

            dve.wait_ge(squares[1], TT)
            mean(1, P, slice(0, TT))
            dve.wait_ge(roots[1], 1)
            step.link(V.reciprocal(stat[:, 1, 3, :], stat[:, 1, 2, :]))
            for t in range(TT):
                V.tensor_scalar(u_tok[0:ROWS[t], t, :], x_tok[0:ROWS[t], t, :], stat[0:ROWS[t], 1, 3, t:t + 1], None,
                                ALU.mult).then_inc(um_ready, 1)

            def turned(dst, b, t, at):
                return V.tensor_tensor(dst, ps[:, b, :].rearrange("p (c t) -> p c t", c=4)[:, :, 0:ROWS[t]],
                                       vec[:, at:at + 4].unsqueeze(2).to_broadcast([P, 4, ROWS[t]]), ALU.mult)

            for t in range(TT):
                for h in range(2):
                    b = wait_filled(dve, ("umT", t, h))
                    turned(uT[:, 4 * h:4 * h + 4, tok(t)], b, t, V_GMOE + 4 * h).then_inc(emptied[b], 1)

            b = wait_filled(dve, "logits")
            for t in range(TT):
                R = ROWS[t]
                ins = V.tensor_tensor(logits[0:R, t, :], ps[0:R, b, t * NE:t * NE + NE], brouter[0:R, :], ALU.add)
                if t < TT - 1:
                    step(ins)
            ins.then_inc(emptied[b], 1)
            wait_read(dve, "logits")
            for t in range(TT):
                last = step(V.max(top[0:ROWS[t], t, :], logits[0:ROWS[t], t, :]))
            step.need(last)
            for t in range(TT):
                V.tensor_scalar(wts[0:ROWS[t], t, 6:7], top[0:ROWS[t], t, 0:1], -1.0, None, ALU.mult) \
                    .then_inc(top_ready, 1)
                last = step(V.max_index(topi[0:ROWS[t], t, :], top[0:ROWS[t], t, :], logits[0:ROWS[t], t, :]))
            step.need(last)
            for t in range(TT):
                last = step(V.tensor_copy(topf[0:ROWS[t], t, :], topi[0:ROWS[t], t, :]))
            step.need(last)
            for t in range(TT):
                for k in range(TOPK):
                    last = step(V.tensor_scalar(onehot[0:ROWS[t], t, k, :], iota_cap[0:ROWS[t], 0:NE],
                                                topf[0:ROWS[t], t, k:k + 1], None, ALU.is_equal))
            step.need(last)
            for t in range(TT):
                R = ROWS[t]
                if t:
                    dve.wait_ge(member_ready, t)
                step.link(V.tensor_tensor(pick[0:R, 0:2, :], onehot[0:R, t, 0:2, :], onehot[0:R, t, 2:4, :], ALU.add))
                V.tensor_tensor(member[0:R, t, :], pick[0:R, 0, :], pick[0:R, 1, :], ALU.add) \
                    .then_inc(member_ready, 1)
            b = wait_filled(dve, "rank")
            V.tensor_copy(rank_w[:], ps[:, b, 0:TT * NE].rearrange("p (t e) -> p t e", t=TT))
            V.tensor_reduce(passes_f[0:1, 0:1], ps[0:1, b, TT * NE:TT * NE + NE], AX.X, ALU.max) \
                .then_inc(emptied[b], 1)
            wait_read(dve, "rank")
            step.link(V.scalar_tensor_tensor(out=slot[:, :, 0:NE], in0=rank_w[:], scalar=1.0, in1=member[:],
                                             op0=ALU.add, op1=ALU.mult))
            step.link(V.tensor_scalar(slot[:, :, 0:NE], slot[:, :, 0:NE], -1.0, None, ALU.add))
            for c in range(1, PASSES):
                step(V.tensor_scalar(slot[:, :, c * NE:c * NE + NE], slot[:, :, 0:NE], float(-CAP * c), None, ALU.add))
            step.link(V.memset(slot[:, :, NCH:NCH + 1], -1.0))

            def select(n):
                for t in range(TT):
                    last = V.tensor_scalar(sel[:, t, :], iota_cap[:], slot[:, t, bass.ds(n, 1)]
                                           if not isinstance(n, int) else slot[:, t, n:n + 1], None, ALU.is_equal)
                last.then_inc(sel_ready, 1)

            def pick_expert(dst, e):
                col = expert_col[:, bass.ds(e, 1)] if not isinstance(e, int) else expert_col[:, e:e + 1]
                return V.tensor_copy(dst, col.to_broadcast([P, CAP]))

            select(0)
            pick_expert(pick_gu, 0).then_inc(pick_gu_ready, 1)
            step.link(V.tensor_scalar(pick[0:1, 0, 0:PASSES], iota_row[0:1, 0:PASSES], passes_f[0:1, 0:1], None,
                                      ALU.is_lt))
            step.link(V.tensor_reduce(passes_f[0:1, 1:2], pick[0:1, 0, 0:PASSES], AX.X, ALU.add))
            V.tensor_copy(passes_i[0:1, 0:1], passes_f[0:1, 1:2]).then_inc(passes_ready, 1)
            xg_gain = vec[:, V_GMOE:V_GMOE + KC].unsqueeze(2).to_broadcast([P, KC, CAP])

            def by_channel(bank):
                return ps[:, bank, :].rearrange("p (j g s) -> p g j s", j=4, g=2)

            def in_halves(buf):
                return buf.rearrange("p (g j) s -> p g j s", g=2)

            def gathered(n):
                dve.wait_ge(filled[B_XT], n + (bank_uses[B_XT] + 1))
                V.tensor_tensor(in_halves(xg), by_channel(B_XT), in_halves(xg_gain), ALU.mult) \
                    .then_inc(emptied[B_XT], 1)

            gathered(0)
            over = logits
            step.link(V.tensor_scalar(over[:], rank_w[:], float(CAP), None, ALU.is_ge))
            for c in range(2, PASSES):
                step.link(V.scalar_tensor_tensor(out=over[:], in0=rank_w[:], scalar=float(CAP * c), in1=over[:],
                                                 op0=ALU.is_ge, op1=ALU.add))
            step.link(V.scalar_tensor_tensor(out=over[:], in0=over[:], scalar=float((NE - 1) * CAP), in1=rank_w[:],
                                             op0=ALU.mult, op1=ALU.add))
            step.link(V.tensor_tensor(over[:], over[:], iota_row[:].unsqueeze(1).to_broadcast([P, TT, NE]), ALU.add))
            for t in range(TT):
                R = ROWS[t]
                step.link(V.tensor_tensor(pick[0:R], onehot[0:R, t, :, :],
                                          over[0:R, t, :].unsqueeze(1).to_broadcast([R, TOPK, NE]), ALU.mult))
                step.link(V.tensor_reduce(row_f[0:R, t, :], pick[0:R], AX.X, ALU.add))
                step(V.tensor_copy(row_i[0:R, t, :], row_f[0:R, t, :]))
            dve.wait_ge(wts_raw, TT)
            for t in range(TT):
                R = ROWS[t]
                step.link(V.reciprocal(wts[0:R, t, 5:6], wts[0:R, t, 4:5]))
                step.link(V.tensor_scalar(wts[0:R, t, 0:TOPK], wts[0:R, t, 0:TOPK], wts[0:R, t, 5:6], None, ALU.mult))

            dve.wait_ge(passes_ready, 1)
            passes = dve.value_load(passes_i[0:1, 0:1], min_val=1, max_val=PASSES)
            with dve.Fori(0, passes) as c:
                with dve.Fori(0, NE) as e:
                    n = c * NE + e
                    select(n + 1)
                    dve.wait_ge(filled[B_O], n + bank_uses[B_O])
                    pick_expert(pick_d, e).then_inc(pick_d_ready, 1)
                    dve.wait_ge(filled[B_G], n + (bank_uses[B_G] + 1))
                    V.tensor_scalar(gate, ps[:, B_G, :], LIMIT, None, ALU.min).then_inc(emptied[B_G], 1)
                    dve.wait_ge(sig_ready, n + 1)
                    V.tensor_tensor(gate, gate, sg, ALU.mult).then_inc(swish_ready, 1)
                    dve.wait_ge(filled[B_U], n + (bank_uses[B_U] + 1))
                    V.tensor_scalar(up, ps[:, B_U, :], LIMIT, -LIMIT, ALU.min, ALU.max).then_inc(emptied[B_U], 1)
                    dve.wait_ge(swish_ready, n + 1)
                    dve.wait_ge(emptied[B_U], n + (bank_uses[B_U] + 1))
                    V.scalar_tensor_tensor(out=up, in0=up, scalar=1.0, in1=gate, op0=ALU.add, op1=ALU.mult) \
                        .then_inc(hidden_ready, 1)
                    pick_expert(pick_gu, e + 1).then_inc(pick_gu_ready, 1)
                    dve.wait_ge(filled[B_HT], n + (bank_uses[B_HT] + 1))
                    V.tensor_copy(in_halves(hT), by_channel(B_HT)).then_inc(emptied[B_HT], 1)
                    gathered(n + 1)

            V.memset(stat[:, 2:5, :, :], 1.0).then_inc(tail_stats_set, 1)
            dve.wait_ge(squares[2], TT)
            mean(2, P, slice(0, TT))
            dve.wait_ge(roots[2], 1)
            step.link(V.reciprocal(stat[:, 2, 3, :], stat[:, 2, 2, :]))
            dve.wait_ge(p_landed, 16 * 5)
            for t in range(TT):
                R = ROWS[t]
                step(V.scalar_tensor_tensor(out=ple[0:R, t, :], in0=ple[0:R, t, :], scalar=stat[0:R, 2, 3, t:t + 1],
                                            in1=g_post[0:R, :], op0=ALU.mult, op1=ALU.mult))

            def tile_rms(g, t):
                R = ROWS[t]
                dve.wait_ge(squares[g], t + 1)
                mean(g, R, slice(t, t + 1))
                dve.wait_ge(roots[g], t + 1)
                step.link(V.reciprocal(stat[0:R, g, 3, t:t + 1], stat[0:R, g, 2, t:t + 1]))

            for t in range(TT):
                R = ROWS[t]
                dve.wait_ge(rows_back[t], 16 * TOPK)
                for k in range(TOPK):
                    ins = V.scalar_tensor_tensor(out=x_tok[0:R, t, :], in0=back[t][0:R, k, :],
                                                 scalar=wts[0:R, t, k:k + 1], in1=x_tok[0:R, t, :],
                                                 op0=ALU.mult, op1=ALU.add)
                    if k < TOPK - 1:
                        step.link(ins)
                ins.then_inc(x2_ready, 1)
                tile_rms(3, t)
                V.tensor_scalar(un[0:R, t, :], x_tok[0:R, t, :], stat[0:R, 3, 3, t:t + 1], None, ALU.mult) \
                    .then_inc(un_ready, 1)
                for h in range(2):
                    b = wait_tail_filled(dve, ("unT", t, h))
                    turned(unT[:, 4 * h:4 * h + 4, tok(t)], b, t, V_GPLE + 4 * h).then_inc(t_emptied[b], 1)
            for t in range(TT):
                R = ROWS[t]
                for half in range(2):
                    wait_tail_read(dve, ("pg", t, half))
                    s = sig[0:R, half, :]
                    x_half = x_tok[0:R, t, 512 * half:512 * half + 512]
                    step.link(V.tensor_tensor(s, s, ple[0:R, t, 512 * half:512 * half + 512], ALU.mult))
                    ins = V.tensor_tensor(x_half, x_half, s, ALU.add)
                    if half == 0:
                        step(ins)
                ins.then_inc(x3_ready, 1)
                tile_rms(4, t)
                V.scalar_tensor_tensor(out=y_tok[0:R, t, :], in0=x_tok[0:R, t, :], scalar=stat[0:R, 4, 3, t:t + 1],
                                       in1=g_last[0:R, :], op0=ALU.mult, op1=ALU.mult).then_inc(y_ready, 1)


_INS = ["x_prompt", "x_sample", "p_prompt", "p_sample", "state_lru_h", "state_conv", "state_pool", "g_mix", "w_in",
        "conv_w", "conv_b", "w_rg_a", "b_rg_a", "w_rg_x", "b_rg_x", "lru_lambda", "pool_w", "pool_scale",
        "w_proj_a", "w_proj_b", "w_out", "g_moe", "w_router", "b_router", "w_gate_up", "b_gate_up", "w_down",
        "b_down", "g_ple", "w_ple_gate", "w_ple", "g_ple_post", "g_final"]
_OUTS = [(1, SEQ, D), (DB, DS, D), (1, 1, D), (1, 1, CONV - 1, D), (1, 1, PB, D),
         (1, DB, D), (1, DB, CONV - 1, D), (1, DB, PB, D)]


def kernel(**inputs):
    import numpy as _np
    import concourse.bacc as _bacc
    from concourse import mybir as _mybir
    from concourse.bass_utils import run_bass_kernel_spmd as _run

    nc = _bacc.Bacc("TRN2", target_bir_lowering=False, num_devices=1)
    arrays, args = {}, []
    for name in _INS:
        a = _np.ascontiguousarray(inputs[name])
        arrays[f"in_{name}"] = a
        args.append(nc.dram_tensor(f"in_{name}", a.shape, _mybir.dt.from_np(a.dtype), kind="ExternalInput").ap())
    for i, shape in enumerate(_OUTS):
        args.append(nc.dram_tensor(f"out_{i}", shape, F32, kind="ExternalOutput").ap())
    hybrid_layer(nc, *args)
    r = _run(nc, [arrays], core_ids=[0])
    return tuple(r.results[0][f"out_{i}"] for i in range(len(_OUTS)))
```

```python
from contextlib import ExitStack

import concourse.bass as bass
from concourse import mybir

ALU = mybir.AluOpType
ACT = mybir.ActivationFunctionType
AX = mybir.AxisListType
F32 = mybir.dt.float32
I32 = mybir.dt.int32
U32 = mybir.dt.uint32

P = 128
D = 1024
KC = D // P
SEQ = 256
DB, DS = 8, 4
NTOK = SEQ + DB * DS
TT = 3
ROWS = [128, 128, 32]
TAIL = 48
CONV = 4
PB = 15
PG = 4
WIN = [2, 4, 8, 16]
PLE = 256
EPS = 1e-6
NE = 32
TOPK = 4
CAP = 64
PASSES = -(-NTOK // CAP)
NCH = NE * PASSES
LIMIT, ALPHA = 7.0, 1.702

XA_W = (CONV - 1) + SEQ + DB * (CONV - 1 + DS)
XC_W = XA_W - (CONV - 1)
XB_W = PB + SEQ + DB * (PB + DS)

SLOTS = 6
FRONT = [("in", 0, 0), ("in", 2, 1), ("in", 1, 2), ("in", 3, 3), ("in", 4, 4), ("in", 5, 5),
         ("in", 6, 0), ("in", 7, 1), ("b", 0, 2), ("b", 1, 3), ("a", 0, 4), ("a", 1, 5),
         ("out", 0, 0), ("out", 1, 1)]
MOE_SLOT = [2, 3, 4, 5, 0, 1]

CHUNK_BANK = {"gate": 0, "hT": 0, "xT": 1, "up": 1, "x": 2, "out": 2}
B_S, B_Y = 3, [4, 5, 6]
PAIRS = NE // 2

RAW_LOADS, GATE_LOADS, SMALL_LOADS = 12, 4, 3

V_GMIX, V_CW, V_CB, V_BRA, V_BRX, V_LAM, V_PS, V_GMOE, V_GPLE = 0, 8, 40, 48, 56, 64, 72, 80, 88
NVEC = 96


def front_uses():
    uses, turn = [0] * SLOTS, {}
    for w, j, s in FRONT:
        turn[(w, j)] = (s, uses[s])
        uses[s] += 1
    return uses, turn


def z_order():
    out = []
    for p in range(4):
        out += [2 * p, 2 * p + 1, 8 + 2 * p, 9 + 2 * p]
    return out + list(range(16, 32))


def plan_psum():
    turns, uses = {}, [0] * 8
    ring, at = [0, 1, 2, 7], [0]

    def take(name, bank=None):
        if bank is None:
            bank = ring[at[0] % 4]
            at[0] += 1
        turns[name] = (bank, uses[bank])
        uses[bank] += 1

    take("vec")
    for c in range(KC):
        take(("uT", c))
    for c in range(KC):
        take(("hist", c))
    order = z_order()
    for n, c in enumerate(order):
        take(("z", c))
        if n % 4 == 3 and n < 16:
            for i in range(4):
                take(("gate", n // 4, i), 3 + i)
        if n % 4 == 1 and 4 < n < 20:
            for e in range(2):
                take(("pool", n // 4 - 1, e))
    for w, states in (("b", [0, 1]), ("a", [2])):
        for i in states:
            for h in range(2):
                take(("state", i, h))
        for c in range(KC):
            take((w, c))
    for t in range(TT):
        for half in range(2):
            take(("out", half, t))
    for t in range(TT):
        for h in range(2):
            take(("xT", t, h))
    take("logits")
    for t in range(TT):
        take(("pT", t))
    take("rank")
    for i in range(TT * 2):
        take(("ple", i // 2, i % 2), 3 + i % 5)
    return turns, uses


def plan_tail():
    names = []
    for kind in ("x2T", "pg"):
        names += [(kind, t, h) for t in range(TT) for h in range(2)]
    return {name: (n % 8, n // 8) for n, name in enumerate(names)}


def chunk_turn(kind, n):
    turn = {"gate": 0, "hT": 1, "xT": 0, "up": 1, "x": -1, "out": 2}[kind]
    return CHUNK_BANK[kind], (max(0, 2 * n + turn) if isinstance(n, int) else n * 2 + turn)


def last_product(w, j):
    if w == "in":
        return ("z", [c for c in z_order() if c // 4 == j][-1])
    return ("out", j, TT - 1) if w == "out" else (w, 4 * j + 3)


def hybrid_layer(nc, x_prompt, x_sample, p_prompt, p_sample, state_lru_h, state_conv, state_pool,
                 g_mix, w_in, conv_w, conv_b, w_rg_a, b_rg_a, w_rg_x, b_rg_x, lru_lambda,
                 pool_w, pool_scale, w_proj_a, w_proj_b, w_out, g_moe, w_router, b_router,
                 w_gate_up, b_gate_up, w_down, b_down, g_ple, w_ple_gate, w_ple, g_ple_post, g_final,
                 y_prompt, y_sample, h_prompt, conv_prompt, pool_prompt, h_sample, conv_sample, pool_sample):
    slot_uses, piece_turn = front_uses()
    turns, bank_uses = plan_psum()
    ctx = ExitStack()
    with ctx:
        def sb(name, shape, dt=F32):
            return ctx.enter_context(nc.sbuf_tensor(name, shape, dt))

        def sem(name):
            return ctx.enter_context(nc.semaphore(name))

        ps = ctx.enter_context(nc.psum_tensor("ps", [P, 8, 512], F32))
        ring = sb("ring", [P, SLOTS, KC, 512])
        x_tok = sb("x_tok", [P, TT, D])
        u_tok = sb("u_tok", [P, TT, D])
        work = sb("work", [P, 5, KC * NTOK])
        uT, ya, yb, ga, gb = (work[:, i, :].rearrange("p (c t) -> p c t", c=KC) for i in range(5))
        ident = sb("ident", [P, P])
        before = sb("before", [P, P])
        ones = sb("ones", [P, P])
        iota_cap = sb("iota_cap", [P, CAP])
        iota_pass = sb("iota_pass", [P, PASSES])
        gate_a = sb("gate_a", [P, KC, P])
        gate_x = sb("gate_x", [P, KC, P])
        poolw = sb("poolw", [P, PG, 2, 256])
        wrouter = sb("wrouter", [P, KC, NE])
        brouter = sb("brouter", [P, NE])
        vec = sb("vec", [P, NVEC])
        lam = sb("lam", [P, 12, KC])
        expert_col = sb("expert_col", [P, NE + 1])
        hist_pool = sb("hist_pool", [P, KC, DB * PB])
        hist_h = sb("hist_h", [P, KC, DB])
        hist_conv = sb("hist_conv", [P, KC, DB * (CONV - 1)])
        tail_a = sb("tail_a", [P, KC, TAIL])
        tail_b = sb("tail_b", [P, KC, TAIL])
        xa = sb("xa", [P, 2, 2 * XA_W])
        mixed = sb("mixed", [P, 2, NTOK])
        inv_count = sb("inv_count", [P, PB])
        stat = sb("stat", [P, 5, 4, TT])
        logits = sb("logits", [P, TT, NE])
        top = sb("top", [P, TT, 8])
        topi = sb("topi", [P, TT, 8], U32)
        topf = sb("topf", [P, TT, 8])
        wts = sb("wts", [P, TT, 8])
        member = sb("member", [P, TT, NE])
        comb = sb("comb", [P, TT, NE])
        pick_d = sb("pick_d", [P, CAP])
        slot = sb("slot", [P, TT, NCH + 1])
        passes_f = sb("passes_f", [P, 4])
        passes_i = sb("passes_i", [P, 1], I32)

        flat_u = u_tok[:].rearrange("p t d -> p (t d)")
        flat_x = x_tok[:].rearrange("p t d -> p (t d)")
        xc, r_, i_, a_ = (flat_u[:, k * 2 * XC_W:(k + 1) * 2 * XC_W].rearrange("p (c w) -> p c w", c=2)
                          for k in range(4))
        xb, s1, s2 = (flat_x[:, k * 2 * XB_W:(k + 1) * 2 * XB_W].rearrange("p (c w) -> p c w", c=2)
                      for k in range(3))
        raw_hist = work[:, 3, 0:D]
        raw_conv = work[:, 3, D:2 * D]
        raw_vec = work[:, 4, 0:P]
        flat_w = work[:].rearrange("p a b -> p (a b)")
        state_z = flat_w[:, 0:2 * D].rearrange("p (i d) -> p i d", i=2)
        at = KC * NTOK
        bias = flat_w[:, at:at + 3 * D]
        at += 3 * D
        state_h = flat_w[:, at:at + D]
        g_last = flat_w[:, at:at + D]
        ple = flat_w[:, 5 * KC * NTOK - TT * D:5 * KC * NTOK].rearrange("p (t d) -> p t d", t=TT)
        p_tok = gate_a[:].rearrange("p c w -> p (c w)")[:, 0:TT * PLE].rearrange("p (t c) -> p t c", t=TT)
        g_post = gate_x[:].rearrange("p c w -> p (c w)")
        wple = poolw[:].rearrange("p a b c -> p (a b c)").rearrange("p (k c) -> p k c", k=2)
        pT = mixed
        square_row = xa[:].rearrange("p a b -> p (a b)")[:, 0:D]
        xg = flat_w[:, 0:KC * CAP].rearrange("p (c s) -> p c s", c=KC)
        gate = flat_w[:, 512:1024]
        up = flat_w[:, 1024:1536]
        sg = flat_w[:, 1536:2048]
        sel = flat_w[:, 2048:2048 + TT * CAP].rearrange("p (t s) -> p t s", s=CAP)
        pick_gu = flat_w[:, 2240:2240 + CAP]
        hT = gate_a[:].rearrange("p c w -> p (c w)")[:, 0:KC * CAP].rearrange("p (c s) -> p c s", s=CAP)
        x_rows = gate_a[:].rearrange("p c w -> p (c w)")[:, 512:1024]
        used = poolw[:].rearrange("p a b c -> p (a b c)")
        o_pair = used[:, 0:D]
        sel_w = used[:, D:D + TT * P].rearrange("p (t s) -> p t s", t=TT)
        sel_wT = used[:, D + TT * P:D + 2 * TT * P].rearrange("p (t s) -> p t s", t=TT)
        old_hist = hist_pool[:].rearrange("p c w -> p (c w)")
        onehot = old_hist[:, 0:TT * TOPK * NE].rearrange("p (t k e) -> p t k e", t=TT, k=TOPK)
        weighted = old_hist[:, 384:384 + TT * TOPK * NE].rearrange("p (t k e) -> p t k e", t=TT, k=TOPK)
        below = old_hist[:, 768:768 + PASSES]
        x2 = u_tok

        x2T = ring[:, MOE_SLOT[2], :, 0:NTOK]
        y_tok = ring[:, MOE_SLOT[3], 0:6, :].rearrange("p a b -> p (a b)").rearrange("p (t d) -> p t d", t=TT)
        sig = ring[:, MOE_SLOT[4], 0:2, :]
        square_tail = ring[:, MOE_SLOT[5], 0:2, :].rearrange("p a b -> p (a b)")

        landed = [sem(f"ring_landed{s}") for s in range(SLOTS)]
        filled = [sem(f"psum_filled{b}") for b in range(8)]
        emptied = [sem(f"psum_emptied{b}") for b in range(8)]
        x_landed = [sem(f"x_landed{t}") for t in range(TT)]
        raw_landed = sem("raw_landed")
        gates_landed = sem("gates_landed")
        small_landed = sem("small_landed")
        consts_set = sem("consts_set")
        gates_zeroed = sem("gates_zeroed")
        lam_abs = sem("lam_abs")
        lam_exp = sem("lam_exp")
        u_ready = sem("u_ready")
        uT_ready = sem("uT_ready")
        xc_ready = sem("xc_ready")
        decay_ready = sem("decay_ready")
        square_ready = sem("square_ready")
        mult_ready = sem("mult_ready")
        h_scanned = sem("h_scanned")
        ya_ready = sem("ya_ready")
        mixed_ready = sem("mixed_ready")
        merged_ready = sem("merged_ready")
        x_back = sem("x_back")
        state_stored = sem("state_stored")
        top_ready = sem("top_ready")
        member_ready = sem("member_ready")
        passes_ready = sem("passes_ready")
        sel_ready = sem("sel_ready")
        pick_gu_ready = sem("pick_gu_ready")
        pick_d_ready = sem("pick_d_ready")
        sig_ready = sem("sig_ready")
        swish_ready = sem("swish_ready")
        hidden_ready = sem("hidden_ready")
        bias_zeroed = sem("bias_zeroed")
        bias_landed = sem("bias_landed")
        t_landed = sem("tail_weights_landed")
        p_landed = sem("p_landed")
        g_last_landed = sem("g_last_landed")
        x_cleared = sem("x_cleared")
        x1_copied = sem("x1_copied")
        sel_w_ready = sem("sel_w_ready")
        ple_ready = sem("ple_ready")
        x2_squared = sem("x2_squared")
        t_filled = [sem(f"tail_filled{b}") for b in range(8)]
        t_emptied = [sem(f"tail_emptied{b}") for b in range(8)]
        y_ready = sem("y_ready")
        y_stored = sem("y_stored")
        dve_step = sem("dve_step")
        act_step = sem("act_step")
        pool_step = sem("pool_step")
        squares = [sem(f"squares{g}") for g in range(5)]
        means = [sem(f"means{g}") for g in range(5)]
        roots = [sem(f"roots{g}") for g in range(5)]
        lam_set = sem("lam_set")
        stat_set = sem("stat_set")
        pads_set = sem("pads_set")
        x3_ready = sem("x3_ready")
        wts_raw = sem("wts_raw")

        def tok(t):
            return slice(t * P, t * P + ROWS[t])

        def prompt_samples(buf, pad):
            return buf[:, pad:pad + SEQ], \
                buf[:, pad + SEQ:pad + SEQ + DB * (pad + DS)].rearrange("p (b w) -> p b w", b=DB)

        def wait_filled(eng, name):
            bank, turn = turns[name]
            eng.wait_ge(filled[bank], turn + 1)
            return bank

        def wait_read(eng, name):
            bank, turn = turns[name]
            eng.wait_ge(emptied[bank], turn + 1)

        def begin_chunk(eng, kind, n):
            bank, turn = chunk_turn(kind, n)
            eng.wait_ge(emptied[bank], turn + bank_uses[bank])
            return bank

        def chunk_filled(eng, kind, n):
            bank, turn = chunk_turn(kind, n)
            eng.wait_ge(filled[bank], turn + (bank_uses[bank] + 1))
            return bank

        def chunk_read(eng, kind, n):
            bank, turn = chunk_turn(kind, n)
            eng.wait_ge(emptied[bank], turn + (bank_uses[bank] + 1))

        def pair_bank(i):
            return B_Y[i % 3], i // 3

        tail_turns = plan_tail()

        def wait_tail_filled(eng, name):
            bank, turn = tail_turns[name]
            eng.wait_ge(t_filled[bank], turn + 1)
            return bank

        def wait_tail_read(eng, name):
            bank, turn = tail_turns[name]
            eng.wait_ge(t_emptied[bank], turn + 1)

        class Chain:
            def __init__(self, eng, s):
                self.eng, self.s, self.n = eng, s, 0

            def __call__(self, ins):
                ins.then_inc(self.s, 1)
                self.n += 1
                return self.n

            def need(self, n):
                self.eng.wait_ge(self.s, n)

            def link(self, ins):
                self.need(self(ins))

        FRONT_IN = {"in": w_in[0], "a": w_proj_a[0], "b": w_proj_b[0], "out": w_out[0]}

        block = ctx.enter_context(nc.Block())


        @block.sync
        def _(sp):
            def piece(dst_slot, src):
                return sp.dma_start(ring[:, dst_slot, :, :], src.rearrange("(k p) c -> p k c", p=P))

            def front_piece_used(w, j):
                bank, turn = turns[last_product(w, j)]
                sp.wait_ge(filled[bank], turn + 1)

            for t in range(2):
                sp.dma_start(x_tok[:, t, :], x_prompt[0, P * t:P * t + P, :]).then_inc(x_landed[t], 16)
            sp.dma_start(x_tok[0:32, 2, :], x_sample.rearrange("b t d -> (b t) d")).then_inc(x_landed[2], 16)
            sp.wait_ge(gates_zeroed, 2)
            for dst, w in ((gate_a, w_rg_a), (gate_x, w_rg_x)):
                heads = w[0].rearrange("(c q) i j -> q i c j", q=2)
                for q in range(2):
                    sp.dma_start(dst[64 * q:64 * q + 64, :, 64 * q:64 * q + 64], heads[q]).then_inc(gates_landed, 16)
            sp.wait_ge(raw_landed, 16 * RAW_LOADS)
            holder = {}
            for w, j, s in FRONT:
                if (w, j) == ("in", 1):
                    sp.dma_start(poolw[:], pool_w[0].rearrange("g (k p) c -> p g k c", p=P)).then_inc(small_landed, 16)
                    sp.dma_start(wrouter[:], w_router[0].rearrange("(k p) e -> p k e", p=P)).then_inc(small_landed, 16)
                    sp.dma_start(brouter[:], b_router[0:1, :].partition_broadcast(P)).then_inc(small_landed, 16)
                if s in holder:
                    front_piece_used(*holder[s])
                piece(s, FRONT_IN[w][:, 512 * j:512 * j + 512]).then_inc(landed[s], 16)
                holder[s] = (w, j)

            gu_rows = w_gate_up[0].rearrange("e k c -> (e k) c")
            dn_rows = w_down[0].rearrange("e k c -> (e k) c")

            def chunk_piece_used(q, n):
                chunk_filled(sp, ["gate", "up", "out"][q // 2], n - 1)

            def expert_piece(q, e):
                if q < 4:
                    src = gu_rows[bass.ds(e * D, D), 512 * q:512 * q + 512]
                else:
                    src = dn_rows[bass.ds(e * D, D), (q - 4) * 512:(q - 4) * 512 + 512]
                piece(MOE_SLOT[q], src).then_inc(landed[MOE_SLOT[q]], 16)

            for q in range(6):
                front_piece_used(*holder[MOE_SLOT[q]])
                expert_piece(q, 0)
            with sp.Fori(1, NE) as e:
                for q in range(6):
                    chunk_piece_used(q, e)
                    expert_piece(q, e)
            sp.wait_ge(passes_ready, 1)
            passes = sp.value_load(passes_i[0:1, 0:1], min_val=1, max_val=PASSES)
            with sp.If(passes > 1):
                with sp.Fori(1, passes) as c:
                    with sp.Fori(0, NE) as e:
                        for q in range(6):
                            chunk_piece_used(q, c * NE + e)
                            expert_piece(q, e)
            for half in range(2):
                chunk_piece_used(half, passes * NE)
                piece(MOE_SLOT[half], w_ple_gate[0][:, 512 * half:512 * half + 512]).then_inc(t_landed, 16)
            for t in range(TT):
                sp.wait_ge(y_ready, t + 1)
                dst = y_prompt[0, P * t:P * t + P, :] if t < 2 else y_sample.rearrange("b t d -> (b t) d")
                sp.dma_start(dst, y_tok[0:ROWS[t], t, :]).then_inc(y_stored, 16)
            sp.wait_ge(y_stored, 16 * TT)

        @block.gpsimd
        def _(pool):
            nc.gpsimd.memset(ident[:], 0.0).then_inc(pool_step, 1)
            nc.gpsimd.memset(before[:], 1.0).then_inc(pool_step, 1)
            pool.wait_ge(pool_step, 2)
            nc.gpsimd.affine_select(out=ident[:], in_=ident[:], compare_op=ALU.not_equal, fill=1.0, base=0,
                                    pattern=[[-1, P]], channel_multiplier=1).then_inc(consts_set, 1)
            nc.gpsimd.affine_select(out=before[:], in_=before[:], compare_op=ALU.is_gt, fill=0.0, base=0,
                                    pattern=[[1, P]], channel_multiplier=-1).then_inc(consts_set, 1)
            nc.gpsimd.memset(ones[:], 1.0).then_inc(consts_set, 1)
            nc.gpsimd.iota(iota_cap[:], pattern=[[1, CAP]], base=0, channel_multiplier=0,
                           allow_small_or_imprecise_dtypes=True).then_inc(consts_set, 1)
            nc.gpsimd.iota(iota_pass[:], pattern=[[CAP, PASSES]], base=0, channel_multiplier=0,
                           allow_small_or_imprecise_dtypes=True).then_inc(consts_set, 1)
            pool.dma_start(pool_sample[0, :, 0:PB - DS, :], state_pool[0, :, DS:PB, :]).then_inc(state_stored, 16)
            pool.wait_ge(mixed_ready, PG)
            pool.wait_ge(x_cleared, 1)
            for t in range(2):
                pool.dma_start(x_tok[:, t, :], x_prompt[0, P * t:P * t + P, :]).then_inc(x_back, 16)
            pool.dma_start(x_tok[0:32, 2, :], x_sample.rearrange("b t d -> (b t) d")).then_inc(x_back, 16)
            for i in range(3):
                for h in range(2):
                    wait_read(pool, ("state", i, h))
            stores = [
                (conv_prompt[0, 0], state_z[13:16, 0, :]),
                (pool_prompt[0, 0], state_z[1:16, 1, :]),
                (h_prompt[0], state_h[15:16, :]),
            ]
            for b in range(DB):
                at = 16 + DS * b
                stores += [(conv_sample[0, b], state_z[at + 1:at + DS, 0, :]),
                           (pool_sample[0, b, PB - DS:PB, :], state_z[at:at + DS, 1, :]),
                           (h_sample[0, b:b + 1, :], state_h[at + DS - 1:at + DS, :])]
            for dst, src in stores:
                pool.dma_start(dst, src).then_inc(state_stored, 16)
            pool.wait_ge(state_stored, 16 * (len(stores) + 1))
            pool.dma_start(g_last, g_final.rearrange("(a d) -> a d", a=1).partition_broadcast(P)) \
                .then_inc(g_last_landed, 16)
            for t in range(2):
                pool.dma_start(p_tok[:, t, :], p_prompt[0, 0, P * t:P * t + P, :]).then_inc(p_landed, 16)
            pool.dma_start(p_tok[0:32, 2, :], p_sample[0].rearrange("b t d -> (b t) d")).then_inc(p_landed, 16)
            pool.dma_start(wple, w_ple[0].rearrange("(k p) c -> p k c", p=P)).then_inc(p_landed, 16)
            pool.dma_start(g_post, g_ple_post[0:1, :].partition_broadcast(P)).then_inc(p_landed, 16)
            wait_filled(pool, ("a", KC - 1))
            nc.gpsimd.memset(bias, 0.0).then_inc(bias_zeroed, 1)
            pool.wait_ge(bias_zeroed, 1)
            pool.dma_start(bias[0:NE, 0:2 * D], b_gate_up[0]).then_inc(bias_landed, 16)
            pool.dma_start(bias[0:NE, 2 * D:3 * D], b_down[0]).then_inc(bias_landed, 16)
            pool.wait_ge(g_last_landed, 16)
            pool.wait_ge(p_landed, 16 * 5)
            pool.wait_ge(bias_landed, 16 * 2)

        @block.tensor
        def _(pe):
            def begin(name):
                bank, turn = turns[name]
                if turn:
                    pe.wait_ge(emptied[bank], turn)
                return bank

            def turn_block(bank, col, src, rows, width=P):
                return pe.transpose(ps[0:width, bank, col:col + rows], src, ident[0:rows, 0:rows])

            def product(name, pairs, out):
                b = begin(name)
                for k, (lhs, rhs) in enumerate(pairs):
                    mm = pe.matmul(out(b), lhs, rhs, start=(k == 0), stop=(k == len(pairs) - 1))
                mm.then_inc(filled[b], 1)

            def wait_piece(w, j):
                s, turn = piece_turn[(w, j)]
                pe.wait_ge(landed[s], 16 * (turn + 1))
                return s

            def channel_block(name, s, c, rhs):
                col = (c % 4) * P
                product(name, [(ring[:, s, k, col:col + P], rhs[:, k, :]) for k in range(KC)],
                        lambda b: ps[:, b, 0:NTOK])

            pe.wait_ge(consts_set, 5)
            pe.wait_ge(raw_landed, 16 * RAW_LOADS)
            b = begin("vec")
            turn_block(b, 0, raw_vec[0:NVEC, :], NVEC).then_inc(filled[b], 1)
            pe.wait_ge(u_ready, TT)
            for c in range(KC):
                b = begin(("uT", c))
                for t in range(TT):
                    mm = turn_block(b, t * P, u_tok[0:ROWS[t], t, c * P:c * P + P], ROWS[t])
                mm.then_inc(filled[b], 1)
            for c in range(KC):
                b = begin(("hist", c))
                turn_block(b, 0, raw_hist[:, c * P:c * P + P], P)
                turn_block(b, P, raw_conv[0:24, c * P:c * P + P], 24).then_inc(filled[b], 1)

            wait_read(pe, ("uT", KC - 2))
            wait_read(pe, ("uT", KC - 1))
            seen = set()
            for n, c in enumerate(z_order()):
                s, _ = piece_turn[("in", c // 4)]
                if c // 4 not in seen:
                    wait_piece("in", c // 4)
                    seen.add(c // 4)
                channel_block(("z", c), s, c, uT)
                if n % 4 == 3 and n < 16:
                    p = n // 4
                    if p == 0:
                        pe.wait_ge(gates_landed, 16 * GATE_LOADS)
                    pe.wait_ge(xc_ready, p + 1)
                    for i in range(4):
                        w = gate_a if i < 2 else gate_x
                        product(("gate", p, i), [(w[:, 2 * p + i % 2, :], xc[:, i % 2, :])],
                                lambda b: ps[:, b, 0:XC_W])
                if n % 4 == 1 and 4 < n < 20:
                    g = n // 4 - 1
                    if g == 0:
                        pe.wait_ge(small_landed, 16 * SMALL_LOADS)
                    pe.wait_ge(mixed_ready, g + 1)
                    for e in range(2):
                        product(("pool", g, e),
                                [(poolw[:, g, k, e * P:e * P + P], mixed[:, k, :]) for k in range(2)],
                                lambda b: ps[:, b, 0:NTOK])
            pe.wait_ge(ya_ready, PG)
            def turn_state(i, src):
                for h in range(2):
                    b = begin(("state", i, h))
                    for c in range(4):
                        mm = turn_block(b, c * P, src[:, 4 * h + c, :], P, TAIL)
                    mm.then_inc(filled[b], 1)

            turn_state(0, tail_a)
            turn_state(1, tail_b)
            wait_read(pe, ("pool", PG - 1, 0))
            wait_read(pe, ("pool", PG - 1, 1))
            for c in range(KC):
                s = wait_piece("b", c // 4)
                channel_block(("b", c), s, c, yb)
            turn_state(2, ya[:, :, NTOK - TAIL:NTOK])
            for c in range(KC):
                s = wait_piece("a", c // 4)
                channel_block(("a", c), s, c, ya)
            pe.wait_ge(merged_ready, KC)
            slots = [wait_piece("out", half) for half in range(2)]

            def turn_residual(t):
                for h in range(2):
                    wait_read(pe, ("out", h, t))
                for h in range(2):
                    b = begin(("xT", t, h))
                    for c in range(4):
                        mm = turn_block(b, c * P, x_tok[0:ROWS[t], t, (4 * h + c) * P:(4 * h + c) * P + P], ROWS[t])
                    mm.then_inc(filled[b], 1)

            for t in range(TT):
                for half in range(2):
                    product(("out", half, t), [(ga[:, k, tok(t)], ring[:, slots[half], k, :]) for k in range(KC)],
                            lambda b: ps[0:ROWS[t], b, :])
            for t in range(TT):
                turn_residual(t)
            for t in range(TT):
                for h in range(2):
                    wait_read(pe, ("xT", t, h))
            b = begin("logits")
            for t in range(TT):
                for k in range(KC):
                    mm = pe.matmul(ps[0:ROWS[t], b, t * NE:t * NE + NE], uT[:, k, tok(t)], wrouter[:, k, :],
                                   start=(k == 0), stop=(k == KC - 1))
            mm.then_inc(filled[b], 1)
            pe.wait_ge(p_landed, 16 * 5)
            for t in range(TT):
                b = begin(("pT", t))
                for k in range(2):
                    mm = turn_block(b, k * P, p_tok[0:ROWS[t], t, k * P:k * P + P], ROWS[t])
                mm.then_inc(filled[b], 1)

            def embed(t, half):
                wait_read(pe, ("pT", t))
                product(("ple", t, half), [(pT[:, k, tok(t)], wple[:, k, 512 * half:512 * half + 512])
                                           for k in range(2)], lambda b: ps[0:ROWS[t], b, :])

            for half in range(2):
                embed(0, half)
            pe.wait_ge(member_ready, 1)
            b = begin("rank")
            for t in range(TT):
                for q in range(t + 1):
                    mm = pe.matmul(ps[:, b, t * NE:t * NE + NE], (before if q == t else ones)[:], member[:, q, :],
                                   start=(q == 0), stop=(q == t))
            for t in range(TT):
                mm = pe.matmul(ps[:, b, TT * NE:TT * NE + NE], ones[:], member[:, t, :],
                               start=(t == 0), stop=(t == TT - 1))
            mm.then_inc(filled[b], 1)

            def wait_chunk_piece(q, n):
                s = MOE_SLOT[q]
                pe.wait_ge(landed[s], n * 16 + 16 * (slot_uses[s] + 1))
                return s

            def half(g):
                return slice(g * CAP, g * CAP + CAP)

            def gather(n):
                pe.wait_ge(sel_ready, n + 1)
                b = begin_chunk(pe, "x", n)
                for t in range(TT):
                    for g in range(2):
                        mm = pe.matmul(ps[half(g), b, :], sel[:, t, :], x_tok[:, t, 512 * g:512 * g + 512],
                                       start=(t == 0), stop=(t == TT - 1))
                mm.then_inc(filled[b], 1)

            def turn_rows(kind, n, src):
                b = begin_chunk(pe, kind, n)
                for j in range(4):
                    mm = pe.transpose(ps[:, b, j * P:j * P + P], src[:, j * P:j * P + P], ident[:])
                mm.then_inc(filled[b], 1)

            def begin_sums(kind, n, pick, at):
                b = begin_chunk(pe, kind, n)
                for g in range(2):
                    pe.matmul(ps[half(g), b, :], pick, bias[:, at + 512 * g:at + 512 * g + 512],
                              start=True, stop=False)

            def weigh(kind, q, n, rows):
                b = CHUNK_BANK[kind]
                slots = [wait_chunk_piece(q + g, n) for g in range(2)]
                for k in range(KC):
                    for g in range(2):
                        mm = pe.matmul(ps[half(g), b, :], rows[:, k, :], ring[:, slots[g], k, :],
                                       start=False, stop=(k == KC - 1))
                mm.then_inc(filled[b], 1)

            gather(0)
            embed(1, 0)
            chunk_read(pe, "x", 0)
            turn_rows("xT", 0, x_rows)
            embed(1, 1)
            embed(2, 0)
            embed(2, 1)
            pe.wait_ge(bias_landed, 16 * 2)
            pe.wait_ge(passes_ready, 1)
            passes = pe.value_load(passes_i[0:1, 0:1], min_val=1, max_val=PASSES)
            with pe.Fori(0, passes) as c:
                with pe.Fori(0, PAIRS) as e2:
                    m = c * PAIRS + e2
                    for i in range(2):
                        n = m * 2 + i
                        pe.wait_ge(pick_gu_ready, n + 1)
                        begin_sums("gate", n, pick_gu, 0)
                        chunk_read(pe, "xT", n)
                        weigh("gate", 0, n, xg)
                        begin_sums("up", n, pick_gu, D)
                        weigh("up", 2, n, xg)
                        gather(n + 1)
                        pe.wait_ge(hidden_ready, n + 1)
                        turn_rows("hT", n, up)
                        chunk_read(pe, "x", n + 1)
                        turn_rows("xT", n + 1, x_rows)
                        if i == 1:
                            pe.wait_ge(sel_w_ready, m + 1)
                            pe.wait_ge(emptied[B_S], m + bank_uses[B_S])
                            for t in range(TT):
                                mm = pe.transpose(ps[:, B_S, t * P:t * P + P], sel_w[:, t, :], ident[:])
                            mm.then_inc(filled[B_S], 1)
                        pe.wait_ge(pick_d_ready, n + 1)
                        begin_sums("out", n, pick_d[:], 2 * D)
                        chunk_read(pe, "hT", n)
                        weigh("out", 4, n, hT)
                    pe.wait_ge(emptied[B_S], m + (bank_uses[B_S] + 1))
                    chunk_read(pe, "out", n)
                    for i in range(2 * TT):
                        bank, turn = pair_bank(i)
                        pe.wait_ge(emptied[bank], m * 2 + (bank_uses[bank] + turn))
                        pe.matmul(ps[:, bank, :], sel_wT[:, i // 2, :], o_pair[:, 512 * (i % 2):512 * (i % 2) + 512],
                                  start=True, stop=True).then_inc(filled[bank], 1)

            def begin_tail(name):
                bank, turn = tail_turns[name]
                if turn:
                    pe.wait_ge(t_emptied[bank], turn)
                return bank

            for bank in B_Y:
                pe.wait_ge(emptied[bank], passes * NE + bank_uses[bank])
            for t in range(TT):
                for h in range(2):
                    b = begin_tail(("x2T", t, h))
                    for c in range(4):
                        mm = turn_block(b, c * P, x2[0:ROWS[t], t, (4 * h + c) * P:(4 * h + c) * P + P], ROWS[t])
                    mm.then_inc(t_filled[b], 1)
            pe.wait_ge(t_landed, 16 * 2)
            for t in range(TT):
                for h in range(2):
                    wait_tail_read(pe, ("x2T", t, h))
                for half_ in range(2):
                    b = begin_tail(("pg", t, half_))
                    for k in range(KC):
                        mm = pe.matmul(ps[0:ROWS[t], b, :], x2T[:, k, tok(t)], ring[:, MOE_SLOT[half_], k, :],
                                       start=(k == 0), stop=(k == KC - 1))
                    mm.then_inc(t_filled[b], 1)

        @block.scalar
        def _(act):
            step = Chain(act, act_step)

            def emptied_by(ins, bank):
                ins.then_inc(emptied[bank], 1)

            vectors = [(V_GMIX, g_mix), (V_CW, conv_w), (V_CB, conv_b), (V_BRA, b_rg_a), (V_BRX, b_rg_x),
                       (V_LAM, lru_lambda), (V_PS, pool_scale), (V_GMOE, g_moe), (V_GPLE, g_ple)]
            loads = []
            for at, v in vectors:
                rows = v.rearrange("a (c p) -> (a c) p", p=P) if v is not conv_w \
                    else v.rearrange("a k (c p) -> (a k c) p", p=P)
                loads.append((raw_vec[at:at + rows.shape[0], :], rows))
            loads.append((raw_hist[0:DB * PB, :], state_pool[0].rearrange("b t d -> (b t) d")))
            loads.append((raw_hist[DB * PB:P, :], state_lru_h[0]))
            loads.append((raw_conv[0:DB * (CONV - 1), :], state_conv[0].rearrange("b t d -> (b t) d")))
            assert len(loads) == RAW_LOADS
            for dst, src in loads:
                act.dma_start(dst, src).then_inc(raw_landed, 16)
            def square_sums(g, t, src, scratch):
                nc.scalar.activation(scratch[0:ROWS[t], :], src, ACT.Square,
                                     accum_out=stat[0:ROWS[t], g, 0, t:t + 1]).then_inc(squares[g], 1)

            act.wait_ge(stat_set, 1)
            for t in range(TT):
                act.wait_ge(x_landed[t], 16)
                if t:
                    act.wait_ge(squares[0], t)
                square_sums(0, t, x_tok[0:ROWS[t], t, :], work[:, 0, 0:D])
            act.wait_ge(means[0], 1)
            nc.scalar.activation(stat[:, 0, 2, :], stat[:, 0, 1, :], ACT.Sqrt).then_inc(roots[0], 1)
            act.wait_ge(lam_abs, 1)
            nc.scalar.activation(lam[:, 2, :], lam[:, 1, :], ACT.Exp, scale=-1.0).then_inc(lam_exp, 1)

            def z_block(name, buf, pad, hist, tail_buf):
                b = wait_filled(act, name)
                main, samples = prompt_samples(buf, pad)
                nc.scalar.copy(main, ps[:, b, 0:SEQ])
                nc.scalar.copy(samples[:, :, pad:], ps[:, b, SEQ:NTOK].rearrange("p (b t) -> p b t", b=DB))
                nc.scalar.copy(samples[:, :, 0:pad], hist.rearrange("p (b t) -> p b t", b=DB))
                nc.scalar.copy(tail_buf, ps[:, b, NTOK - TAIL:NTOK]).then_inc(emptied[b], 1)

            def z_lru(p, i):
                c = 2 * p + i
                z_block(("z", c), xa[:, p % 2, i * XA_W:(i + 1) * XA_W], CONV - 1, hist_conv[:, c, :],
                        tail_a[:, c, :])

            def z_pool(p, i):
                c = 2 * p + i
                act.wait_ge(mixed_ready, p) if p else act.wait_ge(pads_set, 1)
                z_block(("z", 8 + c), xb[:, i, :], PB, hist_pool[:, c, :], tail_b[:, c, :])

            def lru_gates(p):
                if p:
                    act.wait_ge(h_scanned, p)
                for i in range(4):
                    b = wait_filled(act, ("gate", p, i))
                    c = 2 * p + i % 2
                    dst, bias = (r_, V_BRA) if i < 2 else (i_, V_BRX)
                    nc.scalar.activation(dst[:, i % 2, :], ps[:, b, 0:XC_W], ACT.Sigmoid,
                                         bias=vec[:, bias + c:bias + c + 1]).then_inc(emptied[b], 1)
                if p == 0:
                    act.wait_ge(lam_set, 1)
                for i in range(2):
                    wait_read(act, ("gate", p, i))
                    nc.scalar.activation(a_[:, i, :], r_[:, i, :], ACT.Exp,
                                         scale=lam[:, 6, 2 * p + i:2 * p + i + 1])
                for i in range(2):
                    last = nc.scalar.activation(r_[:, i, :], r_[:, i, :], ACT.Tanh,
                                                scale=lam[:, 7, 2 * p + i:2 * p + i + 1])
                last.then_inc(decay_ready, 1)

            def lru_mult(p):
                act.wait_ge(square_ready, p + 1)
                nc.scalar.activation(r_.rearrange("p c w -> p (c w)"), xa[:, p % 2, 0:2 * XC_W], ACT.Sqrt) \
                    .then_inc(mult_ready, 1)

            def lru_out(p):
                act.wait_ge(h_scanned, p + 1)
                for i in range(2):
                    nc.scalar.copy(ya[:, 2 * p + i, 0:SEQ], xc[:, i, 0:SEQ])
                    last = nc.scalar.copy(ya[:, 2 * p + i, SEQ:NTOK].rearrange("p (b t) -> p b t", b=DB),
                                          xc[:, i, SEQ:XC_W].rearrange("p (b w) -> p b w", b=DB)[:, :, CONV - 1:])
                last.then_inc(ya_ready, 1)

            def pool_out(g):
                for e in range(2):
                    b = wait_filled(act, ("pool", g, e))
                    c = 2 * g + e
                    nc.scalar.activation(yb[:, c, :], ps[:, b, 0:NTOK], ACT.Identity,
                                         scale=vec[:, V_PS + c:V_PS + c + 1]).then_inc(emptied[b], 1)

            def z_gate(c):
                b = wait_filled(act, ("z", c))
                dst = ga[:, c - 16, :] if c < 24 else gb[:, c - 24, :]
                nc.scalar.activation(dst, ps[:, b, 0:NTOK], ACT.Sigmoid).then_inc(emptied[b], 1)

            wait_read(act, ("hist", KC - 2))
            wait_read(act, ("hist", KC - 1))
            wait_read(act, ("hist", KC - 3))
            wait_read(act, ("hist", KC - 4))
            for p in range(4):
                z_lru(p, 0)
                if p:
                    lru_mult(p - 1)
                z_lru(p, 1)
                if p:
                    pool_out(p - 1)
                    lru_out(p - 1)
                z_pool(p, 0)
                z_pool(p, 1)
                lru_gates(p)
            z_gate(16)
            lru_mult(3)
            z_gate(17)
            pool_out(3)
            lru_out(3)
            for c in range(18, 32):
                z_gate(c)

            for i in range(3):
                for h in range(2):
                    b = wait_filled(act, ("state", i, h))
                    dst = state_h[0:TAIL, 512 * h:512 * h + 512] if i == 2 else \
                        state_z[0:TAIL, i, 512 * h:512 * h + 512]
                    nc.scalar.copy(dst, ps[0:TAIL, b, :]).then_inc(emptied[b], 1)

            for t in range(TT):
                for half in range(2):
                    wait_read(act, ("out", half, t))
                square_sums(1, t, x_tok[0:ROWS[t], t, :], u_tok[:, t, :])
                act.wait_ge(means[1], t + 1)
                nc.scalar.activation(stat[0:ROWS[t], 1, 2, t:t + 1], stat[0:ROWS[t], 1, 1, t:t + 1], ACT.Sqrt) \
                    .then_inc(roots[1], 1)
            act.wait_ge(squares[1], TT)
            for t in range(TT):
                nc.scalar.copy(x2[0:ROWS[t], t, :], x_tok[0:ROWS[t], t, :]).then_inc(x1_copied, 1)
            for t in range(TT):
                b = wait_filled(act, ("pT", t))
                nc.scalar.copy(pT[:, :, tok(t)], ps[:, b, 0:2 * P].rearrange("p (k t) -> p k t", k=2)[:, :, 0:ROWS[t]]) \
                    .then_inc(emptied[b], 1)
            for t in range(TT):
                act.wait_ge(top_ready, t + 1)
                nc.scalar.activation(wts[0:ROWS[t], t, 0:TOPK], top[0:ROWS[t], t, 0:TOPK], ACT.Exp,
                                     bias=wts[0:ROWS[t], t, 6:7],
                                     accum_out=wts[0:ROWS[t], t, 4:5]).then_inc(wts_raw, 1)

            def embedded(t):
                for h in range(2):
                    b = wait_filled(act, ("ple", t, h))
                    nc.scalar.copy(ple[0:ROWS[t], t, 512 * h:512 * h + 512], ps[0:ROWS[t], b, :]) \
                        .then_inc(emptied[b], 1)
                for h in range(2):
                    wait_read(act, ("ple", t, h))
                if t:
                    act.wait_ge(squares[2], t)
                square_sums(2, t, ple[0:ROWS[t], t, :], square_row)

            embedded(0)

            def copy_inputs(n):
                b = chunk_filled(act, "x", n)
                nc.scalar.copy(x_rows, ps[:, b, :]).then_inc(emptied[b], 1)

            copy_inputs(0)
            embedded(1)
            embedded(2)
            act.wait_ge(means[2], 1)
            nc.scalar.activation(stat[:, 2, 2, :], stat[:, 2, 1, :], ACT.Sqrt).then_inc(roots[2], 1)

            act.wait_ge(passes_ready, 1)
            passes = act.value_load(passes_i[0:1, 0:1], min_val=1, max_val=PASSES)
            with act.Fori(0, passes) as c:
                with act.Fori(0, PAIRS) as e2:
                    m = c * PAIRS + e2
                    for i in range(2):
                        n = m * 2 + i
                        chunk_read(act, "gate", n)
                        nc.scalar.activation(sg, gate, ACT.Sigmoid, scale=ALPHA).then_inc(sig_ready, 1)
                        copy_inputs(n + 1)
                        if i == 1:
                            act.wait_ge(filled[B_S], m + (bank_uses[B_S] + 1))
                            nc.scalar.copy(sel_wT.rearrange("p t s -> p (t s)"), ps[:, B_S, 0:TT * P]) \
                                .then_inc(emptied[B_S], 1)
                        b = chunk_filled(act, "out", n)
                        rows = o_pair[CAP * i:CAP * i + CAP, :]
                        nc.scalar.copy(rows[:, 0:512], ps[0:CAP, b, :])
                        nc.scalar.copy(rows[:, 512:1024], ps[CAP:2 * CAP, b, :]).then_inc(emptied[b], 1)

            for t in range(TT):
                for i in range(2 * TT):
                    if i // 2 == t:
                        bank, turn = pair_bank(i)
                        act.wait_ge(emptied[bank], passes * NE + (bank_uses[bank] + turn - 1))
                if t:
                    act.wait_ge(squares[3], t)
                square_sums(3, t, x2[0:ROWS[t], t, :], square_tail)
            act.wait_ge(means[3], 1)
            nc.scalar.activation(stat[:, 3, 2, :], stat[:, 3, 1, :], ACT.Sqrt).then_inc(roots[3], 1)
            act.wait_ge(x2_squared, 1)
            for t in range(TT):
                R = ROWS[t]
                if t:
                    act.wait_ge(x3_ready, t)
                for half in range(2):
                    b = wait_tail_filled(act, ("pg", t, half))
                    nc.scalar.activation(sig[0:R, half, :], ps[0:R, b, :], ACT.Sigmoid,
                                         scale=stat[0:R, 3, 3, t:t + 1]).then_inc(t_emptied[b], 1)
                act.wait_ge(x3_ready, t + 1)
                square_sums(4, t, x2[0:R, t, :], square_tail)
                act.wait_ge(means[4], t + 1)
                nc.scalar.activation(stat[0:R, 4, 2, t:t + 1], stat[0:R, 4, 1, t:t + 1], ACT.Sqrt) \
                    .then_inc(roots[4], 1)

        @block.vector
        def _(dve):
            step = Chain(dve, dve_step)
            V = nc.vector

            V.memset(stat[:], 1.0).then_inc(stat_set, 1)
            V.memset(gate_a[:], 0.0).then_inc(gates_zeroed, 1)
            V.memset(gate_x[:], 0.0).then_inc(gates_zeroed, 1)
            V.memset(topf[:], -1.0)
            V.memset(wts[:], 1.0)
            for k in range(PB):
                V.memset(inv_count[:, k:k + 1], 1.0 / (k + 1))
            step.link(V.memset(xa[:].rearrange("p b (c w) -> p (b c) w", c=2)[:, :, 0:CONV - 1], 0.0))

            def mean(g, rows, cols):
                V.tensor_scalar(stat[0:rows, g, 1, cols], stat[0:rows, g, 0, cols], 1.0 / D, EPS,
                                ALU.mult, ALU.add).then_inc(means[g], 1)

            dve.wait_ge(squares[0], TT)
            mean(0, P, slice(0, TT))
            dve.wait_ge(roots[0], 1)
            step.link(V.reciprocal(stat[:, 0, 3, :], stat[:, 0, 2, :]))
            for t in range(TT):
                V.tensor_scalar(u_tok[0:ROWS[t], t, :], x_tok[0:ROWS[t], t, :], stat[0:ROWS[t], 0, 3, t:t + 1], None,
                                ALU.mult).then_inc(u_ready, 1)
            dve.wait_ge(u_ready, TT)
            V.memset(xb[:, :, 0:PB], 0.0).then_inc(pads_set, 1)

            b = wait_filled(dve, "vec")
            V.tensor_copy(vec[:], ps[:, b, 0:NVEC]).then_inc(emptied[b], 1)
            wait_read(dve, "vec")
            for c in range(KC):
                b = wait_filled(dve, ("uT", c))
                V.tensor_scalar(uT[:, c, :], ps[:, b, 0:NTOK], vec[:, V_GMIX + c:V_GMIX + c + 1], None,
                                ALU.mult).then_inc(emptied[b], 1)
            V.tensor_copy(expert_col[:, 0:NE], ident[:, 0:NE])
            V.tensor_copy(expert_col[:, NE:NE + 1], ident[:, 0:1])
            for c in range(KC):
                b = wait_filled(dve, ("hist", c))
                V.tensor_copy(hist_pool[:, c, :], ps[:, b, 0:DB * PB])
                V.tensor_copy(hist_h[:, c, :], ps[:, b, DB * PB:P])
                V.tensor_copy(hist_conv[:, c, :], ps[:, b, P:P + DB * (CONV - 1)]).then_inc(emptied[b], 1)

            lm = vec[:, V_LAM:V_LAM + KC]
            L = [lam[:, k, :] for k in range(12)]
            step.link(V.tensor_scalar(L[0], lm, -1.0, None, ALU.mult))
            V.tensor_tensor(L[1], lm, L[0], ALU.max).then_inc(lam_abs, 1)
            step.link(V.tensor_scalar(L[3], L[0], 0.0, None, ALU.max))
            dve.wait_ge(lam_exp, 1)
            step.link(V.tensor_scalar(L[4], L[2], 2.0, None, ALU.add))
            step.link(V.reciprocal(L[5], L[4]))
            step.link(V.tensor_tensor(L[8], L[2], L[5], ALU.mult))
            step.link(V.tensor_tensor(L[9], L[8], L[8], ALU.mult))
            step.link(V.tensor_scalar(L[10], L[9], 1.0 / 17, None, ALU.mult))
            for m in range(15, 1, -2):
                step.link(V.scalar_tensor_tensor(out=L[10], in0=L[10], scalar=1.0 / m, in1=L[9], op0=ALU.add,
                                                 op1=ALU.mult))
            step.link(V.scalar_tensor_tensor(out=L[11], in0=L[10], scalar=1.0, in1=L[8], op0=ALU.add, op1=ALU.mult))
            step.link(V.scalar_tensor_tensor(out=L[11], in0=L[11], scalar=2.0, in1=L[3], op0=ALU.mult, op1=ALU.add))
            V.tensor_scalar(L[6], L[11], -8.0, None, ALU.mult)
            V.tensor_scalar(L[7], L[11], 8.0, None, ALU.mult).then_inc(lam_set, 1)

            def conv(p):
                for i in range(2):
                    wait_read(dve, ("z", 2 * p + i))
                if p:
                    dve.wait_ge(ya_ready, p)
                before_ = [0, 0]
                for k in range(CONV):
                    for i in range(2):
                        c = 2 * p + i
                        src = xa[:, p % 2, i * XA_W + k:i * XA_W + k + XC_W]
                        w = vec[:, V_CW + k * KC + c:V_CW + k * KC + c + 1]
                        if k == 0:
                            ins = V.tensor_scalar(xc[:, i, :], src, w, vec[:, V_CB + c:V_CB + c + 1],
                                                  ALU.mult, ALU.add)
                        else:
                            step.need(before_[i])
                            ins = V.scalar_tensor_tensor(out=xc[:, i, :], in0=src, scalar=w, in1=xc[:, i, :],
                                                         op0=ALU.mult, op1=ALU.add)
                        if k == CONV - 1 and i == 1:
                            ins.then_inc(xc_ready, 1)
                        else:
                            before_[i] = step(ins)

            def pooling(g):
                for i in range(2):
                    wait_read(dve, ("z", 8 + 2 * g + i))
                src, dst, spare = xb, s1, s2
                for lev in range(g + 1):
                    sh = 1 << lev
                    lo = 2 * sh - 1
                    step.link(V.tensor_tensor(dst[:, :, lo:], src[:, :, lo:], src[:, :, lo - sh:XB_W - sh], ALU.add))
                    src, dst, spare = dst, (spare if lev == 0 else src), None
                w = WIN[g]
                head = src[:, :, PB:PB + w - 1]
                step.link(V.scalar_tensor_tensor(out=head, in0=head, scalar=float(w),
                                                 in1=inv_count[:, 0:w - 1].unsqueeze(1).to_broadcast([P, 2, w - 1]),
                                                 op0=ALU.mult, op1=ALU.mult))
                if g:
                    wait_filled(dve, ("pool", g - 1, 1))
                V.scalar_tensor_tensor(out=mixed[:, :, 0:SEQ], in0=src[:, :, PB:PB + SEQ], scalar=1.0 / w,
                                       in1=xb[:, :, PB:PB + SEQ], op0=ALU.mult, op1=ALU.subtract)
                for i in range(2):
                    own = [prompt_samples(t[:, i, :], PB)[1][:, :, PB:] for t in (src, xb)]
                    last = V.scalar_tensor_tensor(out=mixed[:, i, SEQ:].rearrange("p (b t) -> p b t", b=DB),
                                                  in0=own[0], scalar=1.0 / w, in1=own[1],
                                                  op0=ALU.mult, op1=ALU.subtract)
                last.then_inc(mixed_ready, 1)

            def lru(p):
                dve.wait_ge(decay_ready, p + 1)
                sq = xa[:, p % 2, 0:2 * XC_W]
                flat = [t.rearrange("p c w -> p (c w)") for t in (a_, r_, i_, xc)]
                step.link(V.tensor_tensor(sq, flat[0], flat[0], ALU.mult))
                V.scalar_tensor_tensor(out=sq, in0=sq, scalar=1.0, in1=flat[1], op0=ALU.add, op1=ALU.mult) \
                    .then_inc(square_ready, 1)
                for i in range(2):
                    wait_read(dve, ("gate", p, 2 + i))
                step(V.tensor_tensor(flat[2], flat[2], flat[3], ALU.mult))
                step(V.memset(a_[:, :, SEQ:].rearrange("p c (b w) -> p c b w", b=DB)[:, :, :, CONV - 2:CONV - 1], 0.0))
                dve.wait_ge(mult_ready, p + 1)
                step(V.memset(xa[:, p % 2, :].rearrange("p (c w) -> p c w", c=2)[:, :, 0:CONV - 1], 0.0))
                step.link(V.memset(r_[:, :, 0:1], 1.0))
                step.link(V.tensor_tensor(flat[2], flat[2], flat[1], ALU.mult))
                step.link(V.tensor_copy(i_[:, :, SEQ:].rearrange("p c (b w) -> p c b w", b=DB)[:, :, :, CONV - 2],
                                        hist_h[:, 2 * p:2 * p + 2, :]))
                for i in range(2):
                    last = V.tensor_tensor_scan(out=xc[:, i, :], data0=a_[:, i, :], data1=i_[:, i, :], initial=0.0,
                                                op0=ALU.mult, op1=ALU.add)
                last.then_inc(h_scanned, 1)

            for p in range(4):
                conv(p)
                pooling(p)
                lru(p)

            dve.wait_ge(mixed_ready, PG)
            V.memset(x_tok[:, TT - 1, :], 0.0).then_inc(x_cleared, 1)

            for c in range(KC):
                b = wait_filled(dve, ("b", c))
                wait_read(dve, ("z", 24 + c))
                V.tensor_tensor(gb[:, c, :], gb[:, c, :], ps[:, b, 0:NTOK], ALU.mult).then_inc(emptied[b], 1)
            for c in range(KC):
                b = wait_filled(dve, ("a", c))
                wait_read(dve, ("z", 16 + c))
                V.tensor_tensor(ga[:, c, :], ga[:, c, :], ps[:, b, 0:NTOK], ALU.mult).then_inc(emptied[b], 1)
                wait_read(dve, ("a", c))
                V.tensor_tensor(ga[:, c, :], ga[:, c, :], gb[:, c, :], ALU.add).then_inc(merged_ready, 1)
            dve.wait_ge(x_back, 16 * TT)

            def turned(dst, bank, t, at):
                return V.tensor_tensor(dst, ps[:, bank, :].rearrange("p (c t) -> p c t", c=4)[:, :, 0:ROWS[t]],
                                       vec[:, at:at + 4].unsqueeze(2).to_broadcast([P, 4, ROWS[t]]), ALU.mult)

            def inverse_root(g, t):
                R = ROWS[t]
                dve.wait_ge(squares[g], t + 1)
                mean(g, R, slice(t, t + 1))
                dve.wait_ge(roots[g], t + 1)
                return V.reciprocal(stat[0:R, g, 3, t:t + 1], stat[0:R, g, 2, t:t + 1])

            for t in range(TT):
                for half in range(2):
                    b = wait_filled(dve, ("out", half, t))
                    x_half = x_tok[0:ROWS[t], t, 512 * half:512 * half + 512]
                    V.tensor_tensor(x_half, x_half, ps[0:ROWS[t], b, :], ALU.add).then_inc(emptied[b], 1)
            dve.wait_ge(state_stored, 16 * (4 + 3 * DB))
            for t in range(TT):
                for h in range(2):
                    b = wait_filled(dve, ("xT", t, h))
                    turned(uT[:, 4 * h:4 * h + 4, tok(t)], b, t, V_GMOE + 4 * h).then_inc(emptied[b], 1)
                step(inverse_root(1, t))

            b = wait_filled(dve, "logits")
            step.need(step.n)
            for t in range(TT):
                R = ROWS[t]
                last = V.scalar_tensor_tensor(out=logits[0:R, t, :], in0=ps[0:R, b, t * NE:t * NE + NE],
                                              scalar=stat[0:R, 1, 3, t:t + 1], in1=brouter[0:R, :],
                                              op0=ALU.mult, op1=ALU.add)
            last.then_inc(emptied[b], 1)
            wait_read(dve, "logits")
            for t in range(TT):
                last = step(V.max(top[0:ROWS[t], t, :], logits[0:ROWS[t], t, :]))
            step.need(last)
            for t in range(TT):
                last = step(V.max_index(topi[0:ROWS[t], t, :], top[0:ROWS[t], t, :], logits[0:ROWS[t], t, :]))
            for t in range(TT):
                V.tensor_scalar(wts[0:ROWS[t], t, 6:7], top[0:ROWS[t], t, 0:1], -1.0, None, ALU.mult) \
                    .then_inc(top_ready, 1)
            step.need(last)
            for t in range(TT):
                last = step(V.tensor_copy(topf[0:ROWS[t], t, :], topi[0:ROWS[t], t, :]))
            step.need(last)
            step.link(V.tensor_tensor(onehot, iota_cap[:, 0:NE].unsqueeze(1).unsqueeze(1)
                                      .to_broadcast([P, TT, TOPK, NE]),
                                      topf[:, :, 0:TOPK].unsqueeze(3).to_broadcast([P, TT, TOPK, NE]), ALU.is_equal))
            V.tensor_reduce(member[:], onehot.rearrange("p t k e -> p t e k"), AX.X, ALU.add) \
                .then_inc(member_ready, 1)
            step.link(V.memset(slot[:, :, NCH:NCH + 1], -1.0))
            b = wait_filled(dve, "rank")
            dve.wait_ge(member_ready, 1)
            step(V.scalar_tensor_tensor(out=slot[:, :, 0:NE],
                                        in0=ps[:, b, 0:TT * NE].rearrange("p (t e) -> p t e", t=TT), scalar=1.0,
                                        in1=member[:], op0=ALU.add, op1=ALU.mult))
            V.tensor_reduce(passes_f[0:1, 0:1], ps[0:1, b, TT * NE:TT * NE + NE], AX.X, ALU.max) \
                .then_inc(emptied[b], 1)
            wait_read(dve, "rank")
            step.link(V.tensor_scalar(slot[:, :, 0:NE], slot[:, :, 0:NE], -1.0, None, ALU.add))

            def select(n):
                for t in range(TT):
                    last = V.tensor_scalar(sel[:, t, :], iota_cap[:], slot[:, t, bass.ds(n, 1)]
                                           if not isinstance(n, int) else slot[:, t, n:n + 1],
                                           stat[:, 1, 3, t:t + 1], ALU.is_equal, ALU.mult)
                last.then_inc(sel_ready, 1)

            def pick_expert(dst, e):
                col = expert_col[:, bass.ds(e, 1)] if not isinstance(e, int) else expert_col[:, e:e + 1]
                return V.tensor_copy(dst, col.to_broadcast([P, CAP]))

            select(0)
            pick_expert(pick_gu, 0).then_inc(pick_gu_ready, 1)
            for c in range(1, PASSES):
                last = step(V.tensor_scalar(slot[:, :, c * NE:c * NE + NE], slot[:, :, 0:NE], float(-CAP * c), None,
                                            ALU.add))
            step.link(V.tensor_scalar(below[0:1, :], iota_pass[0:1, :], passes_f[0:1, 0:1], None, ALU.is_lt))
            step.link(V.tensor_reduce(passes_f[0:1, 1:2], below[0:1, :], AX.X, ALU.add))
            V.tensor_copy(passes_i[0:1, 0:1], passes_f[0:1, 1:2]).then_inc(passes_ready, 1)
            dve.wait_ge(wts_raw, TT)
            step.link(V.reciprocal(wts[:, :, 5:6], wts[:, :, 4:5]))
            step.link(V.tensor_tensor(wts[:, :, 0:TOPK], wts[:, :, 0:TOPK], wts[:, :, 5:6].to_broadcast([P, TT, TOPK]),
                                      ALU.mult))
            step.link(V.tensor_tensor(weighted, onehot, wts[:, :, 0:TOPK].unsqueeze(3)
                                      .to_broadcast([P, TT, TOPK, NE]), ALU.mult))
            step.link(V.tensor_reduce(comb[:], weighted.rearrange("p t k e -> p t e k"), AX.X, ALU.add))

            xg_gain = vec[:, V_GMOE:V_GMOE + KC].unsqueeze(2).to_broadcast([P, KC, CAP])

            def by_channel(bank):
                return ps[:, bank, :].rearrange("p (j g s) -> p g j s", j=4, g=2)

            def in_halves(buf):
                return buf.rearrange("p (g j) s -> p g j s", g=2)

            def gathered(n):
                b = chunk_filled(dve, "xT", n)
                V.tensor_tensor(in_halves(xg), by_channel(b), in_halves(xg_gain), ALU.mult).then_inc(emptied[b], 1)

            gathered(0)
            dve.wait_ge(squares[2], TT)
            mean(2, P, slice(0, TT))
            dve.wait_ge(roots[2], 1)
            step.link(V.reciprocal(stat[:, 2, 3, :], stat[:, 2, 2, :]))
            for t in range(TT):
                R = ROWS[t]
                last = step(V.scalar_tensor_tensor(out=ple[0:R, t, :], in0=ple[0:R, t, :],
                                                   scalar=stat[0:R, 2, 3, t:t + 1], in1=g_post[0:R, :],
                                                   op0=ALU.mult, op1=ALU.mult))
            step.need(last)
            dve.wait_ge(x1_copied, TT)

            dve.wait_ge(passes_ready, 1)
            passes = dve.value_load(passes_i[0:1, 0:1], min_val=1, max_val=PASSES)
            with dve.Fori(0, passes) as c:
                with dve.Fori(0, PAIRS) as e2:
                    m = c * PAIRS + e2
                    for i in range(2):
                        n, e = m * 2 + i, e2 * 2 + i
                        bank, turn = chunk_turn("out", n)
                        dve.wait_ge(filled[bank], turn + (bank_uses[bank] - 1))
                        select(n + 1)
                        pick_expert(pick_d[:], e).then_inc(pick_d_ready, 1)
                        if i == 0:
                            for q in range(2):
                                for t in range(TT):
                                    last = V.tensor_scalar(sel_w[:, t, CAP * q:CAP * q + CAP], iota_cap[:],
                                                           slot[:, t, bass.ds(m * 2 + q, 1)],
                                                           comb[:, t, bass.ds(e2 * 2 + q, 1)],
                                                           ALU.is_equal, ALU.mult)
                            last.then_inc(sel_w_ready, 1)
                        b = chunk_filled(dve, "gate", n)
                        V.tensor_scalar(gate, ps[:, b, :], LIMIT, None, ALU.min).then_inc(emptied[b], 1)
                        dve.wait_ge(sig_ready, n + 1)
                        V.tensor_tensor(gate, gate, sg, ALU.mult).then_inc(swish_ready, 1)
                        b = chunk_filled(dve, "up", n)
                        V.tensor_scalar(up, ps[:, b, :], LIMIT, -LIMIT, ALU.min, ALU.max).then_inc(emptied[b], 1)
                        dve.wait_ge(swish_ready, n + 1)
                        chunk_read(dve, "up", n)
                        V.scalar_tensor_tensor(out=up, in0=up, scalar=1.0, in1=gate, op0=ALU.add, op1=ALU.mult) \
                            .then_inc(hidden_ready, 1)
                        pick_expert(pick_gu, e + 1).then_inc(pick_gu_ready, 1)
                        b = chunk_filled(dve, "hT", n)
                        V.tensor_copy(in_halves(hT), by_channel(b)).then_inc(emptied[b], 1)
                        gathered(n + 1)
                    for i in range(2 * TT):
                        bank, turn = pair_bank(i)
                        dve.wait_ge(filled[bank], m * 2 + (bank_uses[bank] + turn + 1))
                        t, at = i // 2, 512 * (i % 2)
                        x_half = x2[0:ROWS[t], t, at:at + 512]
                        V.tensor_tensor(x_half, x_half, ps[0:ROWS[t], bank, :], ALU.add).then_inc(emptied[bank], 1)

            for t in range(TT):
                for h in range(2):
                    b = wait_tail_filled(dve, ("x2T", t, h))
                    turned(x2T[:, 4 * h:4 * h + 4, tok(t)], b, t, V_GPLE + 4 * h).then_inc(t_emptied[b], 1)
            dve.wait_ge(squares[3], TT)
            mean(3, P, slice(0, TT))
            dve.wait_ge(roots[3], 1)
            V.reciprocal(stat[:, 3, 3, :], stat[:, 3, 2, :]).then_inc(x2_squared, 1)
            dve.wait_ge(g_last_landed, 16)
            for t in range(TT):
                R = ROWS[t]
                for h in range(2):
                    wait_tail_read(dve, ("pg", t, h))
                    s = sig[0:R, h, :]
                    x_half = x2[0:R, t, 512 * h:512 * h + 512]
                    step.link(V.tensor_tensor(s, s, ple[0:R, t, 512 * h:512 * h + 512], ALU.mult))
                    ins = V.tensor_tensor(x_half, x_half, s, ALU.add)
                    if h == 0:
                        step(ins)
                ins.then_inc(x3_ready, 1)
                step.link(inverse_root(4, t))
                V.scalar_tensor_tensor(out=y_tok[0:R, t, :], in0=x2[0:R, t, :], scalar=stat[0:R, 4, 3, t:t + 1],
                                       in1=g_last[0:R, :], op0=ALU.mult, op1=ALU.mult).then_inc(y_ready, 1)


_INS = ["x_prompt", "x_sample", "p_prompt", "p_sample", "state_lru_h", "state_conv", "state_pool", "g_mix", "w_in",
        "conv_w", "conv_b", "w_rg_a", "b_rg_a", "w_rg_x", "b_rg_x", "lru_lambda", "pool_w", "pool_scale",
        "w_proj_a", "w_proj_b", "w_out", "g_moe", "w_router", "b_router", "w_gate_up", "b_gate_up", "w_down",
        "b_down", "g_ple", "w_ple_gate", "w_ple", "g_ple_post", "g_final"]
_OUTS = [(1, SEQ, D), (DB, DS, D), (1, 1, D), (1, 1, CONV - 1, D), (1, 1, PB, D),
         (1, DB, D), (1, DB, CONV - 1, D), (1, DB, PB, D)]


def kernel(**inputs):
    import numpy as _np
    import concourse.bacc as _bacc
    from concourse import mybir as _mybir
    from concourse.bass_utils import run_bass_kernel_spmd as _run

    nc = _bacc.Bacc("TRN2", target_bir_lowering=False, num_devices=1)
    arrays, args = {}, []
    for name in _INS:
        a = _np.ascontiguousarray(inputs[name])
        arrays[f"in_{name}"] = a
        args.append(nc.dram_tensor(f"in_{name}", a.shape, _mybir.dt.from_np(a.dtype), kind="ExternalInput").ap())
    for i, shape in enumerate(_OUTS):
        args.append(nc.dram_tensor(f"out_{i}", shape, F32, kind="ExternalOutput").ap())
    hybrid_layer(nc, *args)
    r = _run(nc, [arrays], core_ids=[0])
    return tuple(r.results[0][f"out_{i}"] for i in range(len(_OUTS)))
```

```python
from contextlib import ExitStack

import concourse.bass as bass
from concourse import mybir

ALU = mybir.AluOpType
ACT = mybir.ActivationFunctionType
AX = mybir.AxisListType
F32 = mybir.dt.float32
BF16 = mybir.dt.bfloat16
I32 = mybir.dt.int32
U32 = mybir.dt.uint32

P = 128
D = 1024
KC = D // P
SEQ = 256
DB, DS = 8, 4
NTOK = SEQ + DB * DS
TT = 3
ROWS = [128, 128, 32]
TAIL = 48
CONV = 4
PB = 15
PG = 4
WIN = [2, 4, 8, 16]
HIST = DB * (PB + 1 + CONV - 1)
PLE = 256
EPS = 1e-6
NE = 32
TOPK = 4
CAP = 64
PASSES = -(-NTOK // CAP)
NCH = NE * PASSES
LIMIT, ALPHA = 7.0, 1.702

XA_W = (CONV - 1) + SEQ + DB * (CONV - 1 + DS)
XC_W = XA_W - (CONV - 1)
XB_W = PB + SEQ + DB * (PB + DS)

SLOTS = 6
FRONT = [("in", 0, 0), ("in", 2, 1), ("in", 1, 2), ("in", 3, 3), ("in", 4, 4), ("in", 5, 5),
         ("in", 6, 0), ("in", 7, 1), ("b", 0, 2), ("b", 1, 3), ("a", 0, 4), ("a", 1, 5),
         ("out", 0, 0), ("out", 1, 1)]
MOE_SLOT = [2, 3, 4, 5, 0, 1]

CHUNK_BANK = {"gate": 0, "hT": 0, "xT": 1, "up": 1, "x": 2, "out": 2}
B_S, B_Y = 3, [4, 5, 6]
PAIRS = NE // 2

GATE_LOADS, SMALL_LOADS = 4, 3

V_GMIX, V_CW, V_CB, V_BRA, V_BRX, V_LAM, V_PS, V_GMOE, V_GPLE = 0, 8, 40, 48, 56, 64, 72, 80, 88
NVEC = 96


def front_pieces():
    uses, turn = [0] * SLOTS, {}
    for w, j, s in FRONT:
        turn[(w, j)] = (s, uses[s])
        uses[s] += 1
    return turn


def z_order():
    out = []
    for p in range(4):
        out += [2 * p, 2 * p + 1, 8 + 2 * p, 9 + 2 * p]
    return out + list(range(16, 32))


def plan_psum():
    turns, uses = {}, [0] * 8
    ring, at = [0, 1, 2, 7], [0]

    def take(name, bank=None):
        if bank is None:
            bank = ring[at[0] % 4]
            at[0] += 1
        turns[name] = (bank, uses[bank])
        uses[bank] += 1

    take("vec")
    for c in range(KC):
        take(("uT", c))
    order = z_order()
    for n, c in enumerate(order):
        take(("z", c))
        if n == 0:
            for i in range(3):
                take(("hist", i), 4 + i)
        if n % 4 == 3 and n < 16:
            for i in range(4):
                take(("gate", n // 4, i), 3 + i)
        if n % 4 == 1 and 4 < n < 20:
            for e in range(2):
                take(("pool", n // 4 - 1, e))
    for w, states in (("b", [0, 1]), ("a", [2])):
        for i in states:
            for h in range(2):
                take(("state", i, h))
        if w == "a":
            for t in range(TT):
                take(("pT", t))
        for c in range(KC):
            take((w, c))
    for t in range(TT):
        for half in range(2):
            take(("out", half, t))
        for h in range(2):
            if t:
                take(("xT", t - 1, h))
    take("logits")
    for h in range(2):
        take(("xT", TT - 1, h))
    take(("ple", 0, 0), 3)
    take(("ple", 0, 1), 4)
    take("rank")
    for i, name in enumerate([("ple", 2, 0), ("ple", 2, 1), ("ple", 1, 0), ("ple", 1, 1)]):
        take(name, 5 + i if i < 2 else 3 + i - 2)
    return turns, uses


def plan_tail():
    names = []
    for kind in ("x2T", "pg"):
        names += [(kind, t, h) for t in range(TT) for h in range(2)]
    return {name: (n % 8, n // 8) for n, name in enumerate(names)}


def chunk_turn(kind, n):
    turn = {"gate": 0, "hT": 1, "xT": 0, "up": 1, "x": -1, "out": 2}[kind]
    return CHUNK_BANK[kind], (max(0, 2 * n + turn) if isinstance(n, int) else n * 2 + turn)


def last_product(w, j):
    if w == "in":
        return ("z", [c for c in z_order() if c // 4 == j][-1])
    return ("out", j, TT - 1) if w == "out" else (w, 4 * j + 3)


def hybrid_layer(nc, x_prompt, x_sample, p_prompt, p_sample, state_lru_h, state_conv, state_pool,
                 g_mix, w_in, conv_w, conv_b, w_rg_a, b_rg_a, w_rg_x, b_rg_x, lru_lambda,
                 pool_w, pool_scale, w_proj_a, w_proj_b, w_out, g_moe, w_router, b_router,
                 w_gate_up, b_gate_up, w_down, b_down, g_ple, w_ple_gate, w_ple, g_ple_post, g_final,
                 y_prompt, y_sample, h_prompt, conv_prompt, pool_prompt, h_sample, conv_sample, pool_sample):
    piece_turn = front_pieces()
    turns, bank_uses = plan_psum()
    ctx = ExitStack()
    with ctx:
        def sb(name, shape, dt=F32):
            return ctx.enter_context(nc.sbuf_tensor(name, shape, dt))

        def sem(name):
            return ctx.enter_context(nc.semaphore(name))

        ps = ctx.enter_context(nc.psum_tensor("ps", [P, 8, 512], F32))
        ring = sb("ring", [P, SLOTS, KC, 512])
        x_tok = sb("x_tok", [P, TT, D])
        u_tok = sb("u_tok", [P, TT, D])
        work = sb("work", [P, 5, KC * NTOK])
        uT, ya, yb, ga, gb = (work[:, i, :].rearrange("p (c t) -> p c t", c=KC) for i in range(5))
        ident = sb("ident", [P, P])
        before = sb("before", [P, P], BF16)
        ones = sb("ones", [P, P], BF16)
        iota_cap = sb("iota_cap", [P, CAP])
        iota_pass = sb("iota_pass", [P, PASSES])
        gate_a = sb("gate_a", [P, KC, P])
        gate_x = sb("gate_x", [P, KC, P])
        poolw = sb("poolw", [P, PG, 2, 256])
        wrouter = sb("wrouter", [P, KC, NE])
        brouter = sb("brouter", [P, NE])
        vec = sb("vec", [P, NVEC])
        lam = sb("lam", [P, 12, KC])
        expert_col = sb("expert_col", [P, NE + 1])
        hist = sb("hist", [P, KC, HIST])
        hist_pool, hist_h, hist_conv = (hist[:, :, a:b] for a, b in
                                        ((0, DB * PB), (DB * PB, P), (P, HIST)))
        tail_a = sb("tail_a", [P, KC, TAIL])
        tail_b = sb("tail_b", [P, KC, TAIL])
        xa = sb("xa", [P, 2, 2 * XA_W])
        mixed = sb("mixed", [P, 2, NTOK])
        inv_count = sb("inv_count", [P, PB])
        stat = sb("stat", [P, 5, 4, TT])
        root_spare = sb("root_spare", [P, TT])
        sig_spare = sb("sig_spare", [P, TT])
        logits = sb("logits", [P, TT, NE])
        top = sb("top", [P, TT, 8])
        topi = sb("topi", [P, TT, 8], U32)
        topf = sb("topf", [P, TT, 8])
        wts = sb("wts", [P, TT, 8])
        chosen = sb("chosen", [P, TT, NE])
        member = sb("member", [P, TT, NE], BF16)
        comb = sb("comb", [P, TT, NE])
        pick_d = sb("pick_d", [P, CAP])
        slot = sb("slot", [P, TT, NCH + 1])
        passes_f = sb("passes_f", [P, 4])
        passes_i = sb("passes_i", [P, 1], I32)

        flat_u = u_tok[:].rearrange("p t d -> p (t d)")
        flat_x = x_tok[:].rearrange("p t d -> p (t d)")
        xc, r_, i_, a_ = (flat_u[:, k * 2 * XC_W:(k + 1) * 2 * XC_W].rearrange("p (c w) -> p c w", c=2)
                          for k in range(4))
        xb, s1, s2 = (flat_x[:, k * 2 * XB_W:(k + 1) * 2 * XB_W].rearrange("p (c w) -> p c w", c=2)
                      for k in range(3))
        raw_hist = work[:, 3, 0:D]
        raw_conv = work[:, 3, D:2 * D]
        raw_vec = work[:, 4, 0:P]
        flat_w = work[:].rearrange("p a b -> p (a b)")
        state_z = flat_w[:, 0:2 * D].rearrange("p (i d) -> p i d", i=2)
        at = KC * NTOK
        bias = flat_w[:, at:at + 3 * D]
        at += 3 * D
        state_h = flat_w[:, at:at + D]
        g_last = flat_w[:, at:at + D]
        ple = flat_w[:, 5 * KC * NTOK - TT * D:5 * KC * NTOK].rearrange("p (t d) -> p t d", t=TT)
        g_post = gate_x[:].rearrange("p c w -> p (c w)")
        p_tok = gate_a[:].rearrange("p c w -> p (c w)")[:, 0:TT * PLE].rearrange("p (t c) -> p t c", t=TT)
        wple = poolw[:].rearrange("p a b c -> p (a b c)").rearrange("p (k c) -> p k c", k=2)
        pT = mixed
        square_row = xa[:].rearrange("p a b -> p (a b)")[:, 0:D]
        xg = flat_w[:, 0:KC * CAP].rearrange("p (c s) -> p c s", c=KC)
        gate = flat_w[:, 512:1024]
        up = flat_w[:, 1024:1536]
        sg = flat_w[:, 1536:2048]
        sel = flat_w[:, 2048:2048 + TT * CAP].rearrange("p (t s) -> p t s", s=CAP)
        pick_gu = flat_w[:, 2240:2240 + CAP]
        hT = gate_a[:].rearrange("p c w -> p (c w)")[:, 0:KC * CAP].rearrange("p (c s) -> p c s", s=CAP)
        x_rows = gate_a[:].rearrange("p c w -> p (c w)")[:, 512:1024]
        used = poolw[:].rearrange("p a b c -> p (a b c)")
        o_pair = used[:, 0:D]
        sel_w = used[:, D:D + TT * P].rearrange("p (t s) -> p t s", t=TT)
        sel_wT = used[:, D + TT * P:D + 2 * TT * P].rearrange("p (t s) -> p t s", t=TT)
        old_hist = hist[:].rearrange("p c w -> p (c w)")
        onehot = old_hist[:, 0:TT * TOPK * NE].rearrange("p (t k e) -> p t k e", t=TT, k=TOPK)
        weighted = old_hist[:, 384:384 + TT * TOPK * NE].rearrange("p (t k e) -> p t k e", t=TT, k=TOPK)
        below = old_hist[:, 768:768 + PASSES]
        x2 = u_tok

        x2T = ring[:, MOE_SLOT[2], :, 0:NTOK]
        y_tok = ring[:, MOE_SLOT[3], 0:6, :].rearrange("p a b -> p (a b)").rearrange("p (t d) -> p t d", t=TT)
        sig = ring[:, MOE_SLOT[4], 0:2, :]
        square_tail = ring[:, MOE_SLOT[5], 0:2, :].rearrange("p a b -> p (a b)")

        landed = [sem(f"ring_landed{s}") for s in range(SLOTS)]
        filled = [sem(f"psum_filled{b}") for b in range(8)]
        emptied = [sem(f"psum_emptied{b}") for b in range(8)]
        x_landed = [sem(f"x_landed{t}") for t in range(TT)]
        quarter_landed = [sem(f"quarter_landed{q}") for q in range(12)]
        quarter_used_up = [[sem(f"quarter_used_{m}{r}") for r in range(3)] for m in ("gate", "up", "down")]
        vec_landed = [sem(f"vec_landed{i}") for i in range(2)]
        hist_landed = sem("hist_landed")
        gates_landed = sem("gates_landed")
        small_landed = sem("small_landed")
        consts_set = sem("consts_set")
        gates_zeroed = sem("gates_zeroed")
        lam_abs = sem("lam_abs")
        lam_exp = sem("lam_exp")
        u_ready = sem("u_ready")
        xc_ready = sem("xc_ready")
        decay_ready = sem("decay_ready")
        square_ready = sem("square_ready")
        mult_ready = sem("mult_ready")
        h_scanned = sem("h_scanned")
        ya_ready = sem("ya_ready")
        mixed_ready = sem("mixed_ready")
        merged_ready = sem("merged_ready")
        x_back = sem("x_back")
        state_stored = sem("state_stored")
        top_ready = sem("top_ready")
        member_ready = sem("member_ready")
        passes_ready = sem("passes_ready")
        sel_ready = sem("sel_ready")
        pick_gu_ready = sem("pick_gu_ready")
        pick_d_ready = sem("pick_d_ready")
        sig_ready = sem("sig_ready")
        swish_ready = sem("swish_ready")
        hidden_ready = sem("hidden_ready")
        bias_zeroed = sem("bias_zeroed")
        bias_landed = sem("bias_landed")
        t_landed = sem("tail_weights_landed")
        p_landed = sem("p_landed")
        g_last_landed = sem("g_last_landed")
        g_post_landed = sem("g_post_landed")
        x_cleared = sem("x_cleared")
        x1_copied = sem("x1_copied")
        sel_w_ready = sem("sel_w_ready")
        x2_squared = sem("x2_squared")
        t_filled = [sem(f"tail_filled{b}") for b in range(8)]
        t_emptied = [sem(f"tail_emptied{b}") for b in range(8)]
        y_ready = sem("y_ready")
        y_stored = sem("y_stored")
        dve_step = sem("dve_step")
        act_step = sem("act_step")
        pool_step = sem("pool_step")
        squares = [sem(f"squares{g}") for g in range(5)]
        means = [sem(f"means{g}") for g in range(5)]
        roots = [sem(f"roots{g}") for g in range(5)]
        lam_set = sem("lam_set")
        stat_set = sem("stat_set")
        pads_set = sem("pads_set")
        x3_ready = sem("x3_ready")
        wts_raw = sem("wts_raw")

        def tok(t):
            return slice(t * P, t * P + ROWS[t])

        def prompt_samples(buf, pad):
            return buf[:, pad:pad + SEQ], \
                buf[:, pad + SEQ:pad + SEQ + DB * (pad + DS)].rearrange("p (b w) -> p b w", b=DB)

        def quarter(q):
            rows = ring[:, MOE_SLOT[q // 2], :, :].rearrange("p a b -> p (a b)").rearrange("p (k c) -> p k c", k=4)
            return rows[:, 2 * (q % 2):2 * (q % 2) + 2, :]

        def column_half(name):
            t, half = (name[2], name[1]) if name[0] == "out" else (name[1], name[2])
            at = ROWS[t] * half if t == TT - 1 else 0
            return slice(at, at + ROWS[t])

        def wait_filled(eng, name):
            bank, turn = turns[name]
            eng.wait_ge(filled[bank], turn + 1)
            return bank

        def wait_read(eng, name):
            bank, turn = turns[name]
            eng.wait_ge(emptied[bank], turn + 1)

        def begin_chunk(eng, kind, n):
            bank, turn = chunk_turn(kind, n)
            eng.wait_ge(emptied[bank], turn + bank_uses[bank])
            return bank

        def chunk_filled(eng, kind, n):
            bank, turn = chunk_turn(kind, n)
            eng.wait_ge(filled[bank], turn + (bank_uses[bank] + 1))
            return bank

        def chunk_read(eng, kind, n):
            bank, turn = chunk_turn(kind, n)
            eng.wait_ge(emptied[bank], turn + (bank_uses[bank] + 1))

        def pair_bank(i):
            return B_Y[i % 3], i // 3

        tail_turns = plan_tail()

        def wait_tail_filled(eng, name):
            bank, turn = tail_turns[name]
            eng.wait_ge(t_filled[bank], turn + 1)
            return bank

        def wait_tail_read(eng, name):
            bank, turn = tail_turns[name]
            eng.wait_ge(t_emptied[bank], turn + 1)

        class Chain:
            def __init__(self, eng, s):
                self.eng, self.s, self.n = eng, s, 0

            def __call__(self, ins):
                ins.then_inc(self.s, 1)
                self.n += 1
                return self.n

            def need(self, n):
                self.eng.wait_ge(self.s, n)

            def link(self, ins):
                self.need(self(ins))

        FRONT_IN = {"in": w_in[0], "a": w_proj_a[0], "b": w_proj_b[0], "out": w_out[0]}

        vectors = [(V_GMIX, g_mix), (V_CW, conv_w), (V_CB, conv_b), (V_BRA, b_rg_a), (V_BRX, b_rg_x),
                   (V_LAM, lru_lambda), (V_PS, pool_scale), (V_GMOE, g_moe), (V_GPLE, g_ple)]

        shares = [vectors[:5], vectors[5:]]

        def load_vectors(eng, part):
            for at, v in shares[part]:
                rows = v.rearrange("a (c p) -> (a c) p", p=P) if v is not conv_w \
                    else v.rearrange("a k (c p) -> (a k c) p", p=P)
                eng.dma_start(raw_vec[at:at + rows.shape[0], :], rows).then_inc(vec_landed[part], 16)

        block = ctx.enter_context(nc.Block())


        @block.sync
        def _(sp):
            def piece(dst_slot, src):
                return sp.dma_start(ring[:, dst_slot, :, :], src.rearrange("(k p) c -> p k c", p=P))

            def front_piece_used(w, j):
                bank, turn = turns[last_product(w, j)]
                sp.wait_ge(filled[bank], turn + 1)

            for t in range(2):
                sp.dma_start(x_tok[:, t, :], x_prompt[0, P * t:P * t + P, :]).then_inc(x_landed[t], 16)
            sp.dma_start(x_tok[0:32, 2, :], x_sample.rearrange("b t d -> (b t) d")).then_inc(x_landed[2], 16)
            sp.wait_ge(gates_zeroed, 2)
            for dst, w in ((gate_a, w_rg_a), (gate_x, w_rg_x)):
                heads = w[0].rearrange("(c q) i j -> q i c j", q=2)
                for q in range(2):
                    sp.dma_start(dst[64 * q:64 * q + 64, :, 64 * q:64 * q + 64], heads[q]).then_inc(gates_landed, 16)
            for i in range(2):
                sp.wait_ge(vec_landed[i], 16 * len(shares[i]))
            holder = {}
            for w, j, s in FRONT:
                if (w, j) == ("in", 1):
                    sp.wait_ge(hist_landed, 16 * 3)
                    sp.dma_start(poolw[:], pool_w[0].rearrange("g (k p) c -> p g k c", p=P)).then_inc(small_landed, 16)
                    sp.dma_start(wrouter[:], w_router[0].rearrange("(k p) e -> p k e", p=P)).then_inc(small_landed, 16)
                    sp.dma_start(brouter[:], b_router[0:1, :].partition_broadcast(P)).then_inc(small_landed, 16)
                if s in holder:
                    front_piece_used(*holder[s])
                piece(s, FRONT_IN[w][:, 512 * j:512 * j + 512]).then_inc(landed[s], 16)
                holder[s] = (w, j)

            gu_rows = w_gate_up[0].rearrange("e k c -> (e k) c")
            dn_rows = w_down[0].rearrange("e k c -> (e k) c")

            def quarter_used(q, n):
                if q % 4 < 3:
                    sp.wait_ge(quarter_used_up[q // 4][q % 4], n)
                else:
                    chunk_filled(sp, ["gate", "up", "out"][q // 4], n - 1)

            def expert_quarter(q, e):
                rows = bass.ds(e * D + 256 * (q % 4), 256)
                src = gu_rows[rows, D * (q // 4):D * (q // 4) + D] if q < 8 else dn_rows[rows, :]
                sp.dma_start(quarter(q), src.rearrange("(k p) c -> p k c", p=P)).then_inc(quarter_landed[q], 16)

            for q in range(12):
                if q % 2 == 0:
                    front_piece_used(*holder[MOE_SLOT[q // 2]])
                expert_quarter(q, 0)
            with sp.Fori(1, NE) as e:
                for q in range(12):
                    quarter_used(q, e)
                    expert_quarter(q, e)
            sp.wait_ge(passes_ready, 1)
            passes = sp.value_load(passes_i[0:1, 0:1], min_val=1, max_val=PASSES)
            with sp.If(passes > 1):
                with sp.Fori(1, passes) as c:
                    with sp.Fori(0, NE) as e:
                        for q in range(12):
                            quarter_used(q, c * NE + e)
                            expert_quarter(q, e)
            for q in range(4):
                quarter_used(q, passes * NE)
                sp.dma_start(quarter(q), w_ple_gate[0][256 * q:256 * q + 256, :]
                             .rearrange("(k p) c -> p k c", p=P)).then_inc(t_landed, 16)
            for t in range(TT):
                sp.wait_ge(y_ready, t + 1)
                dst = y_prompt[0, P * t:P * t + P, :] if t < 2 else y_sample.rearrange("b t d -> (b t) d")
                sp.dma_start(dst, y_tok[0:ROWS[t], t, :]).then_inc(y_stored, 16)
            sp.wait_ge(y_stored, 16 * TT)

        @block.gpsimd
        def _(pool):
            nc.gpsimd.memset(ident[:], 0.0).then_inc(pool_step, 1)
            nc.gpsimd.memset(before[:], 1.0).then_inc(pool_step, 1)
            pool.wait_ge(pool_step, 2)
            nc.gpsimd.affine_select(out=ident[:], in_=ident[:], compare_op=ALU.not_equal, fill=1.0, base=0,
                                    pattern=[[-1, P]], channel_multiplier=1).then_inc(consts_set, 1)
            nc.gpsimd.affine_select(out=before[:], in_=before[:], compare_op=ALU.is_gt, fill=0.0, base=0,
                                    pattern=[[1, P]], channel_multiplier=-1).then_inc(consts_set, 1)
            nc.gpsimd.memset(ones[:], 1.0).then_inc(consts_set, 1)
            nc.gpsimd.iota(iota_cap[:], pattern=[[1, CAP]], base=0, channel_multiplier=0,
                           allow_small_or_imprecise_dtypes=True).then_inc(consts_set, 1)
            nc.gpsimd.iota(iota_pass[:], pattern=[[CAP, PASSES]], base=0, channel_multiplier=0,
                           allow_small_or_imprecise_dtypes=True).then_inc(consts_set, 1)
            load_vectors(pool, 1)
            for dst, src in ((raw_hist[0:DB * PB, :], state_pool[0].rearrange("b t d -> (b t) d")),
                             (raw_hist[DB * PB:P, :], state_lru_h[0]),
                             (raw_conv[0:DB * (CONV - 1), :], state_conv[0].rearrange("b t d -> (b t) d"))):
                pool.dma_start(dst, src).then_inc(hist_landed, 16)
            pool.dma_start(pool_sample[0, :, 0:PB - DS, :], state_pool[0, :, DS:PB, :]).then_inc(state_stored, 16)
            pool.wait_ge(mixed_ready, PG)
            pool.wait_ge(x_cleared, 1)
            for t in range(2):
                pool.dma_start(x_tok[:, t, :], x_prompt[0, P * t:P * t + P, :]).then_inc(x_back, 16)
            pool.dma_start(x_tok[0:32, 2, :], x_sample.rearrange("b t d -> (b t) d")).then_inc(x_back, 16)
            wait_filled(pool, ("gate", 3, 3))
            wait_filled(pool, ("pool", 3, 1))
            for t in range(2):
                pool.dma_start(p_tok[:, t, :], p_prompt[0, 0, P * t:P * t + P, :]).then_inc(p_landed, 16)
            pool.dma_start(p_tok[0:32, 2, :], p_sample[0].rearrange("b t d -> (b t) d")).then_inc(p_landed, 16)
            pool.dma_start(wple, w_ple[0].rearrange("(k p) c -> p k c", p=P)).then_inc(p_landed, 16)
            pool.dma_start(g_post, g_ple_post[0:1, :].partition_broadcast(P)).then_inc(g_post_landed, 16)
            for i in range(3):
                for h in range(2):
                    wait_read(pool, ("state", i, h))
            stores = [
                (conv_prompt[0, 0], state_z[13:16, 0, :]),
                (pool_prompt[0, 0], state_z[1:16, 1, :]),
                (h_prompt[0], state_h[15:16, :]),
            ]
            for b in range(DB):
                at = 16 + DS * b
                stores += [(conv_sample[0, b], state_z[at + 1:at + DS, 0, :]),
                           (pool_sample[0, b, PB - DS:PB, :], state_z[at:at + DS, 1, :]),
                           (h_sample[0, b:b + 1, :], state_h[at + DS - 1:at + DS, :])]
            for dst, src in stores:
                pool.dma_start(dst, src).then_inc(state_stored, 16)
            pool.wait_ge(state_stored, 16 * (len(stores) + 1))
            pool.dma_start(g_last, g_final.rearrange("(a d) -> a d", a=1).partition_broadcast(P)) \
                .then_inc(g_last_landed, 16)
            wait_filled(pool, ("a", KC - 1))
            nc.gpsimd.memset(bias, 0.0).then_inc(bias_zeroed, 1)
            pool.wait_ge(bias_zeroed, 1)
            pool.dma_start(bias[0:NE, 0:2 * D], b_gate_up[0]).then_inc(bias_landed, 16)
            pool.dma_start(bias[0:NE, 2 * D:3 * D], b_down[0]).then_inc(bias_landed, 16)
            pool.wait_ge(g_last_landed, 16)
            pool.wait_ge(g_post_landed, 16)
            pool.wait_ge(p_landed, 16 * 4)

        @block.tensor
        def _(pe):
            def begin(name):
                bank, turn = turns[name]
                if turn:
                    pe.wait_ge(emptied[bank], turn)
                return bank

            def turn_block(bank, col, src, rows, width=P):
                return pe.transpose(ps[0:width, bank, col:col + rows], src, ident[0:rows, 0:rows])

            def product(name, pairs, out, ready=None):
                b = begin(name)
                for k, (lhs, rhs) in enumerate(pairs):
                    if ready is not None:
                        pe.wait_ge(ready, k + 1)
                    mm = pe.matmul(out(b), lhs, rhs, start=(k == 0), stop=(k == len(pairs) - 1))
                mm.then_inc(filled[b], 1)

            def wait_piece(w, j):
                s, turn = piece_turn[(w, j)]
                pe.wait_ge(landed[s], 16 * (turn + 1))
                return s

            def channel_block(name, s, c, rhs):
                col = (c % 4) * P
                product(name, [(ring[:, s, k, col:col + P], rhs[:, k, :]) for k in range(KC)],
                        lambda b: ps[:, b, 0:NTOK])

            def column_products(kind, t, rows, weights):
                names = [("out", h, t) if kind == "out" else (kind, t, h) for h in range(2)]
                if t < TT - 1:
                    for name, w in zip(names, weights):
                        product(name, list(zip(rows, w)), lambda b: ps[0:ROWS[t], b, :],
                                merged_ready if name == ("out", 0, 0) else None)
                    return
                banks = [begin(name) for name in names]
                for k, row in enumerate(rows):
                    for name, w, b in zip(names, weights, banks):
                        mm = pe.matmul(ps[column_half(name), b, :], row, w[k], start=(k == 0),
                                       stop=(k == len(rows) - 1))
                        if k == len(rows) - 1:
                            mm.then_inc(filled[b], 1)

            pe.wait_ge(consts_set, 5)
            for i in range(2):
                pe.wait_ge(vec_landed[i], 16 * len(shares[i]))
            b = begin("vec")
            turn_block(b, 0, raw_vec[0:NVEC, :], NVEC).then_inc(filled[b], 1)
            pe.wait_ge(u_ready, TT)
            for c in range(KC):
                b = begin(("uT", c))
                for t in range(TT):
                    mm = turn_block(b, t * P, u_tok[0:ROWS[t], t, c * P:c * P + P], ROWS[t])
                mm.then_inc(filled[b], 1)

            def turn_histories():
                pe.wait_ge(hist_landed, 16 * 3)
                for i in range(3):
                    b = begin(("hist", i))
                    for c in range(3 * i, min(3 * i + 3, KC)):
                        turn_block(b, (c % 3) * HIST, raw_hist[:, c * P:c * P + P], P)
                        mm = turn_block(b, (c % 3) * HIST + P, raw_conv[0:24, c * P:c * P + P], 24)
                    mm.then_inc(filled[b], 1)

            wait_read(pe, ("uT", KC - 2))
            wait_read(pe, ("uT", KC - 1))
            seen = set()
            for n, c in enumerate(z_order()):
                s, _ = piece_turn[("in", c // 4)]
                if c // 4 not in seen:
                    wait_piece("in", c // 4)
                    seen.add(c // 4)
                channel_block(("z", c), s, c, uT)
                if n == 0:
                    turn_histories()
                if n % 4 == 3 and n < 16:
                    p = n // 4
                    if p == 0:
                        pe.wait_ge(gates_landed, 16 * GATE_LOADS)
                    pe.wait_ge(xc_ready, p + 1)
                    for i in range(4):
                        w = gate_a if i < 2 else gate_x
                        product(("gate", p, i), [(w[:, 2 * p + i % 2, :], xc[:, i % 2, :])],
                                lambda b: ps[:, b, 0:XC_W])
                if n % 4 == 1 and 4 < n < 20:
                    g = n // 4 - 1
                    if g == 0:
                        pe.wait_ge(small_landed, 16 * SMALL_LOADS)
                    pe.wait_ge(mixed_ready, g + 1)
                    for e in range(2):
                        product(("pool", g, e),
                                [(poolw[:, g, k, e * P:e * P + P], mixed[:, k, :]) for k in range(2)],
                                lambda b: ps[:, b, 0:NTOK])
            pe.wait_ge(ya_ready, PG)
            def turn_state(i, src):
                for h in range(2):
                    b = begin(("state", i, h))
                    for c in range(4):
                        mm = turn_block(b, c * P, src[:, 4 * h + c, :], P, TAIL)
                    mm.then_inc(filled[b], 1)

            turn_state(0, tail_a)
            turn_state(1, tail_b)
            wait_read(pe, ("pool", PG - 1, 0))
            wait_read(pe, ("pool", PG - 1, 1))
            for c in range(KC):
                s = wait_piece("b", c // 4)
                channel_block(("b", c), s, c, yb)
            turn_state(2, ya[:, :, NTOK - TAIL:NTOK])
            pe.wait_ge(p_landed, 16 * 4)
            for t in range(TT):
                b = begin(("pT", t))
                for k in range(2):
                    mm = turn_block(b, k * P, p_tok[0:ROWS[t], t, k * P:k * P + P], ROWS[t])
                mm.then_inc(filled[b], 1)
            for c in range(KC):
                s = wait_piece("a", c // 4)
                channel_block(("a", c), s, c, ya)
            slots = [wait_piece("out", half) for half in range(2)]

            def turn_residual(t):
                for h in range(2):
                    wait_read(pe, ("out", h, t))
                for h in range(2):
                    b = begin(("xT", t, h))
                    for c in range(4):
                        mm = turn_block(b, c * P, x_tok[0:ROWS[t], t, (4 * h + c) * P:(4 * h + c) * P + P], ROWS[t])
                    mm.then_inc(filled[b], 1)

            def router_logits(t):
                for h in range(2):
                    wait_read(pe, ("xT", t, h))
                M = min(ROWS[t], 64)
                for r in range(0, ROWS[t], M):
                    for k in range(KC):
                        mm = pe.matmul(ps[r:r + M, b, t * NE:t * NE + NE], uT[:, k, t * P + r:t * P + r + M],
                                       wrouter[:, k, :], start=(k == 0), stop=(k == KC - 1))
                return mm

            for t in range(TT):
                column_products("out", t, [ga[:, k, tok(t)] for k in range(KC)],
                                [[ring[:, slots[half], k, :] for k in range(KC)] for half in range(2)])
                if t:
                    turn_residual(t - 1)
            b = begin("logits")
            router_logits(0)
            turn_residual(TT - 1)
            for t in range(1, TT):
                mm = router_logits(t)
            mm.then_inc(filled[b], 1)
            for t in range(TT):
                wait_read(pe, ("pT", t))

            def embed(t, halves):
                if t == TT - 1:
                    column_products("ple", t, [pT[:, k, tok(t)] for k in range(2)],
                                    [[wple[:, k, 512 * h:512 * h + 512] for k in range(2)] for h in range(2)])
                    return
                for h in halves:
                    product(("ple", t, h), [(pT[:, k, tok(t)], wple[:, k, 512 * h:512 * h + 512]) for k in range(2)],
                            lambda b: ps[0:ROWS[t], b, :])

            embed(0, [0, 1])
            pe.wait_ge(member_ready, 1)
            b = begin("rank")
            for t in range(TT):
                for q in range(t + 1):
                    mm = pe.matmul(ps[:, b, t * NE:t * NE + NE], (before if q == t else ones)[:], member[:, q, :],
                                   start=(q == 0), stop=(q == t))
            for t in range(TT):
                mm = pe.matmul(ps[:, b, TT * NE:TT * NE + NE], ones[:], member[:, t, :],
                               start=(t == 0), stop=(t == TT - 1))
            mm.then_inc(filled[b], 1)

            def half(g):
                return slice(g * CAP, g * CAP + CAP)

            def gather(n):
                pe.wait_ge(sel_ready, n + 1)
                b = begin_chunk(pe, "x", n)
                for t in range(TT):
                    for g in range(2):
                        mm = pe.matmul(ps[half(g), b, :], sel[:, t, :], x_tok[:, t, 512 * g:512 * g + 512],
                                       start=(t == 0), stop=(t == TT - 1))
                mm.then_inc(filled[b], 1)

            def turn_rows(kind, n, src):
                b = begin_chunk(pe, kind, n)
                for j in range(4):
                    mm = pe.transpose(ps[:, b, j * P:j * P + P], src[:, j * P:j * P + P], ident[:])
                mm.then_inc(filled[b], 1)

            def begin_sums(kind, n, pick, at):
                b = begin_chunk(pe, kind, n)
                for g in range(2):
                    pe.matmul(ps[half(g), b, :], pick, bias[:, at + 512 * g:at + 512 * g + 512],
                              start=True, stop=False)

            def weigh(kind, q, n, rows):
                b = CHUNK_BANK[kind]
                for k in range(KC):
                    if k % 2 == 0:
                        pe.wait_ge(quarter_landed[q + k // 2], n * 16 + 16)
                    for g in range(2):
                        mm = pe.matmul(ps[half(g), b, :], rows[:, k, :],
                                       quarter(q + k // 2)[:, k % 2, 512 * g:512 * g + 512],
                                       start=False, stop=(k == KC - 1))
                    if k % 2 == 1 and k < KC - 1:
                        mm.then_inc(quarter_used_up[q // 4][k // 2], 1)
                mm.then_inc(filled[b], 1)

            embed(2, [0, 1])
            embed(1, [0])
            gather(0)
            embed(1, [1])
            chunk_read(pe, "x", 0)
            turn_rows("xT", 0, x_rows)
            pe.wait_ge(bias_landed, 16 * 2)
            pe.wait_ge(passes_ready, 1)
            passes = pe.value_load(passes_i[0:1, 0:1], min_val=1, max_val=PASSES)
            with pe.Fori(0, passes) as c:
                with pe.Fori(0, PAIRS) as e2:
                    m = c * PAIRS + e2
                    for i in range(2):
                        n = m * 2 + i
                        pe.wait_ge(pick_gu_ready, n + 1)
                        begin_sums("gate", n, pick_gu, 0)
                        chunk_read(pe, "xT", n)
                        weigh("gate", 0, n, xg)
                        begin_sums("up", n, pick_gu, D)
                        weigh("up", 4, n, xg)
                        gather(n + 1)
                        pe.wait_ge(hidden_ready, n + 1)
                        turn_rows("hT", n, up)
                        chunk_read(pe, "x", n + 1)
                        turn_rows("xT", n + 1, x_rows)
                        if i == 1:
                            pe.wait_ge(sel_w_ready, m + 1)
                            pe.wait_ge(emptied[B_S], m + bank_uses[B_S])
                            for t in range(TT):
                                mm = pe.transpose(ps[:, B_S, t * P:t * P + P], sel_w[:, t, :], ident[:])
                            mm.then_inc(filled[B_S], 1)
                        pe.wait_ge(pick_d_ready, n + 1)
                        begin_sums("out", n, pick_d[:], 2 * D)
                        chunk_read(pe, "hT", n)
                        weigh("out", 8, n, hT)
                    pe.wait_ge(emptied[B_S], m + (bank_uses[B_S] + 1))
                    chunk_read(pe, "out", n)
                    for i in range(2 * TT):
                        bank, turn = pair_bank(i)
                        pe.wait_ge(emptied[bank], m * 2 + (bank_uses[bank] + turn))
                        pe.matmul(ps[:, bank, :], sel_wT[:, i // 2, :], o_pair[:, 512 * (i % 2):512 * (i % 2) + 512],
                                  start=True, stop=True).then_inc(filled[bank], 1)

            def begin_tail(name):
                bank, turn = tail_turns[name]
                if turn:
                    pe.wait_ge(t_emptied[bank], turn)
                return bank

            for bank in B_Y:
                pe.wait_ge(emptied[bank], passes * NE + bank_uses[bank])
            for t in range(TT):
                for h in range(2):
                    b = begin_tail(("x2T", t, h))
                    for c in range(4):
                        mm = turn_block(b, c * P, x2[0:ROWS[t], t, (4 * h + c) * P:(4 * h + c) * P + P], ROWS[t])
                    mm.then_inc(t_filled[b], 1)
            pe.wait_ge(t_landed, 16 * 4)

            def gate_rows(k, h):
                return quarter(k // 2)[:, k % 2, 512 * h:512 * h + 512]

            for t in range(TT):
                for h in range(2):
                    wait_tail_read(pe, ("x2T", t, h))
                if t < TT - 1:
                    for h in range(2):
                        b = begin_tail(("pg", t, h))
                        for k in range(KC):
                            mm = pe.matmul(ps[0:ROWS[t], b, :], x2T[:, k, tok(t)], gate_rows(k, h),
                                           start=(k == 0), stop=(k == KC - 1))
                        mm.then_inc(t_filled[b], 1)
                    continue
                banks = [begin_tail(("pg", t, h)) for h in range(2)]
                for k in range(KC):
                    for h, b in enumerate(banks):
                        mm = pe.matmul(ps[column_half(("pg", t, h)), b, :], x2T[:, k, tok(t)],
                                       gate_rows(k, h), start=(k == 0), stop=(k == KC - 1))
                        if k == KC - 1:
                            mm.then_inc(t_filled[b], 1)

        @block.scalar
        def _(act):
            step = Chain(act, act_step)

            load_vectors(act, 0)

            def square_sums(g, t, src, scratch):
                nc.scalar.activation(scratch[0:ROWS[t], :], src, ACT.Square,
                                     accum_out=stat[0:ROWS[t], g, 0, t:t + 1]).then_inc(squares[g], 1)

            act.wait_ge(stat_set, 1)
            for t in range(TT):
                act.wait_ge(x_landed[t], 16)
                if t:
                    act.wait_ge(squares[0], t)
                square_sums(0, t, x_tok[0:ROWS[t], t, :], work[:, 0, 0:D])
            act.wait_ge(means[0], 1)
            nc.scalar.activation(stat[:, 0, 2, :], stat[:, 0, 1, :], ACT.Sqrt).then_inc(roots[0], 1)
            act.wait_ge(lam_abs, 1)
            nc.scalar.activation(lam[:, 2, :], lam[:, 1, :], ACT.Exp, scale=-1.0).then_inc(lam_exp, 1)

            def z_block(name, buf, pad, hist, tail_buf):
                b = wait_filled(act, name)
                main, samples = prompt_samples(buf, pad)
                nc.scalar.copy(main, ps[:, b, 0:SEQ])
                nc.scalar.copy(samples[:, :, pad:], ps[:, b, SEQ:NTOK].rearrange("p (b t) -> p b t", b=DB))
                nc.scalar.copy(samples[:, :, 0:pad], hist.rearrange("p (b t) -> p b t", b=DB))
                nc.scalar.copy(tail_buf, ps[:, b, NTOK - TAIL:NTOK]).then_inc(emptied[b], 1)

            def z_lru(p, i):
                c = 2 * p + i
                z_block(("z", c), xa[:, p % 2, i * XA_W:(i + 1) * XA_W], CONV - 1, hist_conv[:, c, :],
                        tail_a[:, c, :])

            def z_pool(p, i):
                c = 2 * p + i
                act.wait_ge(mixed_ready, p) if p else act.wait_ge(pads_set, 1)
                z_block(("z", 8 + c), xb[:, i, :], PB, hist_pool[:, c, :], tail_b[:, c, :])

            def lru_gates(p):
                if p:
                    act.wait_ge(h_scanned, p)
                for i in range(4):
                    b = wait_filled(act, ("gate", p, i))
                    c = 2 * p + i % 2
                    dst, bias = (r_, V_BRA) if i < 2 else (i_, V_BRX)
                    nc.scalar.activation(dst[:, i % 2, :], ps[:, b, 0:XC_W], ACT.Sigmoid,
                                         bias=vec[:, bias + c:bias + c + 1]).then_inc(emptied[b], 1)
                if p == 0:
                    act.wait_ge(lam_set, 1)
                for i in range(2):
                    wait_read(act, ("gate", p, i))
                    nc.scalar.activation(a_[:, i, :], r_[:, i, :], ACT.Exp,
                                         scale=lam[:, 6, 2 * p + i:2 * p + i + 1])
                for i in range(2):
                    last = nc.scalar.activation(r_[:, i, :], r_[:, i, :], ACT.Tanh,
                                                scale=lam[:, 7, 2 * p + i:2 * p + i + 1])
                last.then_inc(decay_ready, 1)

            def lru_mult(p):
                act.wait_ge(square_ready, p + 1)
                nc.scalar.activation(r_.rearrange("p c w -> p (c w)"), xa[:, p % 2, 0:2 * XC_W], ACT.Sqrt) \
                    .then_inc(mult_ready, 1)

            def lru_out(p):
                act.wait_ge(h_scanned, p + 1)
                for i in range(2):
                    nc.scalar.copy(ya[:, 2 * p + i, 0:SEQ], xc[:, i, 0:SEQ])
                    last = nc.scalar.copy(ya[:, 2 * p + i, SEQ:NTOK].rearrange("p (b t) -> p b t", b=DB),
                                          xc[:, i, SEQ:XC_W].rearrange("p (b w) -> p b w", b=DB)[:, :, CONV - 1:])
                last.then_inc(ya_ready, 1)

            def pool_out(g):
                for e in range(2):
                    b = wait_filled(act, ("pool", g, e))
                    c = 2 * g + e
                    nc.scalar.activation(yb[:, c, :], ps[:, b, 0:NTOK], ACT.Identity,
                                         scale=vec[:, V_PS + c:V_PS + c + 1]).then_inc(emptied[b], 1)

            def z_gate(c):
                b = wait_filled(act, ("z", c))
                dst = ga[:, c - 16, :] if c < 24 else gb[:, c - 24, :]
                nc.scalar.activation(dst, ps[:, b, 0:NTOK], ACT.Sigmoid).then_inc(emptied[b], 1)

            for i in range(3):
                wait_read(act, ("hist", i))
            for p in range(4):
                z_lru(p, 0)
                if p:
                    lru_mult(p - 1)
                z_lru(p, 1)
                if p:
                    pool_out(p - 1)
                    lru_out(p - 1)
                z_pool(p, 0)
                z_pool(p, 1)
                lru_gates(p)
            z_gate(16)
            lru_mult(3)
            z_gate(17)
            pool_out(3)
            lru_out(3)
            for c in range(18, 32):
                z_gate(c)

            for i in range(3):
                for h in range(2):
                    b = wait_filled(act, ("state", i, h))
                    dst = state_h[0:TAIL, 512 * h:512 * h + 512] if i == 2 else \
                        state_z[0:TAIL, i, 512 * h:512 * h + 512]
                    nc.scalar.copy(dst, ps[0:TAIL, b, :]).then_inc(emptied[b], 1)

            for t in range(TT):
                b = wait_filled(act, ("pT", t))
                both = ps[:, b, 0:2 * P].rearrange("p (k t) -> p k t", k=2)
                nc.scalar.copy(pT[:, :, tok(t)], both[:, :, 0:ROWS[t]]).then_inc(emptied[b], 1)

            for t in range(TT):
                for half in range(2):
                    wait_read(act, ("out", half, t))
                square_sums(1, t, x_tok[0:ROWS[t], t, :], u_tok[:, t, :])
                act.wait_ge(means[1], t + 1)
                nc.scalar.activation(stat[0:ROWS[t], 1, 2, t:t + 1], stat[0:ROWS[t], 1, 1, t:t + 1], ACT.Sqrt) \
                    .then_inc(roots[1], 1)
            for t in range(TT):
                act.wait_ge(top_ready, t + 1)
                nc.scalar.activation(wts[0:ROWS[t], t, 0:TOPK], top[0:ROWS[t], t, 0:TOPK], ACT.Exp,
                                     bias=wts[0:ROWS[t], t, 6:7],
                                     accum_out=wts[0:ROWS[t], t, 4:5]).then_inc(wts_raw, 1)

            def embedded(t, h):
                b = wait_filled(act, ("ple", t, h))
                nc.scalar.copy(ple[0:ROWS[t], t, 512 * h:512 * h + 512], ps[column_half(("ple", t, h)), b, :]) \
                    .then_inc(emptied[b], 1)

            for t, h in ((0, 0), (0, 1), (2, 0), (2, 1), (1, 0)):
                embedded(t, h)

            def copy_inputs(n):
                b = chunk_filled(act, "x", n)
                nc.scalar.copy(x_rows, ps[:, b, :]).then_inc(emptied[b], 1)

            copy_inputs(0)
            embedded(1, 1)
            for t in range(TT):
                for h in range(2):
                    wait_read(act, ("ple", t, h))
                if t:
                    act.wait_ge(squares[2], t)
                square_sums(2, t, ple[0:ROWS[t], t, :], square_row)
            act.wait_ge(means[2], 1)
            nc.scalar.activation(stat[:, 2, 2, :], stat[:, 2, 1, :], ACT.Sqrt).then_inc(roots[2], 1)

            act.wait_ge(squares[1], TT)
            for t in range(TT):
                nc.scalar.copy(x2[0:ROWS[t], t, :], x_tok[0:ROWS[t], t, :]).then_inc(x1_copied, 1)
            act.wait_ge(passes_ready, 1)
            passes = act.value_load(passes_i[0:1, 0:1], min_val=1, max_val=PASSES)
            with act.Fori(0, passes) as c:
                with act.Fori(0, PAIRS) as e2:
                    m = c * PAIRS + e2
                    for i in range(2):
                        n = m * 2 + i
                        chunk_read(act, "gate", n)
                        nc.scalar.activation(sg, gate, ACT.Sigmoid, scale=ALPHA).then_inc(sig_ready, 1)
                        copy_inputs(n + 1)
                        if i == 1:
                            act.wait_ge(filled[B_S], m + (bank_uses[B_S] + 1))
                            nc.scalar.copy(sel_wT.rearrange("p t s -> p (t s)"), ps[:, B_S, 0:TT * P]) \
                                .then_inc(emptied[B_S], 1)
                        b = chunk_filled(act, "out", n)
                        rows = o_pair[CAP * i:CAP * i + CAP, :]
                        nc.scalar.copy(rows[:, 0:512], ps[0:CAP, b, :])
                        nc.scalar.copy(rows[:, 512:1024], ps[CAP:2 * CAP, b, :]).then_inc(emptied[b], 1)

            for t in range(TT):
                for i in range(2 * TT):
                    if i // 2 == t:
                        bank, turn = pair_bank(i)
                        act.wait_ge(emptied[bank], passes * NE + (bank_uses[bank] + turn - 1))
                if t:
                    act.wait_ge(squares[3], t)
                square_sums(3, t, x2[0:ROWS[t], t, :], square_tail)
            act.wait_ge(means[3], 1)
            nc.scalar.activation(stat[:, 3, 2, :], stat[:, 3, 1, :], ACT.Sqrt).then_inc(roots[3], 1)
            act.wait_ge(x2_squared, 1)
            for t in range(TT):
                R = ROWS[t]
                if t:
                    act.wait_ge(x3_ready, t)
                for half in range(2):
                    b = wait_tail_filled(act, ("pg", t, half))
                    nc.scalar.activation(sig[0:R, half, :], ps[column_half(("pg", t, half)), b, :], ACT.Sigmoid,
                                         scale=stat[0:R, 3, 3, t:t + 1]).then_inc(t_emptied[b], 1)
                nc.scalar.activation(root_spare[0:R, t:t + 1], stat[0:R, 3, 3, t:t + 1], ACT.Sqrt)
                act.wait_ge(x3_ready, t + 1)
                square_sums(4, t, x2[0:R, t, :], square_tail)
                act.wait_ge(means[4], t + 1)
                nc.scalar.activation(stat[0:R, 4, 2, t:t + 1], stat[0:R, 4, 1, t:t + 1], ACT.Sqrt) \
                    .then_inc(roots[4], 1)
                if t < TT - 1:
                    nc.scalar.activation(sig_spare[0:R, t:t + 1], stat[0:R, 3, 3, t:t + 1], ACT.Sigmoid)

        @block.vector
        def _(dve):
            step = Chain(dve, dve_step)
            V = nc.vector

            V.memset(stat[:], 1.0).then_inc(stat_set, 1)
            V.memset(gate_a[:], 0.0).then_inc(gates_zeroed, 1)
            V.memset(gate_x[:], 0.0).then_inc(gates_zeroed, 1)
            V.memset(topf[:], -1.0)
            V.memset(wts[:], 1.0)
            for k in range(PB):
                V.memset(inv_count[:, k:k + 1], 1.0 / (k + 1))
            step.link(V.memset(xa[:].rearrange("p b (c w) -> p (b c) w", c=2)[:, :, 0:CONV - 1], 0.0))

            def mean(g, rows, cols):
                V.tensor_scalar(stat[0:rows, g, 1, cols], stat[0:rows, g, 0, cols], 1.0 / D, EPS,
                                ALU.mult, ALU.add).then_inc(means[g], 1)

            dve.wait_ge(squares[0], TT)
            mean(0, P, slice(0, TT))
            dve.wait_ge(roots[0], 1)
            step.link(V.reciprocal(stat[:, 0, 3, :], stat[:, 0, 2, :]))
            for t in range(TT):
                V.tensor_scalar(u_tok[0:ROWS[t], t, :], x_tok[0:ROWS[t], t, :], stat[0:ROWS[t], 0, 3, t:t + 1], None,
                                ALU.mult).then_inc(u_ready, 1)
            dve.wait_ge(u_ready, TT)
            V.memset(xb[:, :, 0:PB], 0.0).then_inc(pads_set, 1)

            b = wait_filled(dve, "vec")
            V.tensor_copy(vec[:], ps[:, b, 0:NVEC]).then_inc(emptied[b], 1)
            wait_read(dve, "vec")
            for c in range(KC):
                b = wait_filled(dve, ("uT", c))
                V.tensor_scalar(uT[:, c, :], ps[:, b, 0:NTOK], vec[:, V_GMIX + c:V_GMIX + c + 1], None,
                                ALU.mult).then_inc(emptied[b], 1)
            V.tensor_copy(expert_col[:, 0:NE], ident[:, 0:NE])
            V.tensor_copy(expert_col[:, NE:NE + 1], ident[:, 0:1])
            for c in range(3):
                b = wait_filled(dve, ("hist", c))
                V.tensor_copy(hist[:, 3 * c:min(3 * c + 3, KC), :],
                              ps[:, b, 0:(min(3 * c + 3, KC) - 3 * c) * HIST].rearrange("p (c w) -> p c w", w=HIST)) \
                    .then_inc(emptied[b], 1)

            lm = vec[:, V_LAM:V_LAM + KC]
            L = [lam[:, k, :] for k in range(12)]
            step.link(V.tensor_scalar(L[0], lm, -1.0, None, ALU.mult))
            V.tensor_tensor(L[1], lm, L[0], ALU.max).then_inc(lam_abs, 1)
            step.link(V.tensor_scalar(L[3], L[0], 0.0, None, ALU.max))
            dve.wait_ge(lam_exp, 1)
            step.link(V.tensor_scalar(L[4], L[2], 2.0, None, ALU.add))
            step.link(V.reciprocal(L[5], L[4]))
            step.link(V.tensor_tensor(L[8], L[2], L[5], ALU.mult))
            step.link(V.tensor_tensor(L[9], L[8], L[8], ALU.mult))
            step.link(V.tensor_scalar(L[10], L[9], 1.0 / 17, None, ALU.mult))
            for m in range(15, 1, -2):
                step.link(V.scalar_tensor_tensor(out=L[10], in0=L[10], scalar=1.0 / m, in1=L[9], op0=ALU.add,
                                                 op1=ALU.mult))
            step.link(V.scalar_tensor_tensor(out=L[11], in0=L[10], scalar=1.0, in1=L[8], op0=ALU.add, op1=ALU.mult))
            step.link(V.scalar_tensor_tensor(out=L[11], in0=L[11], scalar=2.0, in1=L[3], op0=ALU.mult, op1=ALU.add))
            V.tensor_scalar(L[6], L[11], -8.0, None, ALU.mult)
            V.tensor_scalar(L[7], L[11], 8.0, None, ALU.mult).then_inc(lam_set, 1)

            def conv(p):
                for i in range(2):
                    wait_read(dve, ("z", 2 * p + i))
                if p:
                    dve.wait_ge(ya_ready, p)
                before_ = [0, 0]
                for k in range(CONV):
                    for i in range(2):
                        c = 2 * p + i
                        src = xa[:, p % 2, i * XA_W + k:i * XA_W + k + XC_W]
                        w = vec[:, V_CW + k * KC + c:V_CW + k * KC + c + 1]
                        if k == 0:
                            ins = V.tensor_scalar(xc[:, i, :], src, w, vec[:, V_CB + c:V_CB + c + 1],
                                                  ALU.mult, ALU.add)
                        else:
                            step.need(before_[i])
                            ins = V.scalar_tensor_tensor(out=xc[:, i, :], in0=src, scalar=w, in1=xc[:, i, :],
                                                         op0=ALU.mult, op1=ALU.add)
                        if k == CONV - 1 and i == 1:
                            ins.then_inc(xc_ready, 1)
                        else:
                            before_[i] = step(ins)

            def pooling(g):
                for i in range(2):
                    wait_read(dve, ("z", 8 + 2 * g + i))
                src, dst, spare = xb, s1, s2
                for lev in range(g + 1):
                    sh = 1 << lev
                    lo = 2 * sh - 1
                    step.link(V.tensor_tensor(dst[:, :, lo:], src[:, :, lo:], src[:, :, lo - sh:XB_W - sh], ALU.add))
                    src, dst, spare = dst, (spare if lev == 0 else src), None
                w = WIN[g]
                head = src[:, :, PB:PB + w - 1]
                step.link(V.scalar_tensor_tensor(out=head, in0=head, scalar=float(w),
                                                 in1=inv_count[:, 0:w - 1].unsqueeze(1).to_broadcast([P, 2, w - 1]),
                                                 op0=ALU.mult, op1=ALU.mult))
                if g:
                    wait_filled(dve, ("pool", g - 1, 1))
                V.scalar_tensor_tensor(out=mixed[:, :, 0:SEQ], in0=src[:, :, PB:PB + SEQ], scalar=1.0 / w,
                                       in1=xb[:, :, PB:PB + SEQ], op0=ALU.mult, op1=ALU.subtract)
                for i in range(2):
                    own = [prompt_samples(t[:, i, :], PB)[1][:, :, PB:] for t in (src, xb)]
                    last = V.scalar_tensor_tensor(out=mixed[:, i, SEQ:].rearrange("p (b t) -> p b t", b=DB),
                                                  in0=own[0], scalar=1.0 / w, in1=own[1],
                                                  op0=ALU.mult, op1=ALU.subtract)
                last.then_inc(mixed_ready, 1)

            def lru(p):
                dve.wait_ge(decay_ready, p + 1)
                sq = xa[:, p % 2, 0:2 * XC_W]
                flat = [t.rearrange("p c w -> p (c w)") for t in (a_, r_, i_, xc)]
                step.link(V.tensor_tensor(sq, flat[0], flat[0], ALU.mult))
                V.scalar_tensor_tensor(out=sq, in0=sq, scalar=1.0, in1=flat[1], op0=ALU.add, op1=ALU.mult) \
                    .then_inc(square_ready, 1)
                for i in range(2):
                    wait_read(dve, ("gate", p, 2 + i))
                step(V.tensor_tensor(flat[2], flat[2], flat[3], ALU.mult))
                step(V.memset(a_[:, :, SEQ:].rearrange("p c (b w) -> p c b w", b=DB)[:, :, :, CONV - 2:CONV - 1], 0.0))
                dve.wait_ge(mult_ready, p + 1)
                step(V.memset(xa[:, p % 2, :].rearrange("p (c w) -> p c w", c=2)[:, :, 0:CONV - 1], 0.0))
                step.link(V.memset(r_[:, :, 0:1], 1.0))
                step.link(V.tensor_tensor(flat[2], flat[2], flat[1], ALU.mult))
                step.link(V.tensor_copy(i_[:, :, SEQ:].rearrange("p c (b w) -> p c b w", b=DB)[:, :, :, CONV - 2],
                                        hist_h[:, 2 * p:2 * p + 2, :]))
                for i in range(2):
                    last = V.tensor_tensor_scan(out=xc[:, i, :], data0=a_[:, i, :], data1=i_[:, i, :], initial=0.0,
                                                op0=ALU.mult, op1=ALU.add)
                last.then_inc(h_scanned, 1)

            for p in range(4):
                conv(p)
                pooling(p)
                lru(p)

            dve.wait_ge(mixed_ready, PG)
            V.memset(x_tok[:, TT - 1, :], 0.0).then_inc(x_cleared, 1)

            for c in range(KC):
                b = wait_filled(dve, ("b", c))
                wait_read(dve, ("z", 24 + c))
                V.tensor_tensor(gb[:, c, :], gb[:, c, :], ps[:, b, 0:NTOK], ALU.mult).then_inc(emptied[b], 1)
            for c in range(KC):
                b = wait_filled(dve, ("a", c))
                wait_read(dve, ("z", 16 + c))
                V.tensor_tensor(ga[:, c, :], ga[:, c, :], ps[:, b, 0:NTOK], ALU.mult).then_inc(emptied[b], 1)
                wait_read(dve, ("a", c))
                V.tensor_tensor(ga[:, c, :], ga[:, c, :], gb[:, c, :], ALU.add).then_inc(merged_ready, 1)
            dve.wait_ge(x_back, 16 * TT)

            def turned(dst, bank, t, at):
                return V.tensor_tensor(dst, ps[:, bank, :].rearrange("p (c t) -> p c t", c=4)[:, :, 0:ROWS[t]],
                                       vec[:, at:at + 4].unsqueeze(2).to_broadcast([P, 4, ROWS[t]]), ALU.mult)

            def inverse_root(g, t):
                R = ROWS[t]
                dve.wait_ge(squares[g], t + 1)
                mean(g, R, slice(t, t + 1))
                dve.wait_ge(roots[g], t + 1)
                return V.reciprocal(stat[0:R, g, 3, t:t + 1], stat[0:R, g, 2, t:t + 1])

            def add_out(t):
                for half in range(2):
                    b = wait_filled(dve, ("out", half, t))
                    x_half = x_tok[0:ROWS[t], t, 512 * half:512 * half + 512]
                    V.tensor_tensor(x_half, x_half, ps[column_half(("out", half, t)), b, :], ALU.add) \
                        .then_inc(emptied[b], 1)

            def channels_of(t):
                for h in range(2):
                    b = wait_filled(dve, ("xT", t, h))
                    turned(uT[:, 4 * h:4 * h + 4, tok(t)], b, t, V_GMOE + 4 * h).then_inc(emptied[b], 1)

            add_out(0)
            add_out(1)
            dve.wait_ge(state_stored, 16 * (4 + 3 * DB))
            channels_of(0)
            step(inverse_root(1, 0))
            add_out(2)
            channels_of(1)
            step(inverse_root(1, 1))
            channels_of(2)
            step(inverse_root(1, 2))

            b = wait_filled(dve, "logits")
            step.need(step.n)
            for t in range(TT):
                R = ROWS[t]
                last = V.scalar_tensor_tensor(out=logits[0:R, t, :], in0=ps[0:R, b, t * NE:t * NE + NE],
                                              scalar=stat[0:R, 1, 3, t:t + 1], in1=brouter[0:R, :],
                                              op0=ALU.mult, op1=ALU.add)
            last.then_inc(emptied[b], 1)
            wait_read(dve, "logits")
            for t in range(TT):
                last = step(V.max(top[0:ROWS[t], t, :], logits[0:ROWS[t], t, :]))
            step.need(last)
            for t in range(TT):
                last = step(V.max_index(topi[0:ROWS[t], t, :], top[0:ROWS[t], t, :], logits[0:ROWS[t], t, :]))
            for t in range(TT):
                V.tensor_scalar(wts[0:ROWS[t], t, 6:7], top[0:ROWS[t], t, 0:1], -1.0, None, ALU.mult) \
                    .then_inc(top_ready, 1)
            step.need(last)
            for t in range(TT):
                last = step(V.tensor_copy(topf[0:ROWS[t], t, :], topi[0:ROWS[t], t, :]))
            step.need(last)
            step.link(V.tensor_tensor(onehot, iota_cap[:, 0:NE].unsqueeze(1).unsqueeze(1)
                                      .to_broadcast([P, TT, TOPK, NE]),
                                      topf[:, :, 0:TOPK].unsqueeze(3).to_broadcast([P, TT, TOPK, NE]), ALU.is_equal))
            step.link(V.tensor_reduce(chosen[:], onehot.rearrange("p t k e -> p t e k"), AX.X, ALU.add))
            V.tensor_copy(member[:], chosen[:]).then_inc(member_ready, 1)
            step.link(V.memset(slot[:, :, NCH:NCH + 1], -1.0))
            b = wait_filled(dve, "rank")
            dve.wait_ge(member_ready, 1)
            step.link(V.scalar_tensor_tensor(out=slot[:, :, 0:NE],
                                        in0=ps[:, b, 0:TT * NE].rearrange("p (t e) -> p t e", t=TT), scalar=1.0,
                                        in1=chosen[:], op0=ALU.add, op1=ALU.mult))
            step.link(V.tensor_scalar(slot[:, :, 0:NE], slot[:, :, 0:NE], -1.0, None, ALU.add))

            def select(n):
                for t in range(TT):
                    last = V.tensor_scalar(sel[:, t, :], iota_cap[:], slot[:, t, bass.ds(n, 1)]
                                           if not isinstance(n, int) else slot[:, t, n:n + 1],
                                           stat[:, 1, 3, t:t + 1], ALU.is_equal, ALU.mult)
                last.then_inc(sel_ready, 1)

            def pick_expert(dst, e):
                col = expert_col[:, bass.ds(e, 1)] if not isinstance(e, int) else expert_col[:, e:e + 1]
                return V.tensor_copy(dst, col.to_broadcast([P, CAP]))

            select(0)
            pick_expert(pick_gu, 0).then_inc(pick_gu_ready, 1)
            V.tensor_reduce(passes_f[0:1, 0:1], ps[0:1, b, TT * NE:TT * NE + NE], AX.X, ALU.max) \
                .then_inc(emptied[b], 1)
            wait_read(dve, "rank")
            for c in range(1, PASSES):
                step(V.tensor_scalar(slot[:, :, c * NE:c * NE + NE], slot[:, :, 0:NE], float(-CAP * c), None,
                                            ALU.add))
            step.link(V.tensor_scalar(below[0:1, :], iota_pass[0:1, :], passes_f[0:1, 0:1], None, ALU.is_lt))
            step.link(V.tensor_reduce(passes_f[0:1, 1:2], below[0:1, :], AX.X, ALU.add))
            V.tensor_copy(passes_i[0:1, 0:1], passes_f[0:1, 1:2]).then_inc(passes_ready, 1)
            dve.wait_ge(wts_raw, TT)
            step.link(V.reciprocal(wts[:, :, 5:6], wts[:, :, 4:5]))
            step.link(V.tensor_tensor(wts[:, :, 0:TOPK], wts[:, :, 0:TOPK], wts[:, :, 5:6].to_broadcast([P, TT, TOPK]),
                                      ALU.mult))
            step.link(V.tensor_tensor(weighted, onehot, wts[:, :, 0:TOPK].unsqueeze(3)
                                      .to_broadcast([P, TT, TOPK, NE]), ALU.mult))
            step.link(V.tensor_reduce(comb[:], weighted.rearrange("p t k e -> p t e k"), AX.X, ALU.add))

            xg_gain = vec[:, V_GMOE:V_GMOE + KC].unsqueeze(2).to_broadcast([P, KC, CAP])

            def by_channel(bank):
                return ps[:, bank, :].rearrange("p (j g s) -> p g j s", j=4, g=2)

            def in_halves(buf):
                return buf.rearrange("p (g j) s -> p g j s", g=2)

            def gathered(n):
                b = chunk_filled(dve, "xT", n)
                V.tensor_tensor(in_halves(xg), by_channel(b), in_halves(xg_gain), ALU.mult).then_inc(emptied[b], 1)

            gathered(0)
            dve.wait_ge(g_post_landed, 16)
            dve.wait_ge(squares[2], TT)
            mean(2, P, slice(0, TT))
            dve.wait_ge(roots[2], 1)
            step.link(V.reciprocal(stat[:, 2, 3, :], stat[:, 2, 2, :]))
            for t in range(TT):
                R = ROWS[t]
                last = step(V.scalar_tensor_tensor(out=ple[0:R, t, :], in0=ple[0:R, t, :],
                                                   scalar=stat[0:R, 2, 3, t:t + 1], in1=g_post[0:R, :],
                                                   op0=ALU.mult, op1=ALU.mult))
            step.need(last)
            dve.wait_ge(x1_copied, TT)

            dve.wait_ge(passes_ready, 1)
            passes = dve.value_load(passes_i[0:1, 0:1], min_val=1, max_val=PASSES)
            with dve.Fori(0, passes) as c:
                with dve.Fori(0, PAIRS) as e2:
                    m = c * PAIRS + e2
                    for i in range(2):
                        n, e = m * 2 + i, e2 * 2 + i
                        bank, turn = chunk_turn("out", n)
                        dve.wait_ge(filled[bank], turn + (bank_uses[bank] - 1))
                        select(n + 1)
                        pick_expert(pick_d[:], e).then_inc(pick_d_ready, 1)
                        if i == 0:
                            for q in range(2):
                                for t in range(TT):
                                    last = V.tensor_scalar(sel_w[:, t, CAP * q:CAP * q + CAP], iota_cap[:],
                                                           slot[:, t, bass.ds(m * 2 + q, 1)],
                                                           comb[:, t, bass.ds(e2 * 2 + q, 1)],
                                                           ALU.is_equal, ALU.mult)
                            last.then_inc(sel_w_ready, 1)
                        b = chunk_filled(dve, "gate", n)
                        V.tensor_scalar(gate, ps[:, b, :], LIMIT, None, ALU.min).then_inc(emptied[b], 1)
                        dve.wait_ge(sig_ready, n + 1)
                        V.tensor_tensor(gate, gate, sg, ALU.mult).then_inc(swish_ready, 1)
                        b = chunk_filled(dve, "up", n)
                        V.tensor_scalar(up, ps[:, b, :], LIMIT, -LIMIT, ALU.min, ALU.max).then_inc(emptied[b], 1)
                        dve.wait_ge(swish_ready, n + 1)
                        chunk_read(dve, "up", n)
                        V.scalar_tensor_tensor(out=up, in0=up, scalar=1.0, in1=gate, op0=ALU.add, op1=ALU.mult) \
                            .then_inc(hidden_ready, 1)
                        pick_expert(pick_gu, e + 1).then_inc(pick_gu_ready, 1)
                        b = chunk_filled(dve, "hT", n)
                        V.tensor_copy(in_halves(hT), by_channel(b)).then_inc(emptied[b], 1)
                        gathered(n + 1)
                    for i in range(2 * TT):
                        bank, turn = pair_bank(i)
                        dve.wait_ge(filled[bank], m * 2 + (bank_uses[bank] + turn + 1))
                        t, at = i // 2, 512 * (i % 2)
                        x_half = x2[0:ROWS[t], t, at:at + 512]
                        V.tensor_tensor(x_half, x_half, ps[0:ROWS[t], bank, :], ALU.add).then_inc(emptied[bank], 1)

            for t in range(TT):
                for h in range(2):
                    b = wait_tail_filled(dve, ("x2T", t, h))
                    turned(x2T[:, 4 * h:4 * h + 4, tok(t)], b, t, V_GPLE + 4 * h).then_inc(t_emptied[b], 1)
            dve.wait_ge(squares[3], TT)
            mean(3, P, slice(0, TT))
            dve.wait_ge(roots[3], 1)
            V.reciprocal(stat[:, 3, 3, :], stat[:, 3, 2, :]).then_inc(x2_squared, 1)
            dve.wait_ge(g_last_landed, 16)
            for t in range(TT):
                R = ROWS[t]
                for h in range(2):
                    wait_tail_read(dve, ("pg", t, h))
                    s = sig[0:R, h, :]
                    x_half = x2[0:R, t, 512 * h:512 * h + 512]
                    step.link(V.tensor_tensor(s, s, ple[0:R, t, 512 * h:512 * h + 512], ALU.mult))
                    ins = V.tensor_tensor(x_half, x_half, s, ALU.add)
                    if h == 0:
                        step(ins)
                ins.then_inc(x3_ready, 1)
                step.link(inverse_root(4, t))
                V.scalar_tensor_tensor(out=y_tok[0:R, t, :], in0=x2[0:R, t, :], scalar=stat[0:R, 4, 3, t:t + 1],
                                       in1=g_last[0:R, :], op0=ALU.mult, op1=ALU.mult).then_inc(y_ready, 1)


_INS = ["x_prompt", "x_sample", "p_prompt", "p_sample", "state_lru_h", "state_conv", "state_pool", "g_mix", "w_in",
        "conv_w", "conv_b", "w_rg_a", "b_rg_a", "w_rg_x", "b_rg_x", "lru_lambda", "pool_w", "pool_scale",
        "w_proj_a", "w_proj_b", "w_out", "g_moe", "w_router", "b_router", "w_gate_up", "b_gate_up", "w_down",
        "b_down", "g_ple", "w_ple_gate", "w_ple", "g_ple_post", "g_final"]
_OUTS = [(1, SEQ, D), (DB, DS, D), (1, 1, D), (1, 1, CONV - 1, D), (1, 1, PB, D),
         (1, DB, D), (1, DB, CONV - 1, D), (1, DB, PB, D)]


def kernel(**inputs):
    import numpy as _np
    import concourse.bacc as _bacc
    from concourse import mybir as _mybir
    from concourse.bass_utils import run_bass_kernel_spmd as _run

    nc = _bacc.Bacc("TRN2", target_bir_lowering=False, num_devices=1)
    arrays, args = {}, []
    for name in _INS:
        a = _np.ascontiguousarray(inputs[name])
        arrays[f"in_{name}"] = a
        args.append(nc.dram_tensor(f"in_{name}", a.shape, _mybir.dt.from_np(a.dtype), kind="ExternalInput").ap())
    for i, shape in enumerate(_OUTS):
        args.append(nc.dram_tensor(f"out_{i}", shape, F32, kind="ExternalOutput").ap())
    hybrid_layer(nc, *args)
    r = _run(nc, [arrays], core_ids=[0])
    return tuple(r.results[0][f"out_{i}"] for i in range(len(_OUTS)))
```
